# Optimizing a Trainium2 kernel written in Bass

```python
import jax
import jax.numpy as jnp
from jax import lax
import numpy as np
import math

D_MODEL = 1024
BATCH = 1
SEQ = 256
DEPTH = 1

N_MIXERS = 4
NORM_EPS = 1e-6
GLA_HEADS = 4
GLA_DK = D_MODEL // 2
GLA_DV = D_MODEL
GLA_RANK = 16
GLA_TAU = 16.0
GLA_CHUNK = 64
GLA_IN = 2 * GLA_DK + 2 * GLA_DV + GLA_RANK
RWKV_HEAD = 64
RWKV_HEADS = D_MODEL // RWKV_HEAD
RWKV_DECAY_RANK = 64
RWKV_A_RANK = 64
RWKV_GATE_RANK = 128
RWKV_GN_EPS = 64e-5
RWKV_SHIFT_MIXES = 6
SB_HEADS = 16
SB_HEAD_DIM = D_MODEL // SB_HEADS
SB_BLOCK = 128
ML_HEADS = 4
ML_DK = D_MODEL // 2
ML_DV = D_MODEL
ML_CHUNK = 64
ML_IN = 2 * ML_DK + 2 * ML_DV + 2 * ML_HEADS
FFN_DIM = 2816
CONV_WIDTH = 3


def rms_norm(x, g, eps=NORM_EPS):
    xf = x.astype(jnp.float32)
    y = xf * lax.rsqrt(jnp.mean(xf * xf, axis=-1, keepdims=True) + eps)
    return (y * g.astype(jnp.float32)).astype(x.dtype)

def _to_chunks(t, chunk):
    b, s, h, d = t.shape
    return t.reshape(b, s // chunk, chunk, h, d).transpose(1, 0, 3, 2, 4)

def _from_chunks(t):
    n, b, h, c, d = t.shape
    return t.transpose(1, 0, 3, 2, 4).reshape(b, n * c, h, d)

def _gates_to_chunks(t, chunk):
    b, s, h = t.shape
    return t.reshape(b, s // chunk, chunk, h).transpose(1, 0, 3, 2)

def gla_mixer(x, w_in, w_alpha_up, b_alpha, out_norm, w_out):
    f32 = jnp.float32
    b, s, _ = x.shape
    h, dk, dv, c = GLA_HEADS, GLA_DK // GLA_HEADS, GLA_DV // GLA_HEADS, GLA_CHUNK
    proj = x @ w_in
    q, k, v, r, a_low = jnp.split(
        proj, [GLA_DK, 2 * GLA_DK, 2 * GLA_DK + GLA_DV, 2 * GLA_DK + 2 * GLA_DV], axis=-1)
    log_alpha = jax.nn.log_sigmoid((a_low @ w_alpha_up + b_alpha).astype(f32)) / GLA_TAU
    q = q.astype(f32).reshape(b, s, h, dk) * dk ** -0.5
    k = k.astype(f32).reshape(b, s, h, dk)
    v = v.astype(f32).reshape(b, s, h, dv)
    qc, kc, vc = _to_chunks(q, c), _to_chunks(k, c), _to_chunks(v, c)
    cum = jnp.cumsum(_to_chunks(log_alpha.reshape(b, s, h, dk), c), axis=3)
    causal = jnp.tril(jnp.ones((c, c), dtype=bool))

    def step(state, inp):
        qi, ki, vi, bi = inp
        q_dec = qi * jnp.exp(bi)
        k_inv = ki * jnp.exp(-bi)
        scores = jnp.where(causal, jnp.einsum('bhtd,bhsd->bhts', q_dec, k_inv), 0.0)
        o = (jnp.einsum('bhts,bhsv->bhtv', scores, vi)
             + jnp.einsum('bhtd,bhdv->bhtv', q_dec, state))
        b_last = bi[:, :, -1:, :]
        k_end = ki * jnp.exp(b_last - bi)
        state = (state * jnp.exp(b_last)[:, :, 0, :, None]
                 + jnp.einsum('bhsd,bhsv->bhdv', k_end, vi))
        return state, o

    state0 = jnp.zeros((b, h, dk, dv), f32)
    _, o = lax.scan(step, state0, (qc, kc, vc, cum))
    o = _from_chunks(o)
    o = rms_norm(o, out_norm.reshape(h, dv)).reshape(b, s, GLA_DV)
    return (o.astype(x.dtype) * jax.nn.silu(r)) @ w_out

def rwkv7_mixer(x, mu, w_rkv, w0, w1, w2, a0, a1, a2, g1, g2, k_k, k_a, r_k, gn_g, gn_b, w_out):
    f32 = jnp.float32
    b, s, d = x.shape
    h, n = RWKV_HEADS, RWKV_HEAD
    x_prev = jnp.pad(x, ((0, 0), (1, 0), (0, 0)))[:, :-1]
    xx = x_prev - x
    xr, xw, xk, xv, xa, xg = (x + xx * mu[j] for j in range(RWKV_SHIFT_MIXES))
    r = xr @ w_rkv[0]
    k = xk @ w_rkv[1]
    v = xv @ w_rkv[2]
    w_log = -jax.nn.softplus(-(w0 + jnp.tanh(xw @ w1) @ w2).astype(f32)) - 0.5
    decay = jnp.exp(-jnp.exp(w_log))
    a = jax.nn.sigmoid((a0 + (xa @ a1) @ a2).astype(f32))
    g = jax.nn.sigmoid(xg @ g1) @ g2
    kk = (k * k_k).astype(f32).reshape(b, s, h, n)
    kk = kk / jnp.maximum(jnp.sqrt(jnp.sum(kk * kk, axis=-1, keepdims=True)), 1e-12)
    k = k.astype(f32) * (1.0 + (a - 1.0) * k_a.astype(f32))
    r = r.astype(f32).reshape(b, s, h, n)
    k = k.reshape(b, s, h, n)
    v = v.astype(f32).reshape(b, s, h, n)
    a = a.reshape(b, s, h, n)
    decay = decay.reshape(b, s, h, n)

    def step(state, inp):
        r_t, w_t, k_t, v_t, kk_t, a_t = inp
        sa = jnp.einsum('bhvk,bhk->bhv', state, -kk_t)
        state = (state * w_t[:, :, None, :]
                 + sa[..., None] * (kk_t * a_t)[:, :, None, :]
                 + v_t[..., None] * k_t[:, :, None, :])
        return state, jnp.einsum('bhvk,bhk->bhv', state, r_t)

    tm = lambda t: jnp.moveaxis(t, 1, 0)
    state0 = jnp.zeros((b, h, n, n), f32)
    _, y = lax.scan(step, state0, (tm(r), tm(decay), tm(k), tm(v), tm(kk), tm(a)))
    y = jnp.moveaxis(y, 0, 1)
    mean = jnp.mean(y, axis=-1, keepdims=True)
    var = jnp.mean(jnp.square(y - mean), axis=-1, keepdims=True)
    yn = ((y - mean) * lax.rsqrt(var + RWKV_GN_EPS)).reshape(b, s, d) * gn_g.astype(f32) + gn_b.astype(f32)
    bonus = jnp.sum(r * k * r_k.astype(f32).reshape(h, n), axis=-1, keepdims=True) * v
    out = (yn + bonus.reshape(b, s, d)).astype(x.dtype) * g
    return out @ w_out

def stick_breaking_mixer(x, w_qkv, w_out):
    f32 = jnp.float32
    b, s, d = x.shape
    h, dh, qb_len = SB_HEADS, SB_HEAD_DIM, SB_BLOCK
    q, k, v = jnp.split(x @ w_qkv, 3, axis=-1)
    q = q.reshape(b, s, h, dh) * dh ** -0.5
    k = k.reshape(b, s, h, dh)
    v = v.reshape(b, s, h, dh)
    n_blocks = s // qb_len
    q_blocks = q.reshape(b, n_blocks, qb_len, h, dh).transpose(1, 0, 3, 2, 4)
    starts = jnp.arange(n_blocks, dtype=jnp.int32) * qb_len
    key_pos = jnp.arange(s, dtype=jnp.int32)

    def block(args):
        q_blk, start = args
        z = jnp.einsum('bhqd,bkhd->bhqk', q_blk, k).astype(f32)
        q_pos = start + jnp.arange(qb_len, dtype=jnp.int32)
        before = key_pos[None, :] < q_pos[:, None]
        log_keep = jnp.where(before, jax.nn.log_sigmoid(-z), 0.0)
        suffix = lax.cumsum(log_keep, axis=3, reverse=True)
        log_w = jax.nn.log_sigmoid(z) + suffix - log_keep
        w = jnp.where(before, jnp.exp(log_w), 0.0)
        return jnp.einsum('bhqk,bkhd->bhqd', w.astype(v.dtype), v)

    o = lax.map(block, (q_blocks, starts))
    o = o.transpose(1, 0, 3, 2, 4).reshape(b, s, d)
    return o @ w_out

def mlstm_mixer(x, w_in, b_if, out_norm, w_out):
    f32 = jnp.float32
    b, s, _ = x.shape
    h, dk, dv, c = ML_HEADS, ML_DK // ML_HEADS, ML_DV // ML_HEADS, ML_CHUNK
    proj = x @ w_in
    q, k, v, o_pre, if_pre = jnp.split(
        proj, [ML_DK, 2 * ML_DK, 2 * ML_DK + ML_DV, 2 * ML_DK + 2 * ML_DV], axis=-1)
    if_pre = (if_pre + b_if).astype(f32)
    i_pre = if_pre[..., :h]
    log_f = jax.nn.log_sigmoid(if_pre[..., h:])
    qc = _to_chunks(q.astype(f32).reshape(b, s, h, dk), c)
    kc = _to_chunks(k.astype(f32).reshape(b, s, h, dk) * dk ** -0.5, c)
    vc = _to_chunks(v.astype(f32).reshape(b, s, h, dv), c)
    ic = _gates_to_chunks(i_pre, c)
    cum_f = jnp.cumsum(_gates_to_chunks(log_f, c), axis=-1)
    causal = jnp.tril(jnp.ones((c, c), dtype=bool))

    def step(carry, inp):
        c_st, n_st, m_prev = carry
        qi, ki, vi, ii, bi = inp
        d_log = jnp.where(causal, bi[..., :, None] - bi[..., None, :] + ii[..., None, :], -jnp.inf)
        inter = bi + m_prev[..., None]
        m_t = jnp.maximum(inter, jnp.max(d_log, axis=-1))
        w_intra = jnp.exp(d_log - m_t[..., None])
        scale = jnp.exp(inter - m_t)
        qk = jnp.einsum('bhtd,bhsd->bhts', qi, ki) * w_intra
        num = (jnp.einsum('bhts,bhsv->bhtv', qk, vi)
               + scale[..., None] * jnp.einsum('bhtd,bhdv->bhtv', qi, c_st))
        den = jnp.sum(qk, axis=-1) + scale * jnp.einsum('bhtd,bhd->bht', qi, n_st)
        h_out = num / jnp.maximum(jnp.abs(den), jnp.exp(-m_t))[..., None]
        b_last = bi[..., -1]
        g_end = b_last[..., None] - bi + ii
        m_new = jnp.maximum(b_last + m_prev, jnp.max(g_end, axis=-1))
        w_end = jnp.exp(g_end - m_new[..., None])
        carry_scale = jnp.exp(b_last + m_prev - m_new)
        c_st = carry_scale[..., None, None] * c_st + jnp.einsum('bhs,bhsd,bhsv->bhdv', w_end, ki, vi)
        n_st = carry_scale[..., None] * n_st + jnp.einsum('bhs,bhsd->bhd', w_end, ki)
        return (c_st, n_st, m_new), h_out

    carry0 = (jnp.zeros((b, h, dk, dv), f32), jnp.zeros((b, h, dk), f32), jnp.zeros((b, h), f32))
    _, hs = lax.scan(step, carry0, (qc, kc, vc, ic, cum_f))
    hs = _from_chunks(hs)
    hs = rms_norm(hs, out_norm.reshape(h, dv)).reshape(b, s, ML_DV)
    return (hs.astype(x.dtype) * jax.nn.sigmoid(o_pre)) @ w_out

def conv_ffn(x, w_up, conv_w, conv_b, w_down):
    s = x.shape[1]
    u = x @ w_up
    u_pad = jnp.pad(u, ((0, 0), (CONV_WIDTH - 1, 0), (0, 0)))
    u = sum(u_pad[:, j:j + s] * conv_w[j] for j in range(CONV_WIDTH)) + conv_b
    gate, up = jnp.split(u, 2, axis=-1)
    return (jax.nn.silu(gate) * up) @ w_down

def first_inputs(seed: int = 0) -> dict:
    key = jax.random.key(seed)
    ks = iter(jax.random.split(key, 96))
    f32 = jnp.float32
    D, F2 = D_MODEL, 2 * FFN_DIM

    def nrm(shape, scale):
        return scale * jax.random.normal(next(ks), shape, f32)

    def dense(fan_in, shape):
        return nrm(shape, fan_in ** -0.5)

    def gain(n):
        return 1.0 + nrm((n,), 0.02)

    def unif(shape, lo, hi):
        return jax.random.uniform(next(ks), shape, f32, lo, hi)

    p = {}

    def ffn_params(i):
        p[f"l{i}_norm2"] = gain(D)
        p[f"l{i}_ffn_w_up"] = dense(D, (D, F2))
        p[f"l{i}_ffn_conv_w"] = dense(CONV_WIDTH, (CONV_WIDTH, F2))
        p[f"l{i}_ffn_conv_b"] = nrm((F2,), 0.02)
        p[f"l{i}_ffn_w_down"] = dense(FFN_DIM, (FFN_DIM, D))

    p["x"] = nrm((BATCH, SEQ, D), 1.0)
    p["l0_norm1"] = gain(D)
    p["l0_gla_w_in"] = dense(D, (D, GLA_IN))
    p["l0_gla_w_alpha_up"] = dense(GLA_RANK, (GLA_RANK, GLA_DK))
    p["l0_gla_b_alpha"] = nrm((GLA_DK,), 0.1)
    p["l0_gla_out_norm"] = gain(GLA_DV)
    p["l0_gla_w_out"] = dense(GLA_DV, (GLA_DV, D))
    ffn_params(0)
    p["l1_norm1"] = gain(D)
    p["l1_rwkv_mu"] = unif((RWKV_SHIFT_MIXES, D), 0.0, 1.0)
    p["l1_rwkv_w_rkv"] = dense(D, (3, D, D))
    p["l1_rwkv_w0"] = unif((D,), -6.0, -1.0)
    p["l1_rwkv_w1"] = dense(D, (D, RWKV_DECAY_RANK))
    p["l1_rwkv_w2"] = nrm((RWKV_DECAY_RANK, D), 0.1 * RWKV_DECAY_RANK ** -0.5)
    p["l1_rwkv_a0"] = nrm((D,), 0.1)
    p["l1_rwkv_a1"] = dense(D, (D, RWKV_A_RANK))
    p["l1_rwkv_a2"] = dense(RWKV_A_RANK, (RWKV_A_RANK, D))
    p["l1_rwkv_g1"] = dense(D, (D, RWKV_GATE_RANK))
    p["l1_rwkv_g2"] = dense(RWKV_GATE_RANK, (RWKV_GATE_RANK, D))
    p["l1_rwkv_k_k"] = 0.85 + nrm((D,), 0.05)
    p["l1_rwkv_k_a"] = 1.0 + nrm((D,), 0.05)
    p["l1_rwkv_r_k"] = nrm((D,), 0.1)
    p["l1_rwkv_gn_g"] = gain(D)
    p["l1_rwkv_gn_b"] = nrm((D,), 0.02)
    p["l1_rwkv_w_out"] = dense(D, (D, D))
    ffn_params(1)
    p["l2_norm1"] = gain(D)
    p["l2_sb_w_qkv"] = dense(D, (D, 3 * D))
    p["l2_sb_w_out"] = dense(D, (D, D))
    ffn_params(2)
    p["l3_norm1"] = gain(D)
    p["l3_ml_w_in"] = dense(D, (D, ML_IN))
    p["l3_ml_b_if"] = jnp.concatenate([nrm((ML_HEADS,), 0.1), unif((ML_HEADS,), 3.0, 6.0)])
    p["l3_ml_out_norm"] = gain(ML_DV)
    p["l3_ml_w_out"] = dense(ML_DV, (ML_DV, D))
    ffn_params(3)
    p["final_norm"] = gain(D)
    return p

def first_block(x,
              l0_norm1, l0_gla_w_in, l0_gla_w_alpha_up, l0_gla_b_alpha, l0_gla_out_norm, l0_gla_w_out,
              l0_norm2, l0_ffn_w_up, l0_ffn_conv_w, l0_ffn_conv_b, l0_ffn_w_down,
              l1_norm1, l1_rwkv_mu, l1_rwkv_w_rkv, l1_rwkv_w0, l1_rwkv_w1, l1_rwkv_w2,
              l1_rwkv_a0, l1_rwkv_a1, l1_rwkv_a2, l1_rwkv_g1, l1_rwkv_g2,
              l1_rwkv_k_k, l1_rwkv_k_a, l1_rwkv_r_k, l1_rwkv_gn_g, l1_rwkv_gn_b, l1_rwkv_w_out,
              l1_norm2, l1_ffn_w_up, l1_ffn_conv_w, l1_ffn_conv_b, l1_ffn_w_down,
              l2_norm1, l2_sb_w_qkv, l2_sb_w_out,
              l2_norm2, l2_ffn_w_up, l2_ffn_conv_w, l2_ffn_conv_b, l2_ffn_w_down,
              l3_norm1, l3_ml_w_in, l3_ml_b_if, l3_ml_out_norm, l3_ml_w_out,
              l3_norm2, l3_ffn_w_up, l3_ffn_conv_w, l3_ffn_conv_b, l3_ffn_w_down,
              final_norm):
    mixers = (
        lambda h: gla_mixer(h, l0_gla_w_in, l0_gla_w_alpha_up, l0_gla_b_alpha, l0_gla_out_norm, l0_gla_w_out),
        lambda h: rwkv7_mixer(h, l1_rwkv_mu, l1_rwkv_w_rkv, l1_rwkv_w0, l1_rwkv_w1, l1_rwkv_w2,
                              l1_rwkv_a0, l1_rwkv_a1, l1_rwkv_a2, l1_rwkv_g1, l1_rwkv_g2,
                              l1_rwkv_k_k, l1_rwkv_k_a, l1_rwkv_r_k, l1_rwkv_gn_g, l1_rwkv_gn_b,
                              l1_rwkv_w_out),
        lambda h: stick_breaking_mixer(h, l2_sb_w_qkv, l2_sb_w_out),
        lambda h: mlstm_mixer(h, l3_ml_w_in, l3_ml_b_if, l3_ml_out_norm, l3_ml_w_out),
    )
    norm1 = (l0_norm1, l1_norm1, l2_norm1, l3_norm1)
    norm2 = (l0_norm2, l1_norm2, l2_norm2, l3_norm2)
    ffns = (
        (l0_ffn_w_up, l0_ffn_conv_w, l0_ffn_conv_b, l0_ffn_w_down),
        (l1_ffn_w_up, l1_ffn_conv_w, l1_ffn_conv_b, l1_ffn_w_down),
        (l2_ffn_w_up, l2_ffn_conv_w, l2_ffn_conv_b, l2_ffn_w_down),
        (l3_ffn_w_up, l3_ffn_conv_w, l3_ffn_conv_b, l3_ffn_w_down),
    )
    for layer in range(DEPTH):
        x = x + mixers[layer % N_MIXERS](rms_norm(x, norm1[layer]))
        x = x + conv_ffn(rms_norm(x, norm2[layer]), *ffns[layer])
    return rms_norm(x, final_norm)


ATT_HEADS = 8
ATT_HEAD_DIM = 128
KV_LATENT = 256
IDX_HEADS = 8
IDX_DIM = 64
TOPK_MAX = 256
Q_BLOCK = 128
ATT_SCALE = ATT_HEAD_DIM ** -0.5
INDEX_SCALE = (IDX_HEADS ** -0.5) * (IDX_DIM ** -0.5)
DN_HEADS = 8
DN_DK = 128
DN_DV = 128
CONV_WIDTH_2 = 4
CHUNK = 64
N_GROUPS = 4
EXPERTS_PER_GROUP = 8
N_EXPERTS = N_GROUPS * EXPERTS_PER_GROUP
EXPERT_TOPK = 2
EXPERT_FF = 512
MOE_BLOCK = 128
LN_EPS = 1e-5
RMS_EPS = 1e-6

ATT_Q_COLS = ATT_HEADS * ATT_HEAD_DIM
IDX_Q_COLS = IDX_HEADS * IDX_DIM
DN_QK_COLS = DN_HEADS * DN_DK
DN_V_COLS = DN_HEADS * DN_DV
CONV_CH = 2 * DN_QK_COLS + DN_V_COLS
COL_SIZES = (ATT_Q_COLS, KV_LATENT, IDX_Q_COLS, IDX_DIM, IDX_HEADS,
             CONV_CH, DN_HEADS, DN_HEADS, DN_V_COLS, 2 * D_MODEL)
N_IN = sum(COL_SIZES)
SPLITS = tuple(int(v) for v in np.cumsum(COL_SIZES)[:-1])


def layer_norm(x, g, b):
    xf = x.astype(jnp.float32)
    mu = jnp.mean(xf, axis=-1, keepdims=True)
    var = jnp.mean(jnp.square(xf - mu), axis=-1, keepdims=True)
    return ((xf - mu) * lax.rsqrt(var + LN_EPS)).astype(x.dtype) * g + b

def rms_norm_2(x, g):
    xf = x.astype(jnp.float32)
    return (xf * lax.rsqrt(jnp.mean(xf * xf, axis=-1, keepdims=True) + RMS_EPS)).astype(x.dtype) * g

def l2_normalize(x):
    return x * lax.rsqrt(jnp.sum(x * x, axis=-1, keepdims=True) + RMS_EPS)

def causal_conv(x, w):
    width = w.shape[0]
    return lax.conv_general_dilated(
        x, w[:, None, :], window_strides=(1,), padding=[(width - 1, 0)],
        dimension_numbers=('NWC', 'WIO', 'NWC'), feature_group_count=x.shape[-1])

def dsa_attention(q_att, c_kv, q_idx, k_idx, w_idx, w_uk, w_uv):
    B, S = c_kv.shape[0], c_kv.shape[1]
    topk = min(TOPK_MAX, S // 4)
    nb = S // Q_BLOCK
    q_lat = jnp.einsum('bshd,hcd->bshc', q_att, w_uk)
    key_pos = jnp.arange(S)
    gather = jax.vmap(lambda table, idx: table[idx])

    def to_blocks(t):
        return jnp.moveaxis(t.reshape((B, nb, Q_BLOCK) + t.shape[2:]), 1, 0)

    def block(args):
        ql, qi, wi, t0 = args
        qpos = t0 + jnp.arange(Q_BLOCK)
        rel = jax.nn.relu(jnp.einsum('bqhd,bsd->bqhs', qi, k_idx))
        iscore = jnp.einsum('bqhs,bqh->bqs', rel, wi).astype(jnp.float32)
        causal = key_pos[None, :] <= qpos[:, None]
        iscore = jnp.where(causal[None], iscore, -jnp.inf)
        _, sel = lax.top_k(iscore, topk)
        kv = gather(c_kv, sel)
        s = jnp.einsum('bqhc,bqkc->bqhk', ql, kv).astype(jnp.float32) * ATT_SCALE
        valid = sel <= qpos[None, :, None]
        s = jnp.where(valid[:, :, None, :], s, -jnp.inf)
        p = jax.nn.softmax(s, axis=-1).astype(kv.dtype)
        return jnp.einsum('bqhk,bqkc->bqhc', p, kv)

    o_lat = lax.map(block, (to_blocks(q_lat), to_blocks(q_idx), to_blocks(w_idx),
                            jnp.arange(nb) * Q_BLOCK))
    o_lat = jnp.moveaxis(o_lat, 0, 1).reshape(B, S, ATT_HEADS, KV_LATENT)
    o = jnp.einsum('bshc,hcd->bshd', o_lat, w_uv)
    return o.reshape(B, S, ATT_HEADS * ATT_HEAD_DIM)

def chunk_gated_delta_rule(q, k, v, beta, g):
    B, S, H, Dk = q.shape
    Dv = v.shape[-1]
    n = S // CHUNK

    def chunks(t):
        return t.reshape(B, n, CHUNK, H, -1).transpose(0, 3, 1, 2, 4)

    q, k, v = chunks(q), chunks(k), chunks(v)
    beta = beta.reshape(B, n, CHUNK, H).transpose(0, 3, 1, 2)
    G = jnp.cumsum(g.reshape(B, n, CHUNK, H).transpose(0, 3, 1, 2), axis=-1)
    tril = jnp.tril(jnp.ones((CHUNK, CHUNK), dtype=bool))
    tril_strict = jnp.tril(jnp.ones((CHUNK, CHUNK), dtype=bool), -1)
    decay = jnp.exp(jnp.where(tril, G[..., :, None] - G[..., None, :], -jnp.inf))
    kb = k * beta[..., None]
    A = jnp.where(tril_strict, jnp.einsum('bhncd,bhnsd->bhncs', kb, k) * decay, 0.0)
    eye = jnp.eye(CHUNK, dtype=A.dtype)
    rhs = jnp.concatenate([v * beta[..., None], kb * jnp.exp(G)[..., None]], axis=-1)
    sol = lax.linalg.triangular_solve(eye + A, rhs, left_side=True, lower=True,
                                      unit_diagonal=True)
    u, w = sol[..., :Dv], sol[..., Dv:]
    qk = jnp.where(tril, jnp.einsum('bhncd,bhnsd->bhncs', q, k) * decay, 0.0)
    q_dec = q * jnp.exp(G)[..., None]
    k_tail = k * jnp.exp(G[..., -1:] - G)[..., None]
    g_last = jnp.exp(G[..., -1])

    def step(state, xs):
        q_n, k_n, u_n, w_n, qk_n, gl_n = xs
        v_new = u_n - jnp.einsum('bhck,bhkv->bhcv', w_n, state)
        o_n = (jnp.einsum('bhck,bhkv->bhcv', q_n, state)
               + jnp.einsum('bhcs,bhsv->bhcv', qk_n, v_new))
        state = state * gl_n[..., None, None] + jnp.einsum('bhck,bhcv->bhkv', k_n, v_new)
        return state, o_n

    xs = tuple(jnp.moveaxis(t, 2, 0) for t in (q_dec, k_tail, u, w, qk, g_last))
    state0 = jnp.zeros((B, H, Dk, Dv), jnp.float32)
    _, o = lax.scan(step, state0, xs)
    return o.transpose(1, 0, 3, 2, 4).reshape(B, S, H, Dv)

def gated_deltanet(qkv, a, b, z, conv_w, a_log, dt_bias, norm_g):
    B, S = qkv.shape[0], qkv.shape[1]
    dtype = qkv.dtype
    qkv = jax.nn.silu(causal_conv(qkv, conv_w)).astype(jnp.float32)
    q = l2_normalize(qkv[..., :DN_QK_COLS].reshape(B, S, DN_HEADS, DN_DK)) * (DN_DK ** -0.5)
    k = l2_normalize(qkv[..., DN_QK_COLS:2 * DN_QK_COLS].reshape(B, S, DN_HEADS, DN_DK))
    v = qkv[..., 2 * DN_QK_COLS:].reshape(B, S, DN_HEADS, DN_DV)
    beta = jax.nn.sigmoid(b.astype(jnp.float32))
    g = -jnp.exp(a_log.astype(jnp.float32)) * jax.nn.softplus(
        a.astype(jnp.float32) + dt_bias.astype(jnp.float32))
    o = chunk_gated_delta_rule(q, k, v, beta, g)
    zf = z.astype(jnp.float32).reshape(B, S, DN_HEADS, DN_DV)
    o = rms_norm_2(o, norm_g.astype(jnp.float32)) * jax.nn.silu(zf)
    return o.reshape(B, S, DN_V_COLS).astype(dtype)

def token_mixer(h, w_in, kv_norm_g, w_uk, w_uv, conv_w, a_log, dt_bias, dn_norm_g,
                w_br_att, w_br_dn, w_out):
    B, S = h.shape[0], h.shape[1]
    proj = h @ w_in
    (q_att, c_kv, q_idx, k_idx, w_idx, qkv, a, b, z, gates) = jnp.split(proj, SPLITS, axis=-1)
    c_kv = rms_norm_2(c_kv, kv_norm_g)
    y_att = dsa_attention(q_att.reshape(B, S, ATT_HEADS, ATT_HEAD_DIM), c_kv,
                          q_idx.reshape(B, S, IDX_HEADS, IDX_DIM), k_idx,
                          w_idx * INDEX_SCALE, w_uk, w_uv)
    y_dn = gated_deltanet(qkv, a, b, z, conv_w, a_log, dt_bias, dn_norm_g)
    gates = jax.nn.sigmoid(gates)
    g_att, g_dn = gates[..., :D_MODEL], gates[..., D_MODEL:]
    merged = g_att * (y_att @ w_br_att) + g_dn * (y_dn @ w_br_dn)
    return merged @ w_out

def hier_moe(h, w_route_grp, w_route_exp, w_gate, w_up, w_down):
    B, S, D = h.shape
    n_tok = B * S
    xt = h.reshape(n_tok, D)
    p_grp = jax.nn.softmax((xt @ w_route_grp).astype(jnp.float32), axis=-1)
    top_gp, g_idx = lax.top_k(p_grp, 1)
    exp_logits = (xt @ w_route_exp).astype(jnp.float32).reshape(n_tok, N_GROUPS, EXPERTS_PER_GROUP)
    in_grp = jnp.take_along_axis(exp_logits, g_idx[:, :, None], axis=1)[:, 0]
    top_pe, e_local = lax.top_k(jax.nn.softmax(in_grp, axis=-1), EXPERT_TOPK)
    gates = top_pe / jnp.sum(top_pe, axis=-1, keepdims=True) * top_gp
    e_idx = g_idx * EXPERTS_PER_GROUP + e_local

    m = n_tok * EXPERT_TOPK
    flat_e = e_idx.reshape(m)
    flat_tok = jnp.repeat(jnp.arange(n_tok), EXPERT_TOPK)
    flat_gate = gates.reshape(m)
    order = jnp.argsort(flat_e)
    se = flat_e[order]
    counts = jnp.bincount(flat_e, length=N_EXPERTS)
    pcounts = (counts + MOE_BLOCK - 1) // MOE_BLOCK * MOE_BLOCK
    starts = jnp.cumsum(counts) - counts
    pends = jnp.cumsum(pcounts)
    pstarts = pends - pcounts
    dest = pstarts[se] + jnp.arange(m) - starts[se]
    nb = -(-m // MOE_BLOCK) + N_EXPERTS
    rows = nb * MOE_BLOCK
    tok_buf = jnp.full((rows,), n_tok, jnp.int32).at[dest].set(flat_tok[order])
    gate_buf = jnp.zeros((rows,), jnp.float32).at[dest].set(flat_gate[order])
    blk_e = jnp.minimum(jnp.searchsorted(pends, jnp.arange(nb) * MOE_BLOCK, side='right'),
                        N_EXPERTS - 1)
    x_pad = jnp.concatenate([xt, jnp.zeros((1, D), xt.dtype)], axis=0)
    xs = x_pad[tok_buf].reshape(nb, MOE_BLOCK, D)

    def expert_block(args):
        xb, e = args
        hb = jax.nn.silu(xb @ w_gate[e]) * (xb @ w_up[e])
        return hb @ w_down[e]

    yb = lax.map(expert_block, (xs, blk_e)).reshape(rows, D)
    yb = yb * gate_buf[:, None].astype(yb.dtype)
    out = jnp.zeros((n_tok + 1, D), yb.dtype).at[tok_buf].add(yb)[:n_tok]
    return out.reshape(B, S, D)

def second_inputs(seed: int = 0) -> dict:
    key = jax.random.key(seed)
    ks = jax.random.split(key, 24)
    f32 = jnp.float32
    L, D = DEPTH, D_MODEL
    beta = (8.0 * DEPTH) ** -0.25

    def nrm(k, shape, scale):
        return jax.random.normal(k, shape, f32) * scale

    dt = jnp.exp(jax.random.uniform(ks[10], (L, DN_HEADS), f32, math.log(1e-3), math.log(1e-1)))
    return {
        'x': nrm(ks[0], (BATCH, SEQ, D), 1.0),
        'c': nrm(ks[1], (BATCH, D), 1.0),
        'w_ada': nrm(ks[2], (L, D, 6 * D), 0.1 * D ** -0.5),
        'b_ada': nrm(ks[3], (L, 6 * D), 0.01),
        'w_in': nrm(ks[4], (L, D, N_IN), D ** -0.5),
        'kv_norm_g': 1.0 + nrm(ks[5], (L, KV_LATENT), 0.02),
        'w_uk': nrm(ks[6], (L, ATT_HEADS, KV_LATENT, ATT_HEAD_DIM), KV_LATENT ** -0.5),
        'w_uv': nrm(ks[7], (L, ATT_HEADS, KV_LATENT, ATT_HEAD_DIM), KV_LATENT ** -0.5),
        'conv_w': nrm(ks[8], (L, CONV_WIDTH_2, CONV_CH), CONV_WIDTH_2 ** -0.5),
        'a_log': jnp.log(jax.random.uniform(ks[9], (L, DN_HEADS), f32, 1.0, 16.0)),
        'dt_bias': dt + jnp.log(-jnp.expm1(-dt)),
        'dn_norm_g': 1.0 + nrm(ks[11], (L, DN_DV), 0.02),
        'w_br_att': nrm(ks[12], (L, ATT_Q_COLS, D), ATT_Q_COLS ** -0.5),
        'w_br_dn': nrm(ks[13], (L, DN_V_COLS, D), DN_V_COLS ** -0.5),
        'w_out': nrm(ks[14], (L, D, D), beta * D ** -0.5),
        'w_route_grp': nrm(ks[15], (L, D, N_GROUPS), D ** -0.5),
        'w_route_exp': nrm(ks[16], (L, D, N_EXPERTS), D ** -0.5),
        'w_gate': nrm(ks[17], (L, N_EXPERTS, D, EXPERT_FF), D ** -0.5),
        'w_up': nrm(ks[18], (L, N_EXPERTS, D, EXPERT_FF), D ** -0.5),
        'w_down': nrm(ks[19], (L, N_EXPERTS, EXPERT_FF, D), beta * EXPERT_FF ** -0.5),
        'ln_g': 1.0 + nrm(ks[20], (L, 2, D), 0.02),
        'ln_b': nrm(ks[21], (L, 2, D), 0.02),
    }

def second_block(x, c, w_ada, b_ada, w_in, kv_norm_g, w_uk, w_uv, conv_w, a_log, dt_bias,
              dn_norm_g, w_br_att, w_br_dn, w_out, w_route_grp, w_route_exp, w_gate,
              w_up, w_down, ln_g, ln_b):
    alpha = (2.0 * DEPTH) ** 0.25
    cond = jax.nn.silu(c)
    for l in range(DEPTH):
        mod = cond @ w_ada[l] + b_ada[l]
        sh1, sc1, gt1, sh2, sc2, gt2 = [m[:, None, :] for m in jnp.split(mod, 6, axis=-1)]
        h = x * (1.0 + sc1) + sh1
        y = token_mixer(h, w_in[l], kv_norm_g[l], w_uk[l], w_uv[l], conv_w[l], a_log[l],
                        dt_bias[l], dn_norm_g[l], w_br_att[l], w_br_dn[l], w_out[l])
        x = layer_norm(alpha * x + (1.0 + gt1) * y, ln_g[l, 0], ln_b[l, 0])
        h = x * (1.0 + sc2) + sh2
        y = hier_moe(h, w_route_grp[l], w_route_exp[l], w_gate[l], w_up[l], w_down[l])
        x = layer_norm(alpha * x + (1.0 + gt2) * y, ln_g[l, 1], ln_b[l, 1])
    return x


def setup_inputs(seed=0):
    out = dict(first_inputs(seed))
    for name, value in second_inputs(seed + 1).items():
        if name != "x":
            out[name + "_2"] = value
    return out


def reference(
    x, l0_norm1, l0_gla_w_in, l0_gla_w_alpha_up, l0_gla_b_alpha, l0_gla_out_norm, l0_gla_w_out,
    l0_norm2, l0_ffn_w_up, l0_ffn_conv_w, l0_ffn_conv_b, l0_ffn_w_down, l1_norm1, l1_rwkv_mu,
    l1_rwkv_w_rkv, l1_rwkv_w0, l1_rwkv_w1, l1_rwkv_w2, l1_rwkv_a0, l1_rwkv_a1, l1_rwkv_a2,
    l1_rwkv_g1, l1_rwkv_g2, l1_rwkv_k_k, l1_rwkv_k_a, l1_rwkv_r_k, l1_rwkv_gn_g, l1_rwkv_gn_b,
    l1_rwkv_w_out, l1_norm2, l1_ffn_w_up, l1_ffn_conv_w, l1_ffn_conv_b, l1_ffn_w_down, l2_norm1,
    l2_sb_w_qkv, l2_sb_w_out, l2_norm2, l2_ffn_w_up, l2_ffn_conv_w, l2_ffn_conv_b,
    l2_ffn_w_down, l3_norm1, l3_ml_w_in, l3_ml_b_if, l3_ml_out_norm, l3_ml_w_out, l3_norm2,
    l3_ffn_w_up, l3_ffn_conv_w, l3_ffn_conv_b, l3_ffn_w_down, final_norm, c_2, w_ada_2, b_ada_2,
    w_in_2, kv_norm_g_2, w_uk_2, w_uv_2, conv_w_2, a_log_2, dt_bias_2, dn_norm_g_2, w_br_att_2,
    w_br_dn_2, w_out_2, w_route_grp_2, w_route_exp_2, w_gate_2, w_up_2, w_down_2, ln_g_2,
    ln_b_2,
):
    x = first_block(
        x, l0_norm1, l0_gla_w_in, l0_gla_w_alpha_up, l0_gla_b_alpha, l0_gla_out_norm,
        l0_gla_w_out, l0_norm2, l0_ffn_w_up, l0_ffn_conv_w, l0_ffn_conv_b, l0_ffn_w_down,
        l1_norm1, l1_rwkv_mu, l1_rwkv_w_rkv, l1_rwkv_w0, l1_rwkv_w1, l1_rwkv_w2, l1_rwkv_a0,
        l1_rwkv_a1, l1_rwkv_a2, l1_rwkv_g1, l1_rwkv_g2, l1_rwkv_k_k, l1_rwkv_k_a, l1_rwkv_r_k,
        l1_rwkv_gn_g, l1_rwkv_gn_b, l1_rwkv_w_out, l1_norm2, l1_ffn_w_up, l1_ffn_conv_w,
        l1_ffn_conv_b, l1_ffn_w_down, l2_norm1, l2_sb_w_qkv, l2_sb_w_out, l2_norm2, l2_ffn_w_up,
        l2_ffn_conv_w, l2_ffn_conv_b, l2_ffn_w_down, l3_norm1, l3_ml_w_in, l3_ml_b_if,
        l3_ml_out_norm, l3_ml_w_out, l3_norm2, l3_ffn_w_up, l3_ffn_conv_w, l3_ffn_conv_b,
        l3_ffn_w_down, final_norm,
    )
    return second_block(
        x, c_2, w_ada_2, b_ada_2, w_in_2, kv_norm_g_2, w_uk_2, w_uv_2, conv_w_2, a_log_2,
        dt_bias_2, dn_norm_g_2, w_br_att_2, w_br_dn_2, w_out_2, w_route_grp_2, w_route_exp_2,
        w_gate_2, w_up_2, w_down_2, ln_g_2, ln_b_2,
    )


_drawn_inputs = setup_inputs


def setup_inputs(seed=0):
    import zlib

    import numpy as np

    out = dict(_drawn_inputs(seed))
    spreads = {}
    factors = {'l0_gla_out_norm': 2.958,
     'l0_norm2': 2.858,
     'l0_ffn_conv_b': 2.822,
     'b_ada_2': 3.515,
     'kv_norm_g_2': 7.494,
     'dn_norm_g_2': 31.643}
    for name, (base, spread) in spreads.items():
        noise = np.random.default_rng([zlib.crc32(name.encode()), seed]).standard_normal(out[name].shape)
        drawn = base * np.exp(spread * noise) if base else spread * noise
        out[name] = jnp.asarray(drawn.astype(out[name].dtype))
    for name, factor in factors.items():
        out[name] = (out[name] * factor).astype(out[name].dtype)
    return out
```

```python
from contextlib import ExitStack

import numpy as np

import concourse.bass as bass
from concourse import mybir

F32 = mybir.dt.float32
I32 = mybir.dt.int32
ALU = mybir.AluOpType
ACT = mybir.ActivationFunctionType
AX_X = mybir.AxisListType.X

P = 128
T = 256
NT = T // P
D = 1024
KD = D // P
HALF = 512
CH = 64
NCH = T // CH

GH, GDK, GDV = 4, 128, 256
GRANK = 16
GTAU = 16.0
FF = 2816
FT = FF // P
RMS_EPS = 1e-6
LN_EPS = 1e-5

AH, ADH = 8, 128
LAT = 256
IH, IDH = 8, 64
TOPK = 64
ATT_SCALE = ADH ** -0.5
INDEX_SCALE = (IH ** -0.5) * (IDH ** -0.5)
NH, NDK = 8, 128
NE, NG, EPG, EF = 32, 4, 8, 512
SLOTS = 32
ALPHA = 2.0 ** 0.25
NEG = -3.0e38
TAKEN = -3.3e38

C_QATT, C_CKV, C_QIDX, C_KIDX, C_WIDX = 0, 1024, 1280, 1792, 1856
C_QKV = 1864
C_A, C_B, C_Z, C_GATES = 4936, 4944, 4952, 5976

CONSTS = {}


def constant_table():
    p = np.arange(P)[:, None]
    c = np.arange(P)[None, :]
    same = (p // CH) == (c // CH)
    parts = [
        ("ident", p == c),
        ("ones", np.ones((P, P))),
        ("upto", same & (p <= c)),
        ("before", same & (p < c)),
        ("chunk", same),
        ("earlier", p < c),
    ]
    for level in range(6):
        b = 1 << level
        pair = (p // (2 * b)) == (c // (2 * b))
        parts.append((f"up{level}", pair & ((p // b) % 2 == 0) & ((c // b) % 2 == 1)))
    for level in range(1, 5):
        b = 1 << level
        pair = (p // (2 * b)) == (c // (2 * b))
        parts.append((f"low{level}", pair & ((p // b) % 2 == 1) & ((c // b) % 2 == 0)))
    c2 = np.arange(T)[None, :]
    parts.append(("causal0", c2 <= p))
    parts.append(("causal1", c2 <= p + P))
    parts.append(("slot", np.broadcast_to(np.arange(T)[None, :], (P, T))))
    parts.append(("first", np.broadcast_to(np.arange(8, 0, -1)[None, :], (P, 8))))
    at = 0
    for name, part in parts:
        CONSTS[name] = (at, part.shape[1])
        at += part.shape[1]
    return np.ascontiguousarray(np.concatenate([x[1].astype(np.float32) for x in parts], axis=1))


CONST_TABLE = constant_table()
NCONST = CONST_TABLE.shape[1]

COLS = {}
for _name, _n in (("norm1", 8), ("out_norm", 8), ("norm2", 8), ("conv_w", 3 * 2 * FT), ("conv_b", 2 * FT),
                  ("cond", 8), ("b_ada", 48), ("kv_g", 2), ("dn_conv", 4 * 24), ("dn_g", 1)):
    COLS[_name] = (sum(n for _, n in COLS.values()), _n)
NCOLS = sum(n for _, n in COLS.values())

ROWS = ("final_norm", "ln_g0", "ln_b0", "ln_g1", "ln_b1")


def build_program(nc, I, out):
    ctx = ExitStack()
    with ctx:
        def sb(name, shape):
            return ctx.enter_context(nc.sbuf_tensor(name, shape, F32))

        S = {}

        def sem(*names):
            for n in names:
                S[n] = ctx.enter_context(nc.semaphore(n))

        U = 2048
        main = sb("main", [P, 24 * U])
        consts = sb("consts", [P, NCONST])
        cols = sb("cols", [P, NCOLS])
        small = sb("small", [P, 384])
        ps = ctx.enter_context(nc.psum_tensor("ps", [P, 8, HALF], F32))

        def unit(i, a=0, b=U):
            return main[:, i * U + a:i * U + b]

        def rows2(i):
            return unit(i).rearrange("p (j d) -> p j d", j=NT)

        def cols8(i):
            return unit(i).rearrange("p (k t) -> p k t", t=T)

        def tiles4(i, half):
            return unit(i, half * 1024, half * 1024 + 1024).rearrange("p (k t) -> p k t", t=T)

        def const(name):
            a, n = CONSTS[name]
            return consts[:, a:a + n]

        def col(name):
            a, n = COLS[name]
            return cols[:, a:a + n]

        def bank(b, n=1):
            return ps[:, b:b + n, :].rearrange("p b c -> p (b c)")

        def link(eng, name, count, ins):
            count[0] += 1
            ins.then_inc(S[name], 1)
            eng.wait_ge(S[name], count[0])

        RING, RING0 = 4, 16
        sem(*[f"ring{i}_loaded" for i in range(RING)], "chunk_done")

        def chunk(n):
            return main[:, (RING0 + 2 * (n % RING)) * U:(RING0 + 2 * (n % RING) + 2) * U]

        def chunk8(n):
            return chunk(n).rearrange("p (k c) -> p k c", k=KD)

        def wide(w, a, n=HALF):
            return w[:, a:a + n].rearrange("(k p) c -> p k c", p=P)

        CHUNKS = []

        def add_chunk(src, k=KD, n=HALF):
            CHUNKS.append((src, k, n))
            return len(CHUNKS) - 1

        w_gla = I["l0_gla_w_in"]
        C_GLA = [add_chunk(wide(w_gla, HALF * i)) for i in range(6)]
        C_GLA_OUT = [add_chunk(wide(I["l0_gla_w_out"], HALF * i)) for i in range(2)]
        N_FIRST = len(CHUNKS)
        w_in = I["w_in_2"].rearrange("b d n -> (b d) n")

        def latent(w):
            return w.rearrange("b h (c p) d -> p (b h c) d", p=P)

        C_CKV = add_chunk(wide(w_in, 1024, LAT), n=LAT)
        C_KW = add_chunk(wide(w_in, 1792, 72), n=72)
        C_QI = add_chunk(wide(w_in, 1280))
        C_QA = [add_chunk(wide(w_in, 0))]
        C_QA.append(add_chunk(wide(w_in, HALF)))
        C_UK = add_chunk(latent(I["w_uk_2"]), k=16, n=P)
        C_UV = add_chunk(latent(I["w_uv_2"]), k=16, n=P)
        C_QKVD = [add_chunk(wide(w_in, 1864 + HALF * i)) for i in range(6)]
        C_GA = [add_chunk(wide(w_in, 5976 + HALF * i)) for i in range(2)]
        C_BRA = [add_chunk(wide(I["w_br_att_2"].rearrange("b d n -> (b d) n"), HALF * i)) for i in range(2)]
        C_AB = add_chunk(wide(w_in, 4936, 16), n=16)
        C_Z = [add_chunk(wide(w_in, 4952 + HALF * i)) for i in range(2)]
        C_GD = [add_chunk(wide(w_in, 7000 + HALF * i)) for i in range(2)]
        C_BRD = [add_chunk(wide(I["w_br_dn_2"].rearrange("b d n -> (b d) n"), HALF * i)) for i in range(2)]
        C_WO = [add_chunk(wide(I["w_out_2"].rearrange("b d n -> (b d) n"), HALF * i)) for i in range(2)]
        N_SECOND = len(CHUNKS)

        def ring_wait(pe, n):
            pe.wait_ge(S[f"ring{n % RING}_loaded"], 16 * (n // RING + 1))

        def load_ring(sp, n):
            if n >= RING:
                sp.wait_ge(S["chunk_done"], n - RING + 1)
            src, k, c = CHUNKS[n]
            dst = chunk(n)[:, 0:k * c].rearrange("p (k c) -> p k c", k=k)
            sp.dma_start(dst, src).then_inc(S[f"ring{n % RING}_loaded"], 16)

        x = rows2(0)
        xn, hT = rows2(1), cols8(2)
        qd, kinv = tiles4(3, 0), tiles4(3, 1)
        kend, kend_rows = tiles4(4, 0), unit(4, 1024).rearrange("p (j c) -> p j c", j=NT)
        v_rows, r_rows = rows2(5), rows2(6)
        la, cum = unit(7, 0, 1024).rearrange("p (j c) -> p j c", j=NT), tiles4(7, 1)
        eb, enb = tiles4(8, 0), tiles4(8, 1)
        kx = tiles4(9, 0)
        soft = unit(9, 1024).rearrange("p (j c) -> p j c", j=NT)
        sc_t = unit(10, 0, 1024).rearrange("p (b c) -> p b c", b=8)
        state = unit(10, 1024).rearrange("p (h c) -> p h c", h=GH)
        y_rows, yT = rows2(11), cols8(1)
        sq = unit(9)
        w_alow = unit(12, 0, KD * GRANK).rearrange("p (k r) -> p k r", k=KD)
        w_aup, b_alpha = main[0:GRANK, 12 * U + 512:12 * U + 1024], main[0:1, 12 * U + 1024:12 * U + 1536]
        alT = main[0:GRANK, 12 * U + 1536:12 * U + 1792]
        ss, rstd = small[:, 0:16], small[:, 16:32]
        up_w = [unit(12 + s).rearrange("p (k g c) -> p k g c", k=KD, g=2) for s in range(2)]
        down_w = [unit(14, s * 1024, s * 1024 + 1024) for s in range(2)]
        conv = [unit(3, s * 1024, s * 1024 + 512).rearrange("p (g t) -> p g t", g=2) for s in range(2)]
        sig = [unit(3, s * 1024 + 512, s * 1024 + 768) for s in range(2)]
        hm = [unit(3, s * 1024 + 768, s * 1024 + 1024) for s in range(2)]
        fnorm = unit(4, 0, 1024)
        ident = const("ident")


        ada_w = main[:, 10 * U:12 * U].rearrange("p (k c) -> p k c", k=KD)
        mod = small[:, 32:80]
        cond = small[:, 80:88]
        h1T = cols8(2)
        qaT, khT, vh, yaT = cols8(3), cols8(4), rows2(5), cols8(6)
        ckv, ckvT = unit(7, 0, 512).rearrange("p (j c) -> p j c", j=NT), unit(7, 512, 1024).rearrange("p (c t) -> p c t", c=2)
        qiT = tiles4(7, 1)
        kiT = unit(8, 0, T)
        score = unit(8, 256, 768).rearrange("p (j s) -> p j s", j=NT)
        causneg = unit(8, 768, 1280).rearrange("p (j s) -> p j s", j=NT)
        keep = unit(8, 1280, 1792).rearrange("p (j s) -> p j s", j=NT)
        relu = unit(9).rearrange("p (b c) -> p b c", b=4)
        prob = [unit(9, 1024 * i, 1024 * i + 1024).rearrange("p (h s) -> p h s", h=4) for i in range(2)]
        probT = [unit(15, 1024 * i, 1024 * i + 1024).rearrange("p (h s q) -> p h s q", h=4, s=2) for i in range(2)]
        widx = small[:, 88:104]
        best = small[:, 104:112]
        amax, asum = small[:, 112:128], small[:, 128:144]
        mixed = cols8(1)
        dnT = unit(10, 0, 3 * U).rearrange("p (n t) -> p n t", t=T)
        def probs(i):
            return unit(i).rearrange("p (n c) -> p n c", c=P)

        dt_row, alog_row = small[:, 144:152], small[:, 152:160]
        g_in, beta, soft_g = small[:, 160:176], small[:, 176:192], small[:, 192:208]
        G_col, G_end, eG, beG, tail = (small[:, 208 + 16 * i:224 + 16 * i] for i in range(5))
        ea_row = small[:, 288:296]
        qT, kT, vT = cols8(10), cols8(11), cols8(12)
        rq, rk = cols8(7), cols8(8)
        eGB, decay, decay_beta = probs(3), probs(4), probs(5)
        AT, qkT, N1 = probs(6), probs(7), probs(5)
        AT_level = [probs(8), probs(9)]
        XT, X = probs(11), probs(12)
        kbG, ktail, vbeta = rows2(13), rows2(14), rows2(15)
        nwT = probs(8)
        dstate, vnew = unit(9, 0, 1024).rearrange("p (h c) -> p h c", h=NH), unit(9, 1024).rearrange("p (h c) -> p h c", h=NH)
        z_rows = rows2(4)
        yd_rows, ydT, gate_d = rows2(6), cols8(5), cols8(12)
        gt_row = unit(13, 0, 1024)
        ln_g, ln_b = unit(14, 0, 1024), unit(14, 1024)
        lnt = rows2(7)
        lsum = small[:, 296:298]
        eps_col = small[:, 298:299]
        gate_w, up2_w, down2_w = ([unit(12 + 6 * s + 2 * m, 0, 2 * U) for s in range(2)] for m in range(3))
        h2T = cols8(2)
        w_route = unit(3, 0, KD * (NG + NE)).rearrange("p (k c) -> p k c", k=KD)
        xsel = unit(3, 512, 768).rearrange("p (k s) -> p k s", k=KD)
        sel = unit(3, 768, 832).rearrange("p (j s) -> p j s", j=NT)
        selg = unit(3, 832, 1088).rearrange("p (j q s) -> p j q s", j=NT, q=4)
        selgT = unit(3, 1088, 1344)
        gact, hrows = main[2 * SLOTS:P, 3 * U + 1344:3 * U + 1600], main[0:2 * SLOTS, 3 * U + 1600:3 * U + 1856]
        hidT = unit(4, 0, P).rearrange("p (t s) -> p t s", t=2)
        yexp = unit(4, 128, 384)
        count_f, count_i = unit(4, 384, 416), unit(4, 416, 448).bitcast(I32)
        logits = unit(5, 0, 72).rearrange("p (j c) -> p j c", j=NT)
        grp, ing, pick1, pick2, gate8, both8 = (unit(5, 128 + 16 * i, 144 + 16 * i).rearrange("p (j c) -> p j c", j=NT) for i in range(6))
        cand, ing2, pickg = (unit(5, 256 + 16 * i, 272 + 16 * i).rearrange("p (j c) -> p j c", j=NT) for i in range(3))
        gmax, gsum, top1, top2, ratio, gat1, gat2, first = (unit(5, 320 + 2 * i, 322 + 2 * i) for i in range(8))
        spread = unit(5, 384, 448).rearrange("p (j g i) -> p j g i", j=NT, g=NG)
        chosen, gates_e, rank = (unit(5, 448 + 64 * i, 512 + 64 * i) for i in range(3))
        zero_row = main[0:1, 5 * U + 1024:5 * U + 1152]
        ln_g2, ln_b2 = unit(8, 0, 1024), unit(8, 1024)
        gt_row2 = unit(10, 0, 1024)
        STEPS = {}
        for group, steps in (
            ("gate_sums", (("alow_done", 1), ("alpha_done", 1), ("cum_done", 1))),
            ("gla_inputs", (("alow_copied", 1), ("logs_ready", 1), ("end_diff", 1), ("q_ready", 1), ("k_ready", 2))),
            ("gla_decays", (("alpha_soft", 1), ("cum_ready", 1), ("decays_ready", 2), ("end_decay", 1))),
            ("delta_sums", (("l2_sum", 2), ("gcols_done", 1), ("GB_done", 1), ("bB_done", 1), ("kk_done", 1), ("kq_done", 1), ("k_turned", 1), ("v_turned", 1), ("X_turned", 1), ("w_done", 1))),
            ("delta_ready", (("ab_y", 1), ("g_ready", 1), ("qk_norm", 2), ("gcols_ready", 1), ("tail_diff", 1), ("dec_ready", 1), ("dbeta_ready", 1), ("AT_ready", 1), ("qkT_ready", 1), ("k_rows_ready", 2), ("v_rows_ready", 1))),
            ("delta_decays", (("l2_sq", 2), ("beta_ready", 1), ("ab_abs", 2), ("ab_soft", 1), ("ea_ready", 1), ("l2_root", 2), ("G_exp", 2), ("dec_exp", 1), ("eGB_ready", 1))),
        ):
            sem(group)
            before = 0
            for step_name, n in steps:
                STEPS[step_name] = (group, before)
                before += n

        def made(step_name):
            return S[STEPS[step_name][0]]

        def after(step_name, n):
            group, before = STEPS[step_name]
            return S[group], before + n

        sem("x_loaded", "consts_loaded", "cols_loaded", "alpha_loaded", "dve_step", "act_step",
            "rows_scaled", "square_summed", "root_taken", "turned", "turned_copied", "norm_var")
        sem(
            "v_copied", "r_ready", 
            "kend_turned", "kend_copied", "gscores_done", "gscores_masked",
            "gla_upd", "gla_state", "gla_inter", "y_ready", "y_turned", "yT_ready", "x1_ready")
        sem("up0_loaded", "up1_loaded", "down0_loaded", "down1_loaded", "up_done", "down_done", "conv_tap",
            "conv_part", "conv_ready", "gate_sig", "hm_ready", "x2_ready", "fnorm_loaded", "x3_ready", "stored")
        sem("ada_loaded", "ada_done", "mod_ready", "cond_ready", "mod_plus", "x_turned", "h1_ready", "ckv_ready", "ckv_turned", "ckvT_ready",
            "kidx_ready", "widx_ready", "qidx_ready", "rel_done", "rel_ready", "rel_used", "qatt_ready", "kh_ready", "vh_ready",
            "conv2_tap", "conv2_ready", "act_silu2", "att_scores", "att_masked", "att_max",
            "att_exp", "att_prob", "att_turned", "att_probT", "att_pv", "ya_ready", "gate_a_ready", "mixed_a_ready")
        sem("rows_small_loaded", 
            
            "qd2_ready", "z_ready",
            "level_masked", "XT_ready", "X_ready", "T1_done", "N1_ready", "X_done", "XT_done", "nw_ready", "u_done",
            "ws_done", "vnew_ready", "dn_inter", "dn_upd", "dstate_ready", "dn_o", "gate_d_ready", "yd_ready", "yd_turned", "ydT_ready",
            "mixed_ready", "gt_done", "gt_ready", "ln_in", "ln_sum", "ln_cent", "ln_gb_loaded", "x4_ready", "eps_ready")
        sem("route_loaded", "h2_turned", "h2_ready", "logits_done", "logits_ready", "group_exp", "ratio_exp", "ratio_in", "chosen_ready", "ranks_done",
            "tables_ready", "zero_ready", "experts_a_loaded", "experts_b_loaded", "expert_done", "sel_ready", "xs_done", "xs_ready",
            "gate_up_done", "gate_act", "h_ready", "h_turned", "hT_ready", "down2_done", "yexp_ready", "placed", "selg_turned", "selgT_ready", "xs_scaled", "experts_summed", "x5_ready", "ln_gb2_loaded", "half_placed")

        block = ctx.enter_context(nc.Block())

        @block.sync
        def _(sp):
            sp.dma_start(x, I["x"].rearrange("b (j p) d -> p (b j) d", p=P)).then_inc(S["x_loaded"], 16)
            sp.dma_start(consts[:], I["consts"]).then_inc(S["consts_loaded"], 16)
            sp.dma_start(cols[:], I["cols"]).then_inc(S["cols_loaded"], 16)
            with nc.allow_non_contiguous_dma(reason="64-byte rows of the low-rank projection"):
                sp.dma_start(w_alow, w_gla[:, 3072:3088].rearrange("(k p) r -> p k r", p=P)).then_inc(S["alpha_loaded"], 16)
            sp.dma_start(w_aup, I["l0_gla_w_alpha_up"]).then_inc(S["alpha_loaded"], 16)
            sp.dma_start(b_alpha, I["l0_gla_b_alpha"].unsqueeze(0)).then_inc(S["alpha_loaded"], 16)
            sp.dma_start(dt_row, I["dt_bias_2"].broadcast_to([P, NH])).then_inc(S["rows_small_loaded"], 16)
            sp.dma_start(alog_row, I["a_log_2"].broadcast_to([P, NH])).then_inc(S["rows_small_loaded"], 16)
            for n in range(N_FIRST):
                load_ring(sp, n)

            def load_ff(i, s, used=None):
                if used is not None:
                    sp.wait_ge(S["up_done"], used)
                w = I["l0_ffn_w_up"].rearrange("(k p) c -> p k c", p=P)
                for g in range(2):
                    sp.dma_start(up_w[s][:, :, g, :], w[:, :, bass.ds(i * P + g * FF, P)]).then_inc(S[f"up{s}_loaded"], 16)
                if used is not None:
                    sp.wait_ge(S["down_done"], used)
                sp.dma_start(down_w[s], I["l0_ffn_w_down"][bass.ds(i * P, P), :]).then_inc(S[f"down{s}_loaded"], 16)

            sp.wait_ge(*after("alpha_done", 1))
            load_ff(0, 0)
            load_ff(1, 1)
            def load_ada(i, used=None):
                if used is not None:
                    sp.wait_ge(S["ada_done"], used)
                sp.dma_start(ada_w, I["w_ada_2"].rearrange("b (k p) c -> p (b k) c", p=P)[:, :, bass.ds(i * HALF, HALF)]).then_inc(S["ada_loaded"], 16)

            sp.wait_ge(S["y_turned"], 4)
            load_ada(0)
            for n in range(N_FIRST, N_FIRST + RING):
                load_ring(sp, n)
            with sp.Fori(1, FT // 2) as i:
                load_ff(i * 2, 0, i * 2 - 1)
                load_ff(i * 2 + 1, 1, i * 2)
                load_ada(i, i)
            load_ada(11, 11)
            sp.dma_start(fnorm, I["final_norm"].unsqueeze(0).broadcast_to([P, D])).then_inc(S["fnorm_loaded"], 16)
            for n in range(N_FIRST + RING, N_SECOND):
                load_ring(sp, n)
            sp.wait_ge(S["dn_o"], 4)
            sp.dma_start(ln_g, I["ln_g_2"][:, 0, :].broadcast_to([P, D])).then_inc(S["ln_gb_loaded"], 16)
            sp.dma_start(ln_b, I["ln_b_2"][:, 0, :].broadcast_to([P, D])).then_inc(S["ln_gb_loaded"], 16)
            w_r = sp.dma_start(w_route[:, :, 0:NG], I["w_route_grp_2"].rearrange("b (k p) c -> p (b k) c", p=P))
            w_r.then_inc(S["route_loaded"], 16)
            sp.dma_start(w_route[:, :, NG:], I["w_route_exp_2"].rearrange("b (k p) c -> p (b k) c", p=P)).then_inc(S["route_loaded"], 16)
            sp.dma_start(ln_g2, I["ln_g_2"][:, 1, :].broadcast_to([P, D])).then_inc(S["ln_gb2_loaded"], 16)
            sp.dma_start(ln_b2, I["ln_b_2"][:, 1, :].broadcast_to([P, D])).then_inc(S["ln_gb2_loaded"], 16)

            def load_expert(e, s, done=None):
                if done is not None:
                    sp.wait_ge(S["expert_done"], done)
                loaded = S["experts_a_loaded" if s == 0 else "experts_b_loaded"]
                for w, name in ((gate_w[s], "w_gate_2"), (up2_w[s], "w_up_2")):
                    sp.dma_start(w.rearrange("p (k c) -> p k c", k=KD),
                                 I[name].rearrange("b e (k p) c -> p (b e) k c", p=P)[:, bass.ds(e, 1)]).then_inc(loaded, 16)
                sp.dma_start(down2_w[s].rearrange("p (k c) -> p k c", k=4),
                             I["w_down_2"].rearrange("b e (k p) c -> p (b e) k c", p=P)[:, bass.ds(e, 1)]).then_inc(loaded, 16)

            sp.wait_ge(S["x4_ready"], 2)
            load_expert(0, 0)
            load_expert(1, 1)
            with sp.Fori(1, NE // 2) as i:
                for s in range(2):
                    load_expert(i * 2 + s, s, i * 2 + s - 1)
            for j in range(NT):
                sp.wait_ge(S["x5_ready"], j + 1)
                sp.dma_start(out.rearrange("b (j p) d -> p (b j) d", p=P)[:, j, :], x[:, j, :]).then_inc(S["stored"], 16)
            sp.wait_ge(S["stored"], 32)

        @block.tensor
        def _(pe):
            def turn_rows(src, banks, done):
                for j in range(NT):
                    for kk in range(2):
                        for q in range(4):
                            m = pe.transpose(ps[:, banks[2 * j + kk], q * P:(q + 1) * P],
                                             src[:, j, (4 * kk + q) * P:(4 * kk + q + 1) * P], ident)
                        m.then_inc(S[done] if done in S else made(done), 1)

            def project_cols(n, banks, lhs=None, first=0, tiles=4, act=None):
                for m4 in range(tiles):
                    for k in range(KD):
                        m = pe.matmul(ps[:, banks[m4 // 2], (m4 % 2) * T:(m4 % 2) * T + T],
                                      chunk8(n)[:, k, m4 * P:(m4 + 1) * P], act[:, k, :], start=(k == 0), stop=(k == KD - 1))
                m.then_inc(S["chunk_done"], 1)

            def project_rows(n, banks, act):
                for j in range(NT):
                    for k in range(KD):
                        m = pe.matmul(ps[:, banks[j], :], act[:, k, j * P:(j + 1) * P], chunk8(n)[:, k, :],
                                      start=(k == 0), stop=(k == KD - 1))
                m.then_inc(S["chunk_done"], 1)

            pe.wait_ge(S["consts_loaded"], 16)
            pe.wait_ge(S["rows_scaled"], 2)
            turn_rows(xn, (0, 1, 2, 3), "turned")
            pe.wait_ge(S["turned_copied"], 4)
            pe.wait_ge(S["alpha_loaded"], 48)
            for k in range(KD):
                m = pe.matmul(ps[0:GRANK, 4, 0:T], w_alow[:, k, :], hT[:, k, :], start=(k == 0), stop=(k == KD - 1))
            m.then_inc(made("alow_done"), 1)
            ring_wait(pe, 0)
            project_cols(0, (0, 1), act=hT)
            pe.wait_ge(*after("alow_copied", 1))
            for j in range(NT):
                pe.matmul(ps[:, 5 + j, :], alT[:, j * P:(j + 1) * P], w_aup, start=True, stop=False)
                m = pe.matmul(ps[:, 5 + j, :], const("ones")[0:1, :], b_alpha, start=False, stop=True)
            m.then_inc(made("alpha_done"), 1)
            ring_wait(pe, 1)
            project_cols(1, (2, 3), act=hT)
            pe.wait_ge(*after("logs_ready", 1))
            for j in range(NT):
                for h in range(GH):
                    m = pe.matmul(ps[:, 5 + j, h * P:(h + 1) * P], la[:, j, h * P:(h + 1) * P], const("upto"), start=True, stop=True)
            m.then_inc(made("cum_done"), 1)
            ring_wait(pe, 2)
            project_rows(2, (4, 7), hT)
            ring_wait(pe, 3)
            pe.wait_ge(*after("q_ready", 1))
            project_rows(3, (0, 1), hT)
            ring_wait(pe, 4)
            pe.wait_ge(S["v_copied"], 2)
            project_rows(4, (4, 7), hT)
            ring_wait(pe, 5)
            pe.wait_ge(*after("k_ready", 2))
            project_rows(5, (2, 3), hT)
            for j in range(NT):
                for h in range(GH):
                    m = pe.transpose(ps[:, 5 + j, h * P:(h + 1) * P], kend[:, h, j * P:(j + 1) * P], ident)
                m.then_inc(S["kend_turned"], 1)
            pe.wait_ge(S["v_copied"], 4)
            for j in range(NT):
                for h in range(GH):
                    t = slice(j * P, (j + 1) * P)
                    m = pe.matmul(ps[:, j, h * P:(h + 1) * P], kinv[:, h, t], qd[:, h, t], start=True, stop=True)
                m.then_inc(S["gscores_done"], 1)

            O_BANK = {(0, 0): 2, (0, 1): 3, (1, 0): 4, (1, 1): 7}

            def gla_update(c, banks):
                j, r = c // 2, (c % 2) * CH
                for h in range(GH):
                    m = pe.matmul(ps[:, banks[h // 2], (h % 2) * GDV:(h % 2 + 1) * GDV],
                                  kend_rows[r:r + CH, j, h * P:(h + 1) * P], v_rows[r:r + CH, j, h * GDV:(h + 1) * GDV],
                                  start=True, stop=True)
                m.then_inc(S["gla_upd"], 1)

            def gla_intra(j):
                for h in range(GH):
                    m = pe.matmul(ps[:, O_BANK[j, h // 2], (h % 2) * GDV:(h % 2 + 1) * GDV], sc_t[:, 4 * j + h, :],
                                  v_rows[:, j, h * GDV:(h + 1) * GDV], start=(h % 2 == 0), stop=False, skip_group_check=True)

            def gla_inter(c, last):
                j, r = c // 2, (c % 2) * CH
                pe.wait_ge(S["gla_state"], c)
                for h in range(GH):
                    m = pe.matmul(ps[r:r + CH, O_BANK[j, h // 2], (h % 2) * GDV:(h % 2 + 1) * GDV],
                                  qd[:, h, c * CH:(c + 1) * CH], state[:, h, :], start=False, stop=last, skip_group_check=True)
                m.then_inc(S["gla_inter"], 1)

            pe.wait_ge(S["kend_copied"], 2)
            gla_update(0, (5, 6))
            pe.wait_ge(S["gscores_masked"], 2)
            gla_update(1, (0, 1))
            pe.wait_ge(S["r_ready"], 4)
            gla_intra(0)
            gla_inter(1, True)
            gla_update(2, (5, 6))
            gla_intra(1)
            gla_inter(2, False)
            gla_inter(3, True)
            pe.wait_ge(S["y_ready"], 2)
            turn_rows(y_rows, (0, 1, 5, 6), "y_turned")
            pe.wait_ge(S["yT_ready"], 4)
            ring_wait(pe, 6)
            project_rows(6, (2, 4), yT)
            ring_wait(pe, 7)
            project_rows(7, (3, 7), yT)
            pe.wait_ge(S["rows_scaled"], 4)
            turn_rows(xn, (4, 5, 6, 7), "turned")
            for j in range(NT):
                for half in range(2):
                    pe.matmul(ps[:, 2 * j + half, :], ident, x[:, j, half * HALF:(half + 1) * HALF], start=True, stop=False)
            pe.wait_ge(S["turned_copied"], 8)

            def ff_up(i, s, free):
                pe.wait_ge(S[f"up{s}_loaded"], (i // 2 + 1) * 32 if isinstance(i, int) else free[1])
                if free[0] is not None:
                    pe.wait_ge(S["conv_ready"], free[0])
                for g in range(2):
                    for k in range(KD):
                        m = pe.matmul(ps[:, 4 + s, g * T:(g + 1) * T], up_w[s][:, k, g, :], hT[:, k, :],
                                      start=(k == 0), stop=(k == KD - 1))
                m.then_inc(S["up_done"], 1)

            def ff_down(done, loaded, s, last=False):
                pe.wait_ge(S["hm_ready"], done)
                pe.wait_ge(S[f"down{s}_loaded"], loaded)
                for j in range(NT):
                    for half in range(2):
                        m = pe.matmul(ps[:, 2 * j + half, :], hm[s][:, j * P:(j + 1) * P],
                                      down_w[s][:, half * HALF:(half + 1) * HALF], start=False, stop=last)
                m.then_inc(S["down_done"], 1)

            def ada(n, loaded):
                pe.wait_ge(S["ada_loaded"], loaded)
                if n is not None:
                    pe.wait_ge(S["mod_ready"], n)
                for m4 in range(4):
                    for k in range(KD):
                        m = pe.matmul(ps[:, 6, m4:m4 + 1], ada_w[:, k, m4 * P:(m4 + 1) * P], cond[:, k:k + 1],
                                      start=(k == 0), stop=(k == KD - 1))
                m.then_inc(S["ada_done"], 1)

            ff_up(0, 0, (None,))
            ff_up(1, 1, (None,))
            pe.wait_ge(S["cond_ready"], 1)
            ada(None, 16)
            ff_down(1, 16, 0)
            with pe.Fori(1, FT // 2) as i:
                ff_up(i * 2, 0, (i * 2 - 1, i * 32 + 32))
                ff_down(i * 2, i * 16, 1)
                ff_up(i * 2 + 1, 1, (i * 2, i * 32 + 32))
                ada(i, i * 16 + 16)
                ff_down(i * 2 + 1, i * 16 + 16, 0)
            ada(11, 16 * 12)
            ff_down(FT, 16 * (FT // 2), 1, last=True)
            def turn_k(src, done):
                for k in range(KD):
                    for j in range(NT):
                        m = pe.transpose(ps[:, 4 + k // 2, (k % 2) * T + j * P:(k % 2) * T + (j + 1) * P], src[:, j, k * P:(k + 1) * P], ident)
                    if k % 2:
                        m.then_inc(S[done] if done in S else made(done), 1)

            pe.wait_ge(S["conv_ready"], FT)
            pe.wait_ge(S["mod_ready"], 12)
            pe.wait_ge(S["x3_ready"], 2)
            turn_k(x, "x_turned")
            pe.wait_ge(S["h1_ready"], 8)
            ring_wait(pe, C_CKV)
            for j in range(NT):
                for k in range(KD):
                    m = pe.matmul(ps[:, 0, j * LAT:(j + 1) * LAT], h1T[:, k, j * P:(j + 1) * P],
                                  chunk(C_CKV)[:, k * LAT:(k + 1) * LAT], start=(k == 0), stop=(k == KD - 1))
            m.then_inc(S["chunk_done"], 1)
            ring_wait(pe, C_KW)
            kw = chunk(C_KW)[:, 0:KD * 72].rearrange("p (k c) -> p k c", k=KD)
            for k in range(KD):
                pe.matmul(ps[0:IDH, 1, 0:T], kw[:, k, 0:IDH], h1T[:, k, :], start=(k == 0), stop=(k == KD - 1))
            for j in range(NT):
                for k in range(KD):
                    m = pe.matmul(ps[:, 2, j * IH:(j + 1) * IH], h1T[:, k, j * P:(j + 1) * P], kw[:, k, IDH:72],
                                  start=(k == 0), stop=(k == KD - 1))
            m.then_inc(S["chunk_done"], 1)
            ring_wait(pe, C_QI)
            project_cols(C_QI, (4, 5), act=h1T)

            def index_scores(j):
                for h in range(IH):
                    r, q = (h % 2) * IDH, h // 2
                    m = pe.matmul(ps[:, 4 + (h % 2) * 2 + q // 2, (q % 2) * T:(q % 2 + 1) * T],
                                  qiT[r:r + IDH, q, j * P:(j + 1) * P], kiT[r:r + IDH, :], start=True, stop=True)
                m.then_inc(S["rel_done"], 1)

            pe.wait_ge(S["qidx_ready"], 1)
            pe.wait_ge(S["kidx_ready"], 2)
            index_scores(0)
            ring_wait(pe, C_QA[0])
            pe.wait_ge(S["widx_ready"], 1)
            project_cols(C_QA[0], (2, 3), act=h1T)
            pe.wait_ge(S["rel_ready"], 4)
            index_scores(1)
            pe.wait_ge(S["ckv_ready"], 2)
            for c in range(2):
                for j in range(NT):
                    m = pe.transpose(ps[:, 0, c * T + j * P:c * T + (j + 1) * P], ckv[:, j, c * P:(c + 1) * P], ident)
            m.then_inc(S["ckv_turned"], 1)
            ring_wait(pe, C_QA[1])
            pe.wait_ge(S["qatt_ready"], 1)
            project_cols(C_QA[1], (2, 3), act=h1T)
            ring_wait(pe, C_UK)
            uk = chunk(C_UK)[:, 0:16 * P].rearrange("p (m d) -> p m d", m=16)
            pe.wait_ge(S["ckvT_ready"], 1)
            pe.wait_ge(S["qatt_ready"], 2)
            for h in range(AH):
                for c in range(2):
                    m = pe.matmul(ps[:, h // 2, (h % 2) * T:(h % 2 + 1) * T], uk[:, 2 * h + c, :], ckvT[:, c, :], start=(c == 0), stop=(c == 1))
            m.then_inc(S["chunk_done"], 1)
            ring_wait(pe, C_UV)
            uv = chunk(C_UV)[:, 0:16 * P].rearrange("p (h c d) -> p c h d", h=AH, c=2)
            pe.wait_ge(S["kh_ready"], 2)
            for j in range(NT):
                for half in range(2):
                    for c in range(2):
                        m = pe.matmul(ps[:, 2 * j + half, :], ckvT[:, c, j * P:(j + 1) * P], uv[:, c, 4 * half:4 * half + 4, :], start=(c == 0), stop=(c == 1))
            m.then_inc(S["chunk_done"], 1)
            pe.wait_ge(S["rel_ready"], 8)
            for i in range(6):
                ring_wait(pe, C_QKVD[i])
                if i >= 2:
                    pe.wait_ge(S["conv2_ready"], 4 * (i - 1))
                project_cols(C_QKVD[i], (4, 5) if i % 2 == 0 else (6, 7), act=h1T)
            pe.wait_ge(S["vh_ready"], 4)
            pe.wait_ge(S["conv2_ready"], 24)
            GROUPS = [(j, g) for j in range(NT) for g in range(2)]

            def att_scores(n):
                j, g = GROUPS[n]
                if n >= 1:
                    pe.wait_ge(S["att_masked"], n)
                for i in range(4):
                    h, w = 4 * g + i, P * (j + 1)
                    m = pe.matmul(ps[:, i // 2, (i % 2) * T:(i % 2) * T + w], qaT[:, h, j * P:(j + 1) * P], khT[:, h, 0:w], start=True, stop=True)
                m.then_inc(S["att_scores"], 1)

            def att_out(n):
                j, g = GROUPS[n]
                pe.wait_ge(S["att_prob"], n + 1)
                if n >= 1:
                    pe.wait_ge(S["att_probT"], n)
                for i in range(4):
                    for s in range(j + 1):
                        m = pe.transpose(ps[:, 4 + i // 2, ((i % 2) * 2 + s) * P:((i % 2) * 2 + s + 1) * P], prob[n % 2][:, i, s * P:(s + 1) * P], ident)
                m.then_inc(S["att_turned"], 1)
                pe.wait_ge(S["att_probT"], n + 1)
                if n >= 2:
                    pe.wait_ge(S["ya_ready"], n - 1)
                for i in range(4):
                    h = 4 * g + i
                    for s in range(j + 1):
                        m = pe.matmul(ps[:, 2 + n % 2, i * P:(i + 1) * P], vh[:, s, h * P:(h + 1) * P], probT[n % 2][:, i, s, :],
                                      start=(s == 0), stop=(s == j))
                m.then_inc(S["att_pv"], 1)

            att_scores(0)
            for n in range(4):
                if n + 1 < 4:
                    att_scores(n + 1)
                att_out(n)
            pe.wait_ge(S["att_masked"], 4)
            pe.wait_ge(S["ya_ready"], 4)
            for i in range(2):
                ring_wait(pe, C_GA[i])
                project_cols(C_GA[i], (2 * i, 2 * i + 1), act=h1T)
            for i in range(2):
                ring_wait(pe, C_BRA[i])
                project_cols(C_BRA[i], (4 + 2 * i, 5 + 2 * i), act=yaT)
            ring_wait(pe, C_AB)
            ab = chunk(C_AB)[:, 0:KD * 16].rearrange("p (k c) -> p k c", k=KD)
            pe.wait_ge(S["gate_a_ready"], 2)
            for j in range(NT):
                for k in range(KD):
                    m = pe.matmul(ps[:, 0, j * 16:(j + 1) * 16], h1T[:, k, j * P:(j + 1) * P], ab[:, k, :], start=(k == 0), stop=(k == KD - 1))
            m.then_inc(S["chunk_done"], 1)
            pe.wait_ge(S["mixed_a_ready"], 2)
            for i, (r, b0) in enumerate(((rq, 4), (rk, 0))):
                pe.wait_ge(*after("l2_sq", i + 1))
                if i == 1:
                    pe.wait_ge(*after("ab_y", 1))
                for b in range(4):
                    m = pe.matmul(bank(b0 + b), const("ones"), r[:, 2 * b:2 * b + 2, :], start=True, stop=True)
                m.then_inc(made("l2_sum"), 1)
            pe.wait_ge(*after("g_ready", 1))
            pe.wait_ge(*after("l2_root", 2))
            for j in range(NT):
                pe.matmul(ps[:, 0, j * 8:(j + 1) * 8], const("upto"), g_in[:, j * 8:(j + 1) * 8], start=True, stop=True)
                m = pe.matmul(ps[:, 0, 16 + j * 8:24 + j * 8], const("chunk"), g_in[:, j * 8:(j + 1) * 8], start=True, stop=True)
            m.then_inc(made("gcols_done"), 1)
            for h in range(NH):
                for j in range(NT):
                    m = pe.matmul(ps[:, 4 + h // 2, (h % 2) * T + j * P:(h % 2) * T + (j + 1) * P],
                                  g_in[:, j * 8 + h:j * 8 + h + 1].broadcast_to([P, P]), const("upto"), start=True, stop=True)
            m.then_inc(made("GB_done"), 1)
            pe.wait_ge(*after("gcols_ready", 1))
            for h in range(NH):
                for j in range(NT):
                    m = pe.matmul(ps[:, h // 2, (h % 2) * T + j * P:(h % 2) * T + (j + 1) * P],
                                  beta[:, j * 8 + h:j * 8 + h + 1].broadcast_to([P, P]), ident, start=True, stop=True)
            m.then_inc(made("bB_done"), 1)

            def each(out0, f):
                for n in range(16):
                    m = f(ps[:, out0 + n // 4, (n % 4) * P:(n % 4 + 1) * P], n // 2, n % 2, n)
                return m

            def span(j):
                return slice(j * P, (j + 1) * P)

            pe.wait_ge(*after("qk_norm", 2))
            pe.wait_ge(*after("eGB_ready", 1))
            each(4, lambda o, h, j, n: pe.matmul(o, kT[:, h, span(j)], kT[:, h, span(j)], start=True, stop=True)).then_inc(made("kk_done"), 1)
            pe.wait_ge(*after("dbeta_ready", 1))
            each(0, lambda o, h, j, n: pe.matmul(o, kT[:, h, span(j)], qT[:, h, span(j)], start=True, stop=True)).then_inc(made("kq_done"), 1)
            pe.wait_ge(*after("AT_ready", 1))
            for j in range(NT):
                for h in range(NH):
                    m = pe.transpose(ps[:, 4 + 2 * j + h // 4, (h % 4) * P:(h % 4 + 1) * P], kT[:, h, span(j)], ident)
            m.then_inc(made("k_turned"), 1)
            pe.wait_ge(*after("qkT_ready", 1))
            for j in range(NT):
                for h in range(NH):
                    m = pe.transpose(ps[:, 2 * j + h // 4, (h % 4) * P:(h % 4 + 1) * P], vT[:, h, span(j)], ident)
            m.then_inc(made("v_turned"), 1)
            pe.wait_ge(*after("k_rows_ready", 2))
            for i in range(2):
                ring_wait(pe, C_Z[i])
                project_rows(C_Z[i], (4 + i, 6 + i), h1T)
            pe.wait_ge(S["XT_ready"], 1)
            pe.wait_ge(S["z_ready"], 4)
            each(4, lambda o, h, j, n: pe.transpose(o, XT[:, n, :], ident)).then_inc(made("X_turned"), 1)
            pe.wait_ge(*after("v_rows_ready", 1))

            def four(g, out0, f):
                for n in range(4 * g, 4 * g + 4):
                    m = f(ps[:, out0 + g, (n % 4) * P:(n % 4 + 1) * P], n)
                return m

            for level in range(1, 6):
                A_l = AT_level[level % 2]
                pe.wait_ge(S["level_masked"], level + 1)
                for g in range(4):
                    pe.wait_ge(S["X_ready"], 4 * (level - 1) + g + 1)
                    if level > 1:
                        pe.wait_ge(S["XT_ready"], 4 * (level - 2) + g + 2)
                    four(g, 0, lambda o, n: pe.matmul(o, A_l[:, n, :], X[:, n, :], start=True, stop=True)).then_inc(S["T1_done"], 1)
                for g in range(4):
                    pe.wait_ge(S["N1_ready"], 4 * (level - 1) + g + 1)
                    if level < 5:
                        four(g, 4, lambda o, n: pe.matmul(o, XT[:, n, :], N1[:, n, :], start=True, stop=True)).then_inc(S["X_done"], 1)
                    four(g, 0, lambda o, n: pe.matmul(o, N1[:, n, :], XT[:, n, :], start=True, stop=True)).then_inc(S["XT_done"], 1)
            pe.wait_ge(S["XT_ready"], 1 + 4 * 5)
            pe.wait_ge(S["X_ready"], 4 * 5)
            each(4, lambda o, h, j, n: pe.matmul(o, kbG[:, j, h * P:(h + 1) * P], XT[:, n, :], start=True, stop=True)).then_inc(made("w_done"), 1)

            def dn_heads(f):
                for h in range(NH):
                    m = f(h)
                return m

            for j in range(NT):
                if j == 1:
                    pe.wait_ge(S["vnew_ready"], 2)
                dn_heads(lambda h: pe.matmul(ps[:, h // 4, (h % 4) * P:(h % 4 + 1) * P], XT[:, 2 * h + j, :], vbeta[:, j, h * P:(h + 1) * P],
                                             start=(h % 4 == 0), stop=False, skip_group_check=True)).then_inc(S["u_done"], 1)
                for half in range(2):
                    c, r = 2 * j + half, half * CH
                    ob = 2 if j == 0 else 6

                    def part(b0, h):
                        return ps[r:r + CH, b0 + h // 4, (h % 4) * P:(h % 4 + 1) * P]

                    if c > 0:
                        pe.wait_ge(S["dstate_ready"], c)
                        pe.wait_ge(S["qd2_ready"], 1)
                        pe.wait_ge(S["nw_ready"], 1)
                        dn_heads(lambda h: pe.matmul(part(0, h), nwT[:, 2 * h + j, r:r + CH], dstate[:, h, :], start=False, stop=True,
                                                     skip_group_check=True)).then_inc(S["ws_done"], 1)
                        dn_heads(lambda h: pe.matmul(part(ob, h), qT[:, h, c * CH:(c + 1) * CH], dstate[:, h, :], start=(h % 4 == 0), stop=False,
                                                     skip_group_check=True)).then_inc(S["dn_inter"], 1)
                    pe.wait_ge(S["vnew_ready"], c + 1)
                    if c < NCH - 1:
                        if c == 0:
                            pe.wait_ge(S["nw_ready"], 1)
                        dn_heads(lambda h: pe.matmul(ps[:, 4 + h // 4, (h % 4) * P:(h % 4 + 1) * P], ktail[r:r + CH, j, h * P:(h + 1) * P],
                                                     vnew[r:r + CH, h, :], start=True, stop=True)).then_inc(S["dn_upd"], 1)
                    dn_heads(lambda h: pe.matmul(part(ob, h), qkT[r:r + CH, 2 * h + j, r:r + CH], vnew[r:r + CH, h, :],
                                                 start=(c == 0 and h % 4 == 0), stop=True, skip_group_check=True)).then_inc(S["dn_o"], 1)
            for i, banks in enumerate(((0, 1), (4, 5))):
                ring_wait(pe, C_GD[i])
                project_cols(C_GD[i], banks, act=h1T)
            pe.wait_ge(S["yd_ready"], 2)
            pe.wait_ge(S["gate_d_ready"], 2)
            turn_rows(yd_rows, (0, 1, 4, 5), "yd_turned")
            pe.wait_ge(S["ydT_ready"], 4)
            for i, banks in enumerate(((2, 3), (6, 7))):
                ring_wait(pe, C_BRD[i])
                project_cols(C_BRD[i], banks, act=ydT)
            pe.wait_ge(S["mixed_ready"], 1)
            for k in range(KD):
                m = pe.matmul(ps[:, 2 + k // 4, (k % 4) * P:(k % 4 + 1) * P], mod[:, 16 + k:17 + k].broadcast_to([P, P]), ident, start=True, stop=True)
            m.then_inc(S["gt_done"], 1)
            pe.wait_ge(S["mixed_ready"], 2)
            for i, banks in enumerate(((0, 4), (1, 5))):
                ring_wait(pe, C_WO[i])
                project_rows(C_WO[i], banks, mixed)
            pe.wait_ge(S["x4_ready"], 2)
            turn_k(x, "h2_turned")
            pe.wait_ge(S["zero_ready"], 1)
            for b in range(4):
                m = pe.matmul(bank(b), zero_row, consts[0:1, 0:HALF], start=True, stop=False, skip_group_check=True)
            pe.wait_ge(S["h2_ready"], 8)
            pe.wait_ge(S["route_loaded"], 32)
            for j in range(NT):
                for k in range(KD):
                    m = pe.matmul(ps[:, 4, j * 36:(j + 1) * 36], h2T[:, k, j * P:(j + 1) * P], w_route[:, k, :], start=(k == 0), stop=(k == KD - 1))
            m.then_inc(S["logits_done"], 1)
            pe.wait_ge(S["chosen_ready"], 1)
            pe.matmul(ps[:, 5, 0:NE], const("earlier"), chosen[:, 0:NE], start=True, stop=True)
            pe.matmul(ps[:, 5, NE:2 * NE], const("ones"), chosen[:, 0:NE], start=True, stop=False)
            pe.matmul(ps[:, 5, NE:2 * NE], const("earlier"), chosen[:, NE:2 * NE], start=False, stop=True)
            pe.matmul(ps[:, 5, 2 * NE:3 * NE], const("ones"), chosen[:, 0:NE], start=True, stop=False)
            pe.matmul(ps[:, 5, 2 * NE:3 * NE], const("ones"), chosen[:, NE:2 * NE], start=False, stop=True).then_inc(S["ranks_done"], 1)
            pe.wait_ge(S["tables_ready"], 1)
            blocks = pe.alloc_register("pe_blocks")
            pe.reg_mov(blocks, 0)

            def pe_block(s):
                n = pe.snap(blocks)
                gw, uw = (w[s].rearrange("p (k c) -> p k c", k=KD) for w in (gate_w, up2_w))
                dw = down2_w[s].rearrange("p (k c) -> p k c", k=4)
                pe.wait_ge(S["sel_ready"], n + 1)
                for k in range(KD):
                    for j in range(NT):
                        m = pe.matmul(ps[:, 4, k * SLOTS:(k + 1) * SLOTS], x[:, j, k * P:(k + 1) * P], sel[:, j, :], start=(j == 0), stop=(j == 1))
                m.then_inc(S["xs_done"], 1)
                pe.wait_ge(S["xs_ready"], n + 1)
                for k in range(KD):
                    for q in range(4):
                        w = (gw, uw)[q // 2][:, k, (q % 2) * T:(q % 2 + 1) * T]
                        m = pe.matmul(ps[q * SLOTS:(q + 1) * SLOTS, 5, 0:T], xsel[:, k, :], w, start=(k == 0), stop=(k == KD - 1))
                m.then_inc(S["gate_up_done"], 1)
                pe.wait_ge(S["h_ready"], n + 1)
                for j in range(NT):
                    m = pe.transpose(ps[:, 6, j * P:(j + 1) * P], selg[:, j].rearrange("p q s -> p (q s)"), ident)
                m.then_inc(S["selg_turned"], 1)
                for t in range(2):
                    m = pe.transpose(ps[:, 4, t * 2 * SLOTS:(t + 1) * 2 * SLOTS], hrows[:, t * P:(t + 1) * P], ident[0:2 * SLOTS, 0:2 * SLOTS])
                m.then_inc(S["h_turned"], 1)
                pe.wait_ge(S["hT_ready"], n + 1)
                for kt in range(4):
                    for q in range(4):
                        m = pe.matmul(ps[q * SLOTS:(q + 1) * SLOTS, 7, 0:T], hidT[:, kt % 2, (kt // 2) * SLOTS:(kt // 2 + 1) * SLOTS],
                                      dw[:, kt, q * T:(q + 1) * T], start=(kt == 0), stop=(kt == 3))
                m.then_inc(S["down2_done"], 1)
                pe.wait_ge(S["yexp_ready"], n + 1)
                pe.wait_ge(S["selgT_ready"], n + 1)
                for part in (((0, 0), (2, 0), (1, 1), (3, 1)), ((1, 0), (3, 0), (0, 1), (2, 1))):
                    for q, j in part:
                        g = slice(q * SLOTS, (q + 1) * SLOTS)
                        m = pe.matmul(ps[:, 2 * j + q // 2, (q % 2) * T:(q % 2 + 1) * T], selgT[g, j * P:(j + 1) * P], yexp[g, :],
                                      start=False, stop=False, skip_group_check=True)
                        m.then_inc(S["placed"], 1)
                    if part[0] == (0, 0):
                        pe.wait_ge(S["placed"], n * 8 + 4)
                pe.wait_ge(S["placed"], n * 8 + 8)
                pe.reg_add(blocks, blocks, 1)

            with pe.Fori(0, NE // 2) as i:
                for s in range(2):
                    pe.wait_ge(S["experts_a_loaded" if s == 0 else "experts_b_loaded"], i * 48 + 48)
                    count = pe.value_load(count_i[0:1, bass.ds(i * 2 + s, 1)], min_val=0, max_val=T)
                    pe_block(s)
                    with pe.If(count > SLOTS):
                        pe_block(s)
                    with pe.If(count > 2 * SLOTS):
                        with pe.Fori(2, T // SLOTS):
                            pe_block(s)
                    pe.drain().then_inc(S["expert_done"], 1)
            pe.drain().then_inc(S["experts_summed"], 1)
            for k in range(KD):
                m = pe.matmul(ps[:, 4 + k // 4, (k % 4) * P:(k % 4 + 1) * P], mod[:, 40 + k:41 + k].broadcast_to([P, P]), ident, start=True, stop=True)
            m.then_inc(S["gt_done"], 1)

        @block.scalar
        def _(act):
            steps = [0]

            def norm_root(r, srcs, n):
                for i, src in enumerate(srcs):
                    act.activation(sq[:, i * src.shape[-1]:(i + 1) * src.shape[-1]], src, ACT.Square, accum_out=ss[:, i:i + 1]).then_inc(S["square_summed"], 1)
                act.wait_ge(S["norm_var"], r + 1)
                act.activation(rstd[:, 0:n], rstd[:, 0:n], ACT.Sqrt).then_inc(S["root_taken"], 1)

            act.wait_ge(S["x_loaded"], 16)
            norm_root(0, [x[:, j, :] for j in range(NT)], NT)
            act.wait_ge(*after("alpha_done", 1))
            z = bank(5, 2).rearrange("p (j c) -> p j c", j=NT)
            act.activation(soft, z, ACT.Abs).then_inc(S["act_step"], 1)
            act.wait_ge(S["act_step"], 1)
            act.activation(soft, soft, ACT.Exp, scale=-1.0).then_inc(S["act_step"], 1)
            act.wait_ge(S["act_step"], 2)
            act.activation(soft, soft, ACT.Ln, bias=1.0).then_inc(made("alpha_soft"), 1)
            act.wait_ge(*after("cum_done", 1))
            by_head = bank(5, 2).rearrange("p (j h t) -> p h j t", j=NT, h=GH)
            act.activation(cum.rearrange("p h (j t) -> p h j t", j=NT), by_head, ACT.Copy, scale=1.0 / GTAU).then_inc(made("cum_ready"), 1)
            act.wait_ge(*after("cum_ready", 1))
            act.activation(eb, cum, ACT.Exp).then_inc(made("decays_ready"), 1)
            act.activation(enb, cum, ACT.Exp, scale=-1.0).then_inc(made("decays_ready"), 1)
            act.wait_ge(*after("end_diff", 1))
            act.activation(kx, kx, ACT.Exp).then_inc(made("end_decay"), 1)
            for half, banks in ((0, (4, 7)), (1, (0, 1))):
                act.wait_ge(S["chunk_done"], 3 + half)
                for j in range(NT):
                    act.activation(v_rows[:, j, half * HALF:(half + 1) * HALF], bank(banks[j]), ACT.Copy).then_inc(S["v_copied"], 1)
            for half, banks in ((0, (4, 7)), (1, (2, 3))):
                act.wait_ge(S["chunk_done"], 5 + half)
                for j in range(NT):
                    act.activation(r_rows[:, j, half * HALF:(half + 1) * HALF], bank(banks[j]), ACT.Silu).then_inc(S["r_ready"], 1)
            for j in range(NT):
                act.wait_ge(S["kend_turned"], j + 1)
                act.activation(kend_rows[:, j, :], bank(5 + j), ACT.Copy).then_inc(S["kend_copied"], 1)
            act.wait_ge(S["gla_inter"], 3)
            o_banks = {(0, 0): 2, (0, 1): 3, (1, 0): 4, (1, 1): 7}
            norm_root(1, [bank(o_banks[j, h // 2])[:, (h % 2) * GDV:(h % 2 + 1) * GDV] for j in range(NT) for h in range(GH)], NT * GH)
            act.wait_ge(S["cols_loaded"], 16)
            act.activation(cond, col("cond"), ACT.Silu).then_inc(S["cond_ready"], 1)
            act.wait_ge(S["x1_ready"], 4)
            norm_root(2, [x[:, j, :] for j in range(NT)], NT)

            def ff_taps(done, s, i):
                act.wait_ge(S["up_done"], done + 1)
                for g in range(2):
                    act.activation(conv[s][:, g, :], ps[:, 4 + s, g * T:(g + 1) * T], ACT.Identity,
                                   scale=cols[:, bass.ds(COLS["conv_w"][0] + 2 * 2 * FT + g * FT + i, 1)],
                                   bias=cols[:, bass.ds(COLS["conv_b"][0] + g * FT + i, 1)]).then_inc(S["conv_tap"], 1)
                act.wait_ge(S["conv_ready"], done + 1)
                act.activation(sig[s], conv[s][:, 0, :], ACT.Silu).then_inc(S["gate_sig"], 1)

            ff_taps(0, 0, 0)
            ff_taps(1, 1, 1)
            with act.Fori(1, FT // 2) as i:
                for s in range(2):
                    act.wait_ge(S["hm_ready"], i * 2 + s - 1)
                    ff_taps(i * 2 + s, s, i * 2 + s)
            act.wait_ge(S["x2_ready"], 1)
            norm_root(3, [x[:, j, :] for j in range(NT)], NT)
            act.wait_ge(S["mod_plus"], 2)
            for k in range(4):
                act.wait_ge(S["x_turned"], k // 2 + 1)
                act.activation(h1T[:, k, :], ps[:, 4 + k // 2, (k % 2) * T:(k % 2 + 1) * T], ACT.Identity, scale=mod[:, 8 + k:9 + k], bias=mod[:, k:k + 1]).then_inc(S["h1_ready"], 1)
            act.wait_ge(S["chunk_done"], C_CKV + 1)
            norm_root(4, [ps[:, 0, j * LAT:(j + 1) * LAT] for j in range(NT)], NT)
            act.wait_ge(S["chunk_done"], C_KW + 1)
            act.activation(kiT[IDH:P, :], ps[0:IDH, 1, 0:T], ACT.Copy).then_inc(S["kidx_ready"], 1)
            act.wait_ge(S["chunk_done"], C_QI + 1)
            act.activation(qiT.rearrange("p k t -> p (k t)"), bank(4, 2), ACT.Copy).then_inc(S["qidx_ready"], 1)
            for j in range(NT):
                act.wait_ge(S["rel_done"], j + 1)
                if j == 1:
                    act.wait_ge(S["rel_used"], 1)
                else:
                    act.wait_ge(S["ckv_ready"], 2)
                for b in range(4):
                    act.activation(relu[:, b, :], bank(4 + b), ACT.Relu).then_inc(S["rel_ready"], 1)
                act.wait_ge(S["chunk_done"], C_QA[j] + 1)
                act.activation(qaT[:, 4 * j:4 * j + 4, :].rearrange("p k t -> p (k t)"), bank(2, 2), ACT.Copy).then_inc(S["qatt_ready"], 1)
            act.wait_ge(S["chunk_done"], C_UK + 1)
            for i in range(2):
                act.activation(khT[:, 4 * i:4 * i + 4, :].rearrange("p k t -> p (k t)"), bank(2 * i, 2), ACT.Copy).then_inc(S["kh_ready"], 1)
            act.wait_ge(S["chunk_done"], C_UV + 1)
            for j in range(NT):
                act.activation(vh[:, j, :], bank(2 * j, 2), ACT.Copy).then_inc(S["vh_ready"], 2)
            for n in range(24):
                act.wait_ge(S["chunk_done"], C_QKVD[n // 4] + 1)
                b = 4 + (n // 4) % 2 * 2 + (n % 4) // 2
                act.activation(dnT[:, n, :], ps[:, b, (n % 2) * T:(n % 2 + 1) * T], ACT.Copy,
                               scale=col("dn_conv")[:, 3 * 24 + n:3 * 24 + n + 1]).then_inc(S["conv2_tap"], 1)
            for i in range(3):
                act.wait_ge(S["conv2_ready"], 8 * (i + 1))
                act.activation(dnT[:, 8 * i:8 * i + 8, :], dnT[:, 8 * i:8 * i + 8, :], ACT.Silu).then_inc(S["act_silu2"], 1)
            for n in range(4):
                j = n // 2
                act.wait_ge(S["att_max"], n + 1)
                for i in range(4):
                    w = P * (j + 1)
                    act.activation(prob[n % 2][:, i, 0:w], prob[n % 2][:, i, 0:w], ACT.Exp, scale=ATT_SCALE, bias=amax[:, 4 * n + i:4 * n + i + 1],
                                   accum_out=asum[:, 4 * n + i:4 * n + i + 1]).then_inc(S["att_exp"], 1)
                act.wait_ge(S["att_turned"], n + 1)
                if n >= 2:
                    act.wait_ge(S["att_pv"], n - 1)
                act.activation(probT[n % 2][:, :, 0:j + 1, :].rearrange("p h s q -> p h (s q)"),
                               bank(4, 2).rearrange("p (h c) -> p h c", h=4)[:, :, 0:P * (j + 1)], ACT.Copy).then_inc(S["att_probT"], 1)
            for i in range(2):
                act.wait_ge(S["chunk_done"], C_GA[i] + 1)
                act.activation(mixed[:, 4 * i:4 * i + 4, :].rearrange("p k t -> p (k t)"), bank(2 * i, 2), ACT.Sigmoid).then_inc(S["gate_a_ready"], 1)
            act.wait_ge(S["att_pv"], 4)
            act.wait_ge(S["eps_ready"], 1)
            act.activation(rq, qT, ACT.Square).then_inc(made("l2_sq"), 1)
            act.activation(rk, kT, ACT.Square).then_inc(made("l2_sq"), 1)
            act.wait_ge(S["chunk_done"], C_AB + 1)
            ab = ps[:, 0, 0:32].rearrange("p (j c) -> p j c", j=NT)
            act.activation(beta.rearrange("p (j c) -> p j c", j=NT), ab[:, :, 8:16], ACT.Sigmoid).then_inc(made("beta_ready"), 1)
            act.wait_ge(*after("ab_y", 1))
            act.activation(soft_g, g_in, ACT.Abs).then_inc(made("ab_abs"), 1)
            act.wait_ge(*after("ab_abs", 1))
            act.activation(soft_g, soft_g, ACT.Exp, scale=-1.0).then_inc(made("ab_abs"), 1)
            act.wait_ge(*after("ab_abs", 2))
            act.activation(soft_g, soft_g, ACT.Ln, bias=1.0).then_inc(made("ab_soft"), 1)
            act.wait_ge(S["rows_small_loaded"], 32)
            act.activation(ea_row, alog_row, ACT.Exp).then_inc(made("ea_ready"), 1)
            for i, (r, b0) in enumerate(((rq, 4), (rk, 0))):
                act.wait_ge(*after("l2_sum", i + 1))
                act.activation(r.rearrange("p k t -> p (k t)"), bank(b0, 4), ACT.Sqrt, bias=eps_col).then_inc(made("l2_root"), 1)
            act.wait_ge(*after("gcols_ready", 1))
            act.activation(eG, G_col, ACT.Exp).then_inc(made("G_exp"), 1)
            act.wait_ge(*after("tail_diff", 1))
            act.activation(tail, tail, ACT.Exp).then_inc(made("G_exp"), 1)
            act.wait_ge(*after("dec_ready", 1))
            act.activation(decay, decay, ACT.Exp).then_inc(made("dec_exp"), 1)
            act.activation(eGB.rearrange("p n c -> p (n c)"), bank(4, 4), ACT.Exp).then_inc(made("eGB_ready"), 1)
            for i in range(2):
                act.wait_ge(S["chunk_done"], C_Z[i] + 1)
                act.wait_ge(*after("qkT_ready", 1))
                for j in range(NT):
                    act.activation(z_rows[:, j, i * HALF:(i + 1) * HALF], bank(4 + i + 2 * j), ACT.Silu).then_inc(S["z_ready"], 1)
            act.wait_ge(*after("X_turned", 1))
            for g in range(4):
                act.activation(X[:, 4 * g:4 * g + 4, :].rearrange("p n c -> p (n c)"), bank(4 + g), ACT.Copy).then_inc(S["X_ready"], 1)
            for n in range(16):
                act.wait_ge(S["X_done"], n + 1)
                g = n % 4
                act.activation(X[:, 4 * g:4 * g + 4, :].rearrange("p n c -> p (n c)"), bank(4 + g), ACT.Copy).then_inc(S["X_ready"], 1)
            act.wait_ge(*after("w_done", 1))
            act.activation(nwT.rearrange("p n c -> p (n c)"), bank(4, 4), ACT.Copy, scale=-1.0).then_inc(S["nw_ready"], 1)
            for i, b0 in enumerate((0, 4)):
                act.wait_ge(S["chunk_done"], C_GD[i] + 1)
                act.activation(gate_d[:, 4 * i:4 * i + 4, :].rearrange("p k t -> p (k t)"), bank(b0, 2), ACT.Sigmoid).then_inc(S["gate_d_ready"], 1)
            act.wait_ge(S["dn_o"], 4)
            norm_root(5, [ps[:, (2 if j == 0 else 6) + h // 4, (h % 4) * P:(h % 4 + 1) * P] for j in range(NT) for h in range(NH)], NT * NH)
            act.wait_ge(S["gt_done"], 1)
            act.activation(gt_row, bank(2, 2), ACT.Copy).then_inc(S["gt_ready"], 1)
            act.wait_ge(S["ln_in"], 2)
            for j in range(NT):
                act.activation(lnt[:, j, :], x[:, j, :], ACT.Copy, accum_out=lsum[:, j:j + 1]).then_inc(S["ln_sum"], 1)
            act.wait_ge(S["ln_cent"], 2)
            norm_root(6, [x[:, j, :] for j in range(NT)], NT)
            act.wait_ge(S["x4_ready"], 2)
            for k in range(4):
                act.wait_ge(S["h2_turned"], k // 2 + 1)
                act.activation(h2T[:, k, :], ps[:, 4 + k // 2, (k % 2) * T:(k % 2 + 1) * T], ACT.Identity, scale=mod[:, 32 + k:33 + k],
                               bias=mod[:, 24 + k:25 + k]).then_inc(S["h2_ready"], 1)
            act.wait_ge(S["logits_ready"], 1)
            act.activation(grp[:, :, 4:8], grp[:, :, 0:4], ACT.Exp).then_inc(S["group_exp"], 1)
            act.wait_ge(S["ratio_in"], 1)
            act.activation(ratio, ratio, ACT.Exp).then_inc(S["ratio_exp"], 1)
            act.wait_ge(S["tables_ready"], 1)
            blocks = act.alloc_register("act_blocks")
            act.reg_mov(blocks, 0)

            def act_block():
                n = act.snap(blocks)
                act.wait_ge(S["gate_up_done"], n + 1)
                act.activation(gact, ps[0:2 * SLOTS, 5, 0:T], ACT.Silu).then_inc(S["gate_act"], 1)
                act.wait_ge(S["h_turned"], n + 1)
                act.activation(hidT.rearrange("p t s -> p (t s)"), ps[:, 4, 0:P], ACT.Copy).then_inc(S["hT_ready"], 1)
                act.wait_ge(S["selg_turned"], n + 1)
                act.activation(selgT, ps[:, 6, 0:T], ACT.Copy).then_inc(S["selgT_ready"], 1)
                act.reg_add(blocks, blocks, 1)

            with act.Fori(0, NE) as e:
                count = act.value_load(count_i[0:1, bass.ds(e, 1)], min_val=0, max_val=T)
                act_block()
                with act.If(count > SLOTS):
                    act_block()
                with act.If(count > 2 * SLOTS):
                    with act.Fori(2, T // SLOTS):
                        act_block()
            act.wait_ge(S["gt_done"], 2)
            act.activation(gt_row2, bank(4, 2), ACT.Copy).then_inc(S["gt_ready"], 1)
            act.wait_ge(S["ln_in"], 4)
            for j in range(NT):
                act.activation(lnt[:, j, :], x[:, j, :], ACT.Copy, accum_out=lsum[:, j:j + 1]).then_inc(S["ln_sum"], 1)
            act.wait_ge(S["ln_cent"], 4)
            norm_root(7, [x[:, j, :] for j in range(NT)], NT)

        @block.vector
        def _(dve):
            steps = [0]
            roots = [0]

            def step(ins):
                steps[0] += 1
                ins.then_inc(S["dve_step"], 1)
                dve.wait_ge(S["dve_step"], steps[0])

            def norm_scale(r, sums, n, width, eps=RMS_EPS):
                dve.wait_ge(S["square_summed"], sums)
                dve.tensor_scalar(rstd[:, 0:n], ss[:, 0:n], 1.0 / width, eps, ALU.mult, ALU.add).then_inc(S["norm_var"], 1)
                dve.wait_ge(S["root_taken"], r + 1)
                step(dve.reciprocal(rstd[:, 0:n], rstd[:, 0:n]))

            def scale_rows(dst):
                for j in range(NT):
                    dve.tensor_scalar(dst[:, j, :], x[:, j, :], rstd[:, j:j + 1], None, ALU.mult).then_inc(S["rows_scaled"], 1)

            def copy_turned(dst, banks, gain, turned, first, done):
                for j in range(NT):
                    for kk in range(2):
                        dve.wait_ge(S[turned], first + 2 * j + kk + 1)
                        dve.tensor_tensor(dst[:, 4 * kk:4 * kk + 4, j * P:(j + 1) * P],
                                          bank(banks[2 * j + kk]).rearrange("p (k t) -> p k t", k=4),
                                          gain[:, 4 * kk:4 * kk + 4].unsqueeze(2).broadcast_to([P, 4, P]), ALU.mult).then_inc(S[done] if done in S else made(done), 1)

            norm_scale(0, NT, NT, D)
            scale_rows(xn)
            dve.wait_ge(S["cols_loaded"], 16)
            copy_turned(hT, (0, 1, 2, 3), col("norm1"), "turned", 0, "turned_copied")
            dve.wait_ge(*after("alow_done", 1))
            dve.tensor_copy(alT, ps[0:GRANK, 4, 0:T]).then_inc(made("alow_copied"), 1)
            dve.wait_ge(*after("alpha_soft", 1))
            z = bank(5, 2).rearrange("p (j c) -> p j c", j=NT)
            dve.scalar_tensor_tensor(out=la, in0=z, scalar=0.0, in1=soft, op0=ALU.min, op1=ALU.subtract).then_inc(made("logs_ready"), 1)
            dve.wait_ge(*after("cum_ready", 1))
            by_chunk = cum.rearrange("p h (c t) -> p (h c) t", t=CH)
            dve.tensor_tensor(kx.rearrange("p h (c t) -> p (h c) t", t=CH), by_chunk[:, :, CH - 1:CH].broadcast_to([P, GH * NCH, CH]),
                              by_chunk, ALU.subtract).then_inc(made("end_diff"), 1)
            dve.wait_ge(*after("decays_ready", 2))
            dve.scalar_tensor_tensor(out=qd.rearrange("p h t -> p (h t)"), in0=bank(0, 2), scalar=GDK ** -0.5,
                                     in1=eb.rearrange("p h t -> p (h t)"), op0=ALU.mult, op1=ALU.mult).then_inc(made("q_ready"), 1)
            dve.tensor_tensor(kinv.rearrange("p h t -> p (h t)"), bank(2, 2), enb.rearrange("p h t -> p (h t)"), ALU.mult).then_inc(made("k_ready"), 1)
            dve.wait_ge(*after("end_decay", 1))
            dve.tensor_tensor(kend.rearrange("p h t -> p (h t)"), bank(2, 2), kx.rearrange("p h t -> p (h t)"), ALU.mult).then_inc(made("k_ready"), 1)
            for j in range(NT):
                dve.wait_ge(S["gscores_done"], j + 1)
                dve.tensor_tensor(sc_t[:, 4 * j:4 * j + 4, :], bank(j).rearrange("p (h t) -> p h t", h=4),
                                  const("upto").unsqueeze(1).broadcast_to([P, 4, P]), ALU.mult).then_inc(S["gscores_masked"], 1)
            dve.wait_ge(S["gla_upd"], 1)
            dve.tensor_copy(state.rearrange("p h c -> p (h c)"), bank(5, 2)).then_inc(S["gla_state"], 1)
            for c, banks in ((1, (0, 1)), (2, (5, 6))):
                dve.wait_ge(S["gla_upd"], c + 1)
                dve.wait_ge(S["gla_inter"], c)
                dve.wait_ge(S["gla_state"], c)
                for h in range(GH):
                    at = c * CH + CH - 1
                    m = dve.scalar_tensor_tensor(out=state[:, h, :], in0=state[:, h, :], scalar=eb[:, h, at:at + 1],
                                                 in1=bank(banks[h // 2])[:, (h % 2) * GDV:(h % 2 + 1) * GDV], op0=ALU.mult, op1=ALU.add)
                m.then_inc(S["gla_state"], 1)
            norm_scale(1, NT + NT * GH, NT * GH, GDV)
            o_banks = {(0, 0): 2, (0, 1): 3, (1, 0): 4, (1, 1): 7}
            for j in range(NT):
                for h in range(GH):
                    g = slice(h * GDV, (h + 1) * GDV)
                    m = dve.scalar_tensor_tensor(out=y_rows[:, j, g], in0=bank(o_banks[j, h // 2])[:, (h % 2) * GDV:(h % 2 + 1) * GDV],
                                                 scalar=rstd[:, 4 * j + h:4 * j + h + 1], in1=r_rows[:, j, g], op0=ALU.mult, op1=ALU.mult)
                m.then_inc(S["y_ready"], 1)
            copy_turned(yT, (0, 1, 5, 6), col("out_norm"), "y_turned", 0, "yT_ready")
            for half, banks in ((0, (2, 4)), (1, (3, 7))):
                dve.wait_ge(S["chunk_done"], 7 + half)
                for j in range(NT):
                    c = slice(half * HALF, (half + 1) * HALF)
                    dve.tensor_tensor(x[:, j, c], x[:, j, c], bank(banks[j]), ALU.add).then_inc(S["x1_ready"], 1)
            dve.wait_ge(S["x1_ready"], 4)
            norm_scale(2, NT + NT * GH + NT, NT, D)
            scale_rows(xn)
            copy_turned(hT, (4, 5, 6, 7), col("norm2"), "turned", 4, "turned_copied")

            def ff_conv(done, s, i, taps):
                dve.wait_ge(S["conv_tap"], taps)
                for tap, gap in ((1, 1), (0, 2)):
                    for g in range(2):
                        m = dve.scalar_tensor_tensor(out=conv[s][:, g, gap:], in0=ps[:, 4 + s, g * T:(g + 1) * T - gap],
                                                     scalar=cols[:, bass.ds(COLS["conv_w"][0] + tap * 2 * FT + g * FT + i, 1)],
                                                     in1=conv[s][:, g, gap:], op0=ALU.mult, op1=ALU.add)
                        if tap == 1:
                            m.then_inc(S["conv_part"], 1)
                            if g == 1:
                                dve.wait_ge(S["conv_part"], taps)
                m.then_inc(S["conv_ready"], 1)

            def ff_mul(done, s, free):
                dve.wait_ge(S["gate_sig"], done + 1)
                if free is not None:
                    dve.wait_ge(S["down_done"], free)
                dve.tensor_tensor(hm[s], sig[s], conv[s][:, 1, :], ALU.mult).then_inc(S["hm_ready"], 1)

            def modulation(i, done):
                dve.wait_ge(S["ada_done"], done)
                dve.tensor_tensor(mod[:, bass.ds(i * 4, 4)], ps[:, 6, 0:4], cols[:, bass.ds(COLS["b_ada"][0] + i * 4, 4)], ALU.add).then_inc(S["mod_ready"], 1)

            for i in range(2):
                ff_conv(i, i, i, 2 * i + 2)
                ff_mul(i, i, None)
            modulation(0, 1)
            with dve.Fori(1, FT // 2) as i:
                for s in range(2):
                    ff_conv(i * 2 + s, s, i * 2 + s, i * 4 + 2 * s + 2)
                    ff_mul(i * 2 + s, s, i * 2 + s - 1)
                modulation(i, i + 1)
            modulation(11, 12)
            dve.wait_ge(S["down_done"], FT)
            dve.tensor_copy(unit(0), bank(0, 4)).then_inc(S["x2_ready"], 1)
            dve.wait_ge(S["x2_ready"], 1)
            norm_scale(3, 2 * NT + NT * GH + NT, NT, D)
            dve.wait_ge(S["fnorm_loaded"], 16)
            for j in range(NT):
                dve.scalar_tensor_tensor(out=x[:, j, :], in0=x[:, j, :], scalar=rstd[:, j:j + 1], in1=fnorm,
                                         op0=ALU.mult, op1=ALU.mult).then_inc(S["x3_ready"], 1)
            dve.wait_ge(S["mod_ready"], 12)
            dve.tensor_scalar(mod[:, 8:24], mod[:, 8:24], 1.0, None, ALU.add).then_inc(S["mod_plus"], 1)
            dve.tensor_scalar(mod[:, 32:48], mod[:, 32:48], 1.0, None, ALU.add).then_inc(S["mod_plus"], 1)
            dve.wait_ge(S["mod_plus"], 2)
            for k in range(4, KD):
                dve.wait_ge(S["x_turned"], k // 2 + 1)
                dve.tensor_scalar(h1T[:, k, :], ps[:, 4 + k // 2, (k % 2) * T:(k % 2 + 1) * T], mod[:, 8 + k:9 + k], mod[:, k:k + 1], ALU.mult, ALU.add).then_inc(S["h1_ready"], 1)
            step(dve.tensor_scalar(causneg.rearrange("p j s -> p (j s)"), consts[:, CONSTS["causal0"][0]:CONSTS["causal0"][0] + 2 * T],
                                   -NEG, NEG, ALU.mult, ALU.add))
            norm_scale(4, 4 * NT + NT * GH, NT, LAT)
            for j in range(NT):
                dve.tensor_scalar(ckv[:, j, :], ps[:, 0, j * LAT:(j + 1) * LAT], rstd[:, j:j + 1], None, ALU.mult).then_inc(S["ckv_ready"], 1)
            dve.wait_ge(S["chunk_done"], C_KW + 1)
            dve.tensor_scalar(widx, ps[:, 2, 0:2 * IH], INDEX_SCALE, None, ALU.mult).then_inc(S["widx_ready"], 1)
            dve.wait_ge(S["kidx_ready"], 1)
            dve.tensor_copy(kiT[0:IDH, :], ps[0:IDH, 1, 0:T]).then_inc(S["kidx_ready"], 1)
            dve.wait_ge(S["widx_ready"], 1)
            for j in range(NT):
                if j == 1:
                    dve.wait_ge(S["ckv_turned"], 1)
                    dve.tensor_tensor(ckvT, bank(0).rearrange("p (c t) -> p c t", c=2), col("kv_g").unsqueeze(2).broadcast_to([P, 2, T]),
                                      ALU.mult).then_inc(S["ckvT_ready"], 1)
                for b in range(4):
                    dve.wait_ge(S["rel_ready"], 4 * j + b + 1)
                    for c in range(2):
                        h = b // 2 + 2 * (2 * (b % 2) + c)
                        w = widx[:, j * IH + h:j * IH + h + 1]
                        if b == 0 and c == 0:
                            step(dve.tensor_scalar(score[:, j, :], relu[:, b, 0:T], w, None, ALU.mult))
                        else:
                            m = dve.scalar_tensor_tensor(out=score[:, j, :], in0=relu[:, b, c * T:(c + 1) * T], scalar=w, in1=score[:, j, :],
                                                         op0=ALU.mult, op1=ALU.add)
                            step(m)
                causal = const(f"causal{j}")
                dve.tensor_tensor(score[:, j, :], score[:, j, :], causal, ALU.mult).then_inc(S["rel_used"], 1)
                dve.wait_ge(S["rel_used"], j + 1)
                step(dve.tensor_tensor(score[:, j, :], score[:, j, :], causneg[:, j, :], ALU.add))
                for _ in range(TOPK // 8):
                    step(dve.max(best, score[:, j, :]))
                    step(dve.match_replace(score[:, j, :], best, score[:, j, :], TAKEN))
                step(dve.tensor_scalar(keep[:, j, :], score[:, j, :], (NEG + TAKEN) / 2, None, ALU.is_lt))
                step(dve.tensor_tensor(keep[:, j, :], keep[:, j, :], causal, ALU.mult))
                step(dve.tensor_scalar(keep[:, j, :], keep[:, j, :], -NEG, NEG, ALU.mult, ALU.add))
            for n in range(24):
                dve.wait_ge(S["conv2_tap"], n // 2 * 2 + 2)
                b = 4 + (n // 4) % 2 * 2 + (n % 4) // 2
                for tap in (2, 1, 0):
                    gap = 3 - tap
                    m = dve.scalar_tensor_tensor(out=dnT[:, n, gap:], in0=ps[:, b, (n % 2) * T:(n % 2 + 1) * T - gap],
                                                 scalar=col("dn_conv")[:, tap * 24 + n:tap * 24 + n + 1], in1=dnT[:, n, gap:], op0=ALU.mult, op1=ALU.add)
                    if tap:
                        step(m)
                m.then_inc(S["conv2_ready"], 1)
            for n in range(4):
                j, w = n // 2, P * (n // 2 + 1)
                dve.wait_ge(S["att_scores"], n + 1)
                if n >= 2:
                    dve.wait_ge(S["att_turned"], n - 1)
                dve.tensor_tensor(prob[n % 2][:, :, 0:w], bank(0, 2).rearrange("p (h s) -> p h s", h=4)[:, :, 0:w],
                                  keep[:, j, 0:w].unsqueeze(1).broadcast_to([P, 4, w]), ALU.add).then_inc(S["att_masked"], 1)
                dve.wait_ge(S["att_masked"], n + 1)
                step(dve.reduce_max(amax[:, 4 * n:4 * n + 4], prob[n % 2][:, :, 0:w], AX_X))
                dve.tensor_scalar(amax[:, 4 * n:4 * n + 4], amax[:, 4 * n:4 * n + 4], -ATT_SCALE, None, ALU.mult).then_inc(S["att_max"], 1)
                dve.wait_ge(S["att_exp"], 4 * n + 4)
                step(dve.reciprocal(asum[:, 4 * n:4 * n + 4], asum[:, 4 * n:4 * n + 4]))
                for i in range(4):
                    m = dve.tensor_scalar(prob[n % 2][:, i, 0:w], prob[n % 2][:, i, 0:w], asum[:, 4 * n + i:4 * n + i + 1], None, ALU.mult)
                m.then_inc(S["att_prob"], 1)
                dve.wait_ge(S["att_pv"], n + 1)
                dve.tensor_copy(yaT[:, 4 * (n % 2):4 * (n % 2) + 4, j * P:(j + 1) * P], bank(2 + n % 2).rearrange("p (h q) -> p h q", h=4)).then_inc(S["ya_ready"], 1)
            for i in range(2):
                dve.wait_ge(S["chunk_done"], C_BRA[i] + 1)
                dve.wait_ge(S["gate_a_ready"], i + 1)
                m4 = mixed[:, 4 * i:4 * i + 4, :].rearrange("p k t -> p (k t)")
                dve.tensor_tensor(m4, m4, bank(4 + 2 * i, 2), ALU.mult).then_inc(S["mixed_a_ready"], 1)
            dve.wait_ge(*after("beta_ready", 1))
            dve.wait_ge(S["rows_small_loaded"], 32)
            ab = ps[:, 0, 0:32].rearrange("p (j c) -> p j c", j=NT)
            per_head = lambda row: row.unsqueeze(1).broadcast_to([P, NT, NH])
            gj = g_in.rearrange("p (j c) -> p j c", j=NT)
            dve.tensor_tensor(gj, ab[:, :, 0:8], per_head(dt_row), ALU.add).then_inc(made("ab_y"), 1)
            dve.wait_ge(*after("ab_y", 1))
            dve.wait_ge(*after("ab_soft", 1))
            dve.wait_ge(*after("ea_ready", 1))
            step(dve.scalar_tensor_tensor(out=g_in, in0=g_in, scalar=0.0, in1=soft_g, op0=ALU.max, op1=ALU.add))
            dve.scalar_tensor_tensor(out=gj, in0=gj, scalar=-1.0, in1=per_head(ea_row), op0=ALU.mult, op1=ALU.mult).then_inc(made("g_ready"), 1)
            for i, (r, t, s) in enumerate(((rq, qT, NDK ** -0.5), (rk, kT, 1.0))):
                dve.wait_ge(*after("l2_root", i + 1))
                step(dve.reciprocal(r, r))
                dve.scalar_tensor_tensor(out=t, in0=t, scalar=s, in1=r, op0=ALU.mult, op1=ALU.mult).then_inc(made("qk_norm"), 1)
            dve.wait_ge(*after("gcols_done", 1))
            dve.tensor_copy(small[:, 208:240], ps[:, 0, 0:32]).then_inc(made("gcols_ready"), 1)
            dve.wait_ge(*after("gcols_ready", 1))
            dve.tensor_tensor(tail, G_end, G_col, ALU.subtract).then_inc(made("tail_diff"), 1)
            dve.wait_ge(*after("GB_done", 1))
            for n in range(16):
                h, j = n // 2, n % 2
                m = dve.tensor_scalar(decay[:, n, :], ps[:, 4 + n // 4, (n % 4) * P:(n % 4 + 1) * P], G_col[:, j * 8 + h:j * 8 + h + 1], 0.0,
                                      ALU.subtract, ALU.min)
            m.then_inc(made("dec_ready"), 1)
            dve.wait_ge(*after("G_exp", 2))
            step(dve.tensor_tensor(beG, beta, eG, ALU.mult))
            dve.wait_ge(*after("dec_exp", 1))

            def all16(c):
                return c.unsqueeze(1).broadcast_to([P, 16, P])

            step(dve.tensor_tensor(decay, decay, all16(const("upto")), ALU.mult))
            dve.wait_ge(*after("bB_done", 1))
            dve.tensor_tensor(decay_beta.rearrange("p n c -> p (n c)"), bank(0, 4), decay.rearrange("p n c -> p (n c)"), ALU.mult).then_inc(made("dbeta_ready"), 1)
            dve.wait_ge(*after("kk_done", 1))
            dve.wait_ge(*after("dbeta_ready", 1))
            dve.tensor_tensor(AT.rearrange("p n c -> p (n c)"), bank(4, 4), decay_beta.rearrange("p n c -> p (n c)"), ALU.mult).then_inc(made("AT_ready"), 1)
            dve.wait_ge(*after("kq_done", 1))
            dve.tensor_tensor(qkT.rearrange("p n c -> p (n c)"), bank(0, 4), decay.rearrange("p n c -> p (n c)"), ALU.mult).then_inc(made("qkT_ready"), 1)

            def rows_times(dst, b0, scal, done):
                for j in range(NT):
                    m = dve.tensor_tensor(dst[:, j, :].rearrange("p (h c) -> p h c", h=NH), bank(b0 + 2 * j, 2).rearrange("p (h c) -> p h c", h=NH),
                                          scal[:, j * 8:(j + 1) * 8].unsqueeze(2).broadcast_to([P, NH, P]), ALU.mult)
                m.then_inc(S[done] if done in S else made(done), 1)

            dve.wait_ge(*after("k_turned", 1))
            rows_times(kbG, 4, beG, "k_rows_ready")
            rows_times(ktail, 4, tail, "k_rows_ready")
            dve.wait_ge(*after("v_turned", 1))
            rows_times(vbeta, 0, beta, "v_rows_ready")
            dve.wait_ge(S["level_masked"], 1)
            dve.scalar_tensor_tensor(out=XT, in0=AT_level[0], scalar=-1.0, in1=all16(ident), op0=ALU.mult, op1=ALU.add).then_inc(S["XT_ready"], 1)
            for level in range(1, 6):
                for g in range(4):
                    n = 4 * (level - 1) + g + 1
                    dve.wait_ge(S["T1_done"], n)
                    dve.scalar_tensor_tensor(out=N1[:, 4 * g:4 * g + 4, :], in0=bank(g).rearrange("p (n c) -> p n c", n=4), scalar=-1.0,
                                             in1=ident.unsqueeze(1).broadcast_to([P, 4, P]), op0=ALU.mult, op1=ALU.add).then_inc(S["N1_ready"], 1)
                for g in range(4):
                    n = 4 * (level - 1) + g + 1
                    dve.wait_ge(S["XT_done"], n)
                    dve.tensor_copy(XT[:, 4 * g:4 * g + 4, :].rearrange("p n c -> p (n c)"), bank(g)).then_inc(S["XT_ready"], 1)
            for j in range(NT):
                for half in range(2):
                    c, r = 2 * j + half, half * CH
                    if half == 0:
                        dve.wait_ge(S["u_done"], j + 1)
                    if c > 0:
                        dve.wait_ge(S["ws_done"], c)
                    dve.tensor_copy(vnew[r:r + CH].rearrange("p h c -> p (h c)"), ps[r:r + CH, 0:2, :].rearrange("p b c -> p (b c)")).then_inc(S["vnew_ready"], 1)
                    if c == NCH - 1:
                        break
                    dve.wait_ge(S["dn_upd"], c + 1)
                    if c == 0:
                        dve.tensor_copy(dstate.rearrange("p h c -> p (h c)"), bank(4, 2)).then_inc(S["dstate_ready"], 1)
                    else:
                        dve.wait_ge(S["dn_inter"], c)
                        dve.wait_ge(S["dstate_ready"], c)
                        for h in range(NH):
                            m = dve.scalar_tensor_tensor(out=dstate[:, h, :], in0=dstate[:, h, :],
                                                         scalar=eGB[:, 2 * h + j, r + CH - 1:r + CH], in1=ps[:, 4 + h // 4, (h % 4) * P:(h % 4 + 1) * P],
                                                         op0=ALU.mult, op1=ALU.add)
                        m.then_inc(S["dstate_ready"], 1)
            norm_scale(5, 4 * NT + NT * GH + NT * NH, NT * NH, P)
            for j in range(NT):
                for h in range(NH):
                    hs = slice(h * P, (h + 1) * P)
                    m = dve.scalar_tensor_tensor(out=yd_rows[:, j, hs], in0=ps[:, (2 if j == 0 else 6) + h // 4, (h % 4) * P:(h % 4 + 1) * P],
                                                 scalar=rstd[:, 8 * j + h:8 * j + h + 1], in1=z_rows[:, j, hs], op0=ALU.mult, op1=ALU.mult)
                m.then_inc(S["yd_ready"], 1)
            copy_turned(ydT, (0, 1, 4, 5), col("dn_g").broadcast_to([P, 8]), "yd_turned", 0, "ydT_ready")
            for i, b0 in enumerate((2, 6)):
                dve.wait_ge(S["chunk_done"], C_BRD[i] + 1)
                dve.wait_ge(S["gate_d_ready"], 2)
                part = slice(4 * i, 4 * i + 4)
                flat = "p k t -> p (k t)"
                step(dve.tensor_tensor(gate_d[:, part, :].rearrange(flat), bank(b0, 2), gate_d[:, part, :].rearrange(flat), ALU.mult))
                dve.tensor_tensor(mixed[:, part, :].rearrange(flat), mixed[:, part, :].rearrange(flat), gate_d[:, part, :].rearrange(flat),
                                  ALU.add).then_inc(S["mixed_ready"], 1)

            def layer_norm(n, banks, waits, gate, sums):
                for j in range(NT):
                    for half in range(2):
                        dve.wait_ge(*waits[half])
                        c = slice(half * HALF, (half + 1) * HALF)
                        step(dve.tensor_tensor(lnt[:, j, c], bank(banks[j, half]), gate[:, c], ALU.mult))
                    dve.scalar_tensor_tensor(out=x[:, j, :], in0=x[:, j, :], scalar=ALPHA, in1=lnt[:, j, :], op0=ALU.mult, op1=ALU.add).then_inc(S["ln_in"], 1)
                dve.wait_ge(S["ln_sum"], NT * (n + 1))
                step(dve.tensor_scalar(lsum, lsum, -1.0 / D, None, ALU.mult))
                for j in range(NT):
                    dve.tensor_scalar(x[:, j, :], x[:, j, :], lsum[:, j:j + 1], None, ALU.add).then_inc(S["ln_cent"], 1)
                norm_scale(6 + n, sums, NT, D, LN_EPS)

            dve.wait_ge(S["gt_ready"], 1)
            SUMS5 = 4 * NT + NT * GH + NT * NH
            layer_norm(0, {(0, 0): 0, (1, 0): 4, (0, 1): 1, (1, 1): 5},
                       [(S["chunk_done"], C_WO[0] + 1), (S["chunk_done"], C_WO[1] + 1)], gt_row, SUMS5 + NT)
            dve.wait_ge(S["ln_gb_loaded"], 32)
            for j in range(NT):
                step(dve.scalar_tensor_tensor(out=x[:, j, :], in0=x[:, j, :], scalar=rstd[:, j:j + 1], in1=ln_g, op0=ALU.mult, op1=ALU.mult))
                dve.tensor_tensor(x[:, j, :], x[:, j, :], ln_b, ALU.add).then_inc(S["x4_ready"], 1)
            for k in range(4, KD):
                dve.wait_ge(S["h2_turned"], k // 2 + 1)
                dve.tensor_scalar(h2T[:, k, :], ps[:, 4 + k // 2, (k % 2) * T:(k % 2 + 1) * T], mod[:, 32 + k:33 + k], mod[:, 24 + k:25 + k],
                                  ALU.mult, ALU.add).then_inc(S["h2_ready"], 1)
            dve.memset(zero_row, 0.0).then_inc(S["zero_ready"], 1)

            def wide8(c, n=8):
                return c.unsqueeze(2).broadcast_to([P, NT, n])

            def earliest_max(values, n, top, onehot):
                step(dve.reduce_max(top, values, AX_X))
                step(dve.tensor_tensor(cand[:, :, 0:n], values, wide8(top, n), ALU.is_equal))
                step(dve.tensor_tensor(cand[:, :, 0:n], cand[:, :, 0:n], const("first")[:, 0:n].unsqueeze(1).broadcast_to([P, NT, n]), ALU.mult))
                step(dve.reduce_max(first, cand[:, :, 0:n], AX_X))
                step(dve.tensor_tensor(onehot, cand[:, :, 0:n], wide8(first, n), ALU.is_equal))

            dve.wait_ge(S["logits_done"], 1)
            step(dve.tensor_copy(logits.rearrange("p j c -> p (j c)"), ps[:, 4, 0:72]))
            earliest_max(logits[:, :, 0:NG], NG, gmax, pickg[:, :, 0:NG])
            dve.tensor_tensor(grp[:, :, 0:NG], logits[:, :, 0:NG], wide8(gmax, NG), ALU.subtract).then_inc(S["logits_ready"], 1)
            for j in range(NT):
                step(dve.tensor_tensor(spread[:, j], logits[:, j, NG:].rearrange("p (g i) -> p g i", g=NG),
                                       pickg[:, j, 0:NG].unsqueeze(2).broadcast_to([P, NG, EPG]), ALU.mult))
                step(dve.reduce_sum(ing[:, j, :], spread[:, j].rearrange("p g i -> p i g"), AX_X))
            earliest_max(ing, EPG, top1, pick1)
            step(dve.scalar_tensor_tensor(out=ing2, in0=pick1, scalar=NEG, in1=ing, op0=ALU.mult, op1=ALU.add))
            earliest_max(ing2, EPG, top2, pick2)
            dve.tensor_tensor(ratio, top2, top1, ALU.subtract).then_inc(S["ratio_in"], 1)
            dve.wait_ge(S["group_exp"], 1)
            step(dve.reduce_sum(gsum, grp[:, :, 4:8], AX_X))
            dve.wait_ge(S["ratio_exp"], 1)
            step(dve.scalar_tensor_tensor(out=gat1, in0=ratio, scalar=1.0, in1=gsum, op0=ALU.add, op1=ALU.mult))
            step(dve.reciprocal(gat1, gat1))
            step(dve.tensor_tensor(gat2, gat1, ratio, ALU.mult))
            step(dve.tensor_tensor(gate8, pick1, wide8(gat1), ALU.mult))
            step(dve.tensor_tensor(cand, pick2, wide8(gat2), ALU.mult))
            step(dve.tensor_tensor(gate8, gate8, cand, ALU.add))
            step(dve.tensor_tensor(both8, pick1, pick2, ALU.add))
            for src, dst in ((both8, chosen), (gate8, gates_e)):
                for j in range(NT):
                    m = dve.tensor_tensor(dst[:, j * NE:(j + 1) * NE].rearrange("p (g i) -> p g i", g=NG), src[:, j].unsqueeze(1).broadcast_to([P, NG, EPG]),
                                          pickg[:, j, 0:NG].unsqueeze(2).broadcast_to([P, NG, EPG]), ALU.mult)
                    if dst is chosen and j == 1:
                        m.then_inc(S["chosen_ready"], 1)
                    else:
                        step(m)
            dve.wait_ge(S["ranks_done"], 1)
            dve.wait_ge(S["chosen_ready"], 1)
            step(dve.scalar_tensor_tensor(out=rank, in0=ps[:, 5, 0:2 * NE], scalar=1.0, in1=chosen, op0=ALU.add, op1=ALU.mult))
            step(dve.tensor_scalar(rank, rank, -1.0, None, ALU.add))
            dve.tensor_copy(count_i, ps[:, 5, 2 * NE:3 * NE]).then_inc(S["tables_ready"], 1)
            dve.wait_ge(S["tables_ready"], 1)
            blocks = dve.alloc_register("dve_blocks")
            dve.reg_mov(blocks, 0)

            def dve_block(e, b):
                n = dve.snap(blocks)
                slots = consts[:, bass.ds(CONSTS["slot"][0] + b * SLOTS, SLOTS)]
                for j in range(NT):
                    r, g = (t[:, bass.ds(j * NE + e, 1)] for t in (rank, gates_e))
                    dve.tensor_scalar(sel[:, j, :], slots, r, None, ALU.is_equal)
                    m = dve.tensor_scalar(selg[:, j], slots.unsqueeze(1).broadcast_to([P, 4, SLOTS]), r, g, ALU.is_equal, ALU.mult)
                m.then_inc(S["sel_ready"], 1)
                dve.wait_ge(S["xs_done"], n + 1)
                xs = ps[:, 4, 0:KD * SLOTS].rearrange("p (k s) -> p k s", k=KD)
                wide_k = lambda c: c.unsqueeze(2).broadcast_to([P, KD, SLOTS])
                dve.tensor_tensor(xsel, xs, wide_k(mod[:, 32:40]), ALU.mult).then_inc(S["xs_scaled"], 1)
                dve.wait_ge(S["xs_scaled"], n + 1)
                dve.tensor_tensor(xsel, xsel, wide_k(mod[:, 24:32]), ALU.add).then_inc(S["xs_ready"], 1)
                dve.wait_ge(S["gate_act"], n + 1)
                dve.tensor_tensor(hrows, gact, ps[2 * SLOTS:P, 5, 0:T], ALU.mult).then_inc(S["h_ready"], 1)
                dve.wait_ge(S["down2_done"], n + 1)
                dve.tensor_copy(yexp, ps[:, 7, 0:T]).then_inc(S["yexp_ready"], 1)
                dve.reg_add(blocks, blocks, 1)

            with dve.Fori(0, NE) as e:
                count = dve.value_load(count_i[0:1, bass.ds(e, 1)], min_val=0, max_val=T)
                dve_block(e, 0)
                with dve.If(count > SLOTS):
                    dve_block(e, 1)
                with dve.If(count > 2 * SLOTS):
                    with dve.Fori(2, T // SLOTS) as b:
                        dve_block(e, b)
            dve.wait_ge(S["gt_ready"], 2)
            dve.wait_ge(S["experts_summed"], 1)
            layer_norm(1, {(0, 0): 0, (0, 1): 1, (1, 0): 2, (1, 1): 3}, [(S["gt_ready"], 2), (S["gt_ready"], 2)], gt_row2, SUMS5 + 2 * NT)
            dve.wait_ge(S["ln_gb2_loaded"], 32)
            for j in range(NT):
                step(dve.scalar_tensor_tensor(out=x[:, j, :], in0=x[:, j, :], scalar=rstd[:, j:j + 1], in1=ln_g2, op0=ALU.mult, op1=ALU.mult))
                dve.tensor_tensor(x[:, j, :], x[:, j, :], ln_b2, ALU.add).then_inc(S["x5_ready"], 1)

        @block.gpsimd
        def _(pool):
            pool.memset(eps_col, 1e-6).then_inc(S["eps_ready"], 1)
            pool.wait_ge(S["consts_loaded"], 16)
            pool.wait_ge(*after("AT_ready", 1))
            for level in range(6):
                if level == 0:
                    pool.wait_ge(*after("qk_norm", 2))
                if level == 2:
                    pool.wait_ge(S["XT_ready"], 1)
                if level >= 3:
                    pool.wait_ge(S["T1_done"], 4 * (level - 2))
                up = const(f"up{level}").unsqueeze(1).broadcast_to([P, 16, P])
                pool.tensor_tensor(AT_level[level % 2], AT, up, ALU.mult).then_inc(S["level_masked"], 1)
            pool.wait_ge(*after("qkT_ready", 1))
            pool.wait_ge(*after("eGB_ready", 1))
            pool.tensor_tensor(probs(10), probs(10), eGB, ALU.mult).then_inc(S["qd2_ready"], 1)


INPUTS = [
    "x", "l0_gla_w_in", "l0_gla_w_alpha_up", "l0_gla_b_alpha", "l0_gla_w_out", "l0_ffn_w_up", "l0_ffn_w_down", "final_norm",
    "w_ada_2", "w_in_2", "w_uk_2", "w_uv_2", "a_log_2", "dt_bias_2", "w_br_att_2", "w_br_dn_2", "w_out_2",
    "w_route_grp_2", "w_route_exp_2", "w_gate_2", "w_up_2", "w_down_2", "ln_g_2", "ln_b_2",
]


def to_cols(a):
    a = np.asarray(a).reshape(-1, P)
    return a.T


def lay_out(inputs):
    arrays = {n: np.ascontiguousarray(inputs[n]) for n in INPUTS}
    parts = {
        "norm1": inputs["l0_norm1"], "out_norm": inputs["l0_gla_out_norm"], "norm2": inputs["l0_norm2"],
        "conv_w": inputs["l0_ffn_conv_w"], "conv_b": inputs["l0_ffn_conv_b"], "cond": inputs["c_2"],
        "b_ada": inputs["b_ada_2"], "kv_g": inputs["kv_norm_g_2"], "dn_conv": inputs["conv_w_2"], "dn_g": inputs["dn_norm_g_2"],
    }
    arrays["cols"] = np.ascontiguousarray(np.concatenate([to_cols(parts[n]) for n in COLS], axis=1))
    arrays["consts"] = CONST_TABLE
    return arrays


def kernel(**inputs):
    import concourse.bacc as bacc
    from concourse.bass_utils import run_bass_kernel_spmd

    nc = bacc.Bacc("TRN2", target_bir_lowering=False, num_devices=1)
    arrays = lay_out(inputs)
    I = {n: nc.dram_tensor(f"in_{n}", a.shape, F32, kind="ExternalInput").ap() for n, a in arrays.items()}
    out = nc.dram_tensor("out", (1, T, D), F32, kind="ExternalOutput").ap()
    build_program(nc, I, out)
    r = run_bass_kernel_spmd(nc, [{f"in_{n}": a for n, a in arrays.items()}], core_ids=[0])
    return r.results[0]["out"]
```

```python
from contextlib import ExitStack

import numpy as np

import concourse.bass as bass
from concourse import mybir

F32 = mybir.dt.float32
I32 = mybir.dt.int32
ALU = mybir.AluOpType
ACT = mybir.ActivationFunctionType
AX_X = mybir.AxisListType.X

P = 128
T = 256
NT = T // P
D = 1024
KD = D // P
HALF = 512
CH = 64
NCH = T // CH

GH, GDK, GDV = 4, 128, 256
GRANK = 16
GTAU = 16.0
FF = 2816
FT = FF // P
RMS_EPS = 1e-6
LN_EPS = 1e-5

AH, ADH = 8, 128
LAT = 256
IH, IDH = 8, 64
TOPK = 64
ATT_SCALE = ADH ** -0.5
INDEX_SCALE = (IH ** -0.5) * (IDH ** -0.5)
NH, NDK = 8, 128
NE, NG, EPG, EF = 32, 4, 8, 512
NSLOT = 3
SLOTS = 32
LAST = NE - NE % NSLOT
ALPHA = 2.0 ** 0.25
NEG = -3.0e38
TAKEN = -3.3e38

AT_Q, AT_CKV, AT_QI = 0, 1024, 1280
AT_KW, AT_QKVD, AT_AB, AT_Z = 1792, 1864, 4936, 4952
AT_GA, AT_GD = 5976, 7000

CONSTS = {}


def constant_table():
    p = np.arange(P)[:, None]
    c = np.arange(P)[None, :]
    same = (p // CH) == (c // CH)
    parts = [
        ("ident", p == c),
        ("ones", np.ones((P, P))),
        ("upto", same & (p <= c)),
        ("before", same & (p < c)),
        ("chunk", same),
        ("earlier", p < c),
    ]
    for level in range(6):
        b = 1 << level
        pair = (p // (2 * b)) == (c // (2 * b))
        parts.append((f"up{level}", pair & ((p // b) % 2 == 0) & ((c // b) % 2 == 1)))
    for level in range(1, 5):
        b = 1 << level
        pair = (p // (2 * b)) == (c // (2 * b))
        parts.append((f"low{level}", pair & ((p // b) % 2 == 1) & ((c // b) % 2 == 0)))
    c2 = np.arange(T)[None, :]
    parts.append(("causal0", c2 <= p))
    parts.append(("causal1", c2 <= p + P))
    parts.append(("slot", np.broadcast_to(np.arange(T)[None, :], (P, T))))
    parts.append(("first", np.broadcast_to(np.arange(8, 0, -1)[None, :], (P, 8))))
    at = 0
    for name, part in parts:
        CONSTS[name] = (at, part.shape[1])
        at += part.shape[1]
    return np.ascontiguousarray(np.concatenate([x[1].astype(np.float32) for x in parts], axis=1))


CONST_TABLE = constant_table()
NCONST = CONST_TABLE.shape[1]

COLS = {}
for _name, _n in (("norm1", 8), ("out_norm", 8), ("norm2", 8), ("conv_w", 3 * 2 * FT), ("conv_b", 2 * FT),
                  ("cond", 8), ("b_ada", 48), ("kv_g", 2), ("dn_conv", 4 * 24), ("dn_g", 1)):
    COLS[_name] = (sum(n for _, n in COLS.values()), _n)
NCOLS = sum(n for _, n in COLS.values())



def build_program(nc, I, out):
    ctx = ExitStack()
    with ctx:
        def sb(name, shape):
            return ctx.enter_context(nc.sbuf_tensor(name, shape, F32))

        S = {}

        def sem(*names):
            for n in names:
                S[n] = ctx.enter_context(nc.semaphore(n))

        U = 2048
        main = sb("main", [P, 24 * U])
        consts = sb("consts", [P, NCONST])
        cols = sb("cols", [P, NCOLS])
        small = sb("small", [P, 384])
        ps = ctx.enter_context(nc.psum_tensor("ps", [P, 8, HALF], F32))

        def unit(i, a=0, b=U):
            return main[:, i * U + a:i * U + b]

        def rows2(i):
            return unit(i).rearrange("p (j d) -> p j d", j=NT)

        def cols8(i):
            return unit(i).rearrange("p (k t) -> p k t", t=T)

        def tiles4(i, half):
            return unit(i, half * 1024, half * 1024 + 1024).rearrange("p (k t) -> p k t", t=T)

        def const(name):
            a, n = CONSTS[name]
            return consts[:, a:a + n]

        def col(name):
            a, n = COLS[name]
            return cols[:, a:a + n]

        def bank(b, n=1):
            return ps[:, b:b + n, :].rearrange("p b c -> p (b c)")

        def link(eng, name, count, ins):
            count[0] += 1
            ins.then_inc(S[name], 1)
            eng.wait_ge(S[name], count[0])

        RING, RING0 = 4, 16
        sem(*[f"ring{i}_loaded" for i in range(RING)], "chunk_done")

        def chunk(n):
            return main[:, (RING0 + 2 * (n % RING)) * U:(RING0 + 2 * (n % RING) + 2) * U]

        def chunk8(n):
            return chunk(n).rearrange("p (k c) -> p k c", k=KD)

        def wide(w, a, n=HALF):
            return w[:, a:a + n].rearrange("(k p) c -> p k c", p=P)

        CHUNKS = []

        def add_chunk(src, k=KD, n=HALF):
            CHUNKS.append((src, k, n))
            return len(CHUNKS) - 1

        w_gla = I["l0_gla_w_in"]
        for i in range(6):
            add_chunk(wide(w_gla, HALF * i))
        for i in range(2):
            add_chunk(wide(I["l0_gla_w_out"], HALF * i))
        N_FIRST = len(CHUNKS)
        w_in = I["w_in_2"].rearrange("b d n -> (b d) n")

        def latent(w):
            return w.rearrange("b h (c p) d -> p (b h c) d", p=P)

        C_CKV = add_chunk(wide(w_in, AT_CKV, LAT), n=LAT)
        C_KW = add_chunk(wide(w_in, AT_KW, 72), n=72)
        C_QI = add_chunk(wide(w_in, AT_QI))
        C_QA = [add_chunk(wide(w_in, AT_Q))]
        C_QA.append(add_chunk(wide(w_in, AT_Q + HALF)))
        C_UK = add_chunk(latent(I["w_uk_2"]), k=16, n=P)
        C_UV = add_chunk(latent(I["w_uv_2"]), k=16, n=P)
        C_QKVD = [add_chunk(wide(w_in, AT_QKVD + HALF * i)) for i in range(6)]
        C_GA = [add_chunk(wide(w_in, AT_GA + HALF * i)) for i in range(2)]
        C_AB = add_chunk(wide(w_in, AT_AB, 16), n=16)
        C_BRA = [add_chunk(wide(I["w_br_att_2"].rearrange("b d n -> (b d) n"), HALF * i)) for i in range(2)]
        C_Z = [add_chunk(wide(w_in, AT_Z + HALF * i)) for i in range(2)]
        C_GD = [add_chunk(wide(w_in, AT_GD + HALF * i)) for i in range(2)]
        C_BRD = [add_chunk(wide(I["w_br_dn_2"].rearrange("b d n -> (b d) n"), HALF * i)) for i in range(2)]
        C_WO = [add_chunk(wide(I["w_out_2"].rearrange("b d n -> (b d) n"), HALF * i)) for i in range(2)]
        N_SECOND = len(CHUNKS)

        def ring_wait(pe, n):
            pe.wait_ge(S[f"ring{n % RING}_loaded"], 16 * (n // RING + 1))

        def load_ring(sp, n):
            if n >= RING:
                sp.wait_ge(S["chunk_done"], n - RING + 1)
            src, k, c = CHUNKS[n]
            dst = chunk(n)[:, 0:k * c].rearrange("p (k c) -> p k c", k=k)
            sp.dma_start(dst, src).then_inc(S[f"ring{n % RING}_loaded"], 16)

        x = rows2(0)
        xn, hT = rows2(1), cols8(2)
        qd, kinv = tiles4(3, 0), tiles4(3, 1)
        kend, kend_rows = tiles4(4, 0), unit(4, 1024).rearrange("p (j c) -> p j c", j=NT)
        v_rows, r_rows = rows2(5), rows2(6)
        la, cum = unit(7, 0, 1024).rearrange("p (j c) -> p j c", j=NT), tiles4(7, 1)
        eb, enb = tiles4(8, 0), tiles4(8, 1)
        kx = tiles4(9, 0)
        soft = unit(9, 1024).rearrange("p (j c) -> p j c", j=NT)
        sc_t = unit(10, 0, 1024).rearrange("p (b c) -> p b c", b=8)
        state = unit(10, 1024).rearrange("p (h c) -> p h c", h=GH)
        y_rows, yT = rows2(11), cols8(1)
        sq = unit(9)
        w_alow = unit(12, 0, KD * GRANK).rearrange("p (k r) -> p k r", k=KD)
        w_aup, b_alpha = main[0:GRANK, 12 * U + 512:12 * U + 1024], main[0:1, 12 * U + 1024:12 * U + 1536]
        alT = main[0:GRANK, 12 * U + 1536:12 * U + 1792]
        ss, rstd = small[:, 0:16], small[:, 16:32]
        up_w = [unit(12 + s).rearrange("p (k g c) -> p k g c", k=KD, g=2) for s in range(2)]
        down_w = [unit(14, s * 1024, s * 1024 + 1024) for s in range(2)]
        conv = [unit(3, s * 1024, s * 1024 + 512).rearrange("p (g t) -> p g t", g=2) for s in range(2)]
        sig = [unit(3, s * 1024 + 512, s * 1024 + 768) for s in range(2)]
        hm = [unit(3, s * 1024 + 768, s * 1024 + 1024) for s in range(2)]
        fnorm = unit(4, 0, 1024)
        ident = const("ident")


        ada_w = main[:, 10 * U:12 * U].rearrange("p (k c) -> p k c", k=KD)
        ada_rows = unit(4, 1024, 1024 + P)
        mod = small[:, 32:80]
        cond = small[:, 80:88]
        h1T = cols8(2)
        qaT, khT, vh, yaT = cols8(3), cols8(4), rows2(5), cols8(6)
        ckv, ckvT = unit(7, 0, 512).rearrange("p (j c) -> p j c", j=NT), unit(7, 512, 1024).rearrange("p (c t) -> p c t", c=2)
        qiT = tiles4(7, 1)
        kiT = unit(8, 0, T)
        score = unit(8, 256, 768).rearrange("p (j s) -> p j s", j=NT)
        causneg = unit(8, 768, 1280).rearrange("p (j s) -> p j s", j=NT)
        keep = unit(8, 1280, 1792).rearrange("p (j s) -> p j s", j=NT)
        relu = unit(9).rearrange("p (b c) -> p b c", b=4)
        prob = [unit(9, 1024 * i, 1024 * i + 1024).rearrange("p (h s) -> p h s", h=4) for i in range(2)]
        probT = [unit(15, 1024 * i, 1024 * i + 1024).rearrange("p (h s q) -> p h s q", h=4, s=2) for i in range(2)]
        widx = small[:, 88:104]
        best = small[:, 104:112]
        amax, asum = small[:, 112:128], small[:, 128:144]
        mixed = cols8(1)
        dnT = unit(10, 0, 3 * U).rearrange("p (n t) -> p n t", t=T)
        def probs(i):
            return unit(i).rearrange("p (n c) -> p n c", c=P)

        dt_row, alog_row = small[:, 144:152], small[:, 152:160]
        g_in, beta, soft_g = small[:, 160:176], small[:, 176:192], small[:, 192:208]
        G_col, G_end, eG, beG, tail = (small[:, 208 + 16 * i:224 + 16 * i] for i in range(5))
        ea_row = small[:, 288:296]
        qT, kT, vT = cols8(10), cols8(11), cols8(12)
        rq, rk = cols8(7), cols8(8)
        eGB, decay, decay_beta = probs(3), probs(4), probs(5)
        AT, qkT, N1 = probs(6), probs(7), probs(5)
        AT_level = [probs(8), probs(9)]
        XT, X = probs(11), probs(12)
        kbG, ktail, vbeta = rows2(13), rows2(14), rows2(15)
        nwT = probs(8)
        dstate, vnew = unit(9, 0, 1024).rearrange("p (h c) -> p h c", h=NH), unit(9, 1024).rearrange("p (h c) -> p h c", h=NH)
        z_rows = rows2(4)
        yd_rows, ydT, gate_d = rows2(6), cols8(5), cols8(12)
        gt_row = unit(9, 0, 1024)
        ln_g, ln_b = unit(11, 0, 1024), unit(11, 1024)
        lnt, centred = rows2(7), rows2(5)
        lsum = small[:, 296:298]
        eps_col = small[:, 298:299]
        gate_w, up2_w, down2_w = ([unit(u + 2 * m, 0, 2 * U) for u in (12, 18, 6)] for m in range(3))
        h2T = cols8(2)
        w_route = unit(3, 0, KD * (NG + NE)).rearrange("p (k c) -> p k c", k=KD)
        xsel = [unit(1, T * i, T * (i + 1)).rearrange("p (k s) -> p k s", k=KD) for i in range(NSLOT)]
        sel = [unit(1, 768 + 64 * i, 832 + 64 * i).rearrange("p (j s) -> p j s", j=NT) for i in range(NSLOT)]
        xrows = unit(1, 960, 960 + T)
        gact = main[2 * SLOTS:P, U + 1216:U + 1472]
        hrows = unit(1, 1472, 1728)
        hidT = unit(1, 1728, 1728 + P).rearrange("p (t s) -> p t s", t=2)
        selg3, selg_over = (unit(3, 512 + T * i, 512 + T * (i + 1)).rearrange("p (j c) -> p j c", j=NT) for i in range(2))
        y3, y_over = unit(4, 0, D), unit(4, D)
        selgT = unit(5, 1280, 1536)
        logitsT = main[0:NG + NE, 5 * U + 1664:5 * U + 1664 + T]
        count_i = unit(5, 1568, 1600).bitcast(I32)
        logits = unit(5, 0, 72).rearrange("p (j c) -> p j c", j=NT)
        grp, ing, pick1, pick2, gate8, both8 = (unit(5, 128 + 16 * i, 144 + 16 * i).rearrange("p (j c) -> p j c", j=NT) for i in range(6))
        cand, ing2, pickg = (unit(5, 256 + 16 * i, 272 + 16 * i).rearrange("p (j c) -> p j c", j=NT) for i in range(3))
        gmax, gsum, top1, top2, ratio, gat1, gat2, first = (unit(5, 320 + 2 * i, 322 + 2 * i) for i in range(8))
        spread = unit(5, 384, 448).rearrange("p (j g i) -> p j g i", j=NT, g=NG)
        chosen, gates_e, rank = (unit(5, 448 + 64 * i, 512 + 64 * i) for i in range(3))
        zero_row = main[0:1, 5 * U + 1024:5 * U + 1152]
        ln_g2, ln_b2 = unit(2, 0, 1024), unit(2, 1024)
        gt_row2 = unit(3, 1024)
        STEPS = {}
        for group, steps in (
            ("gate_sums", (("alow_done", 1), ("alpha_done", 1), ("cum_done", 1))),
            ("gla_inputs", (("alow_copied", 1), ("logs_ready", 1), ("end_diff", 1), ("q_ready", 1), ("k_ready", 2))),
            ("gla_decays", (("alpha_soft", 1), ("cum_ready", 1), ("decays_ready", 2), ("end_decay", 1))),
            ("delta_sums", (("l2_sum", 2), ("gcols_done", 1), ("GB_done", 1), ("bB_done", 1), ("kk_done", 1), ("kq_done", 1), ("k_turned", 1), ("v_turned", 1), ("X_turned", 1), ("w_done", 1))),
            ("delta_ready", (("ab_y", 1), ("g_ready", 1), ("qk_norm", 2), ("gcols_ready", 1), ("tail_diff", 1), ("dec_ready", 1), ("dbeta_ready", 1), ("AT_ready", 1), ("qkT_ready", 1), ("k_rows_ready", 2), ("v_rows_ready", 1))),
            ("delta_decays", (("l2_sq", 2), ("beta_ready", 1), ("ab_abs", 2), ("ea_ready", 1), ("ab_soft", 1), ("l2_root", 2), ("G_exp", 2), ("dec_exp", 1), ("eGB_ready", 1))),
        ):
            sem(group)
            before = 0
            for step_name, n in steps:
                STEPS[step_name] = (group, before)
                before += n

        def made(step_name):
            return S[STEPS[step_name][0]]

        def after(step_name, n):
            group, before = STEPS[step_name]
            return S[group], before + n

        sem("x_loaded", "consts_loaded", "cols_loaded", "alpha_loaded", "dve_step", "act_step",
            "rows_scaled", "square_summed", "root_taken", "turned", "turned_copied", "norm_var")
        sem(
            "v_copied", "r_ready", 
            "kend_turned", "kend_copied", "gscores_done", "gscores_masked",
            "gla_upd", "gla_state", "gla_inter", "y_ready", "y_turned", "yT_ready", "x1_ready")
        sem("up0_loaded", "up1_loaded", "down0_loaded", "down1_loaded", "up_done", "down_done", "conv_tap",
            "conv_part", "conv_ready", "gate_sig", "hm_ready", "x2_ready", "fnorm_loaded", "x3_ready", "stored")
        sem("ada_loaded", "ada_done", "mod_ready", "cond_ready", "mod_plus", "x_turned", "h1_ready", "ckv_ready", "ckv_turned", "ckvT_ready",
            "kidx_ready", "widx_ready", "qidx_ready", "rel_done", "rel_ready", "rel_used", "qatt_ready", "kh_ready", "vh_ready",
            "conv2_tap", "conv2_ready", "dn_qkv_ready", "att_scores", "att_masked", "att_max",
            "att_exp", "att_prob", "att_turned", "att_probT", "att_pv", "ya_ready", "gate_a_ready", "mixed_a_ready")
        sem("rows_small_loaded", 
            
            "qd2_ready", "z_ready",
            "level_masked", "XT_ready", "X_ready", "T1_done", "N1_ready", "X_done", "XT_done", "nw_ready", "u_done",
            "ws_done", "vnew_ready", "dn_inter", "dn_upd", "dstate_ready", "dn_o", "gate_d_ready", "yd_ready", "yd_turned", "ydT_ready",
            "mixed_ready", "gt_done", "gt_ready", "ln_in", "ln_sum", "ln_mean", "ln_gb_loaded", "x4_ready", "eps_ready", "l2_log")
        sem("route_loaded", "logitsT_ready", "logits_turned", "h2_turned", "h2_ready", "logits_done", "logits_ready", "group_exp", "ratio_exp", "ratio_in", "chosen_ready", "ranks_done",
            "tables_ready", "zero_ready", "expert0_loaded", "expert1_loaded", "expert2_loaded", "expert_done", "sel_ready", "xs_done", "xs_ready",
            "gate_up_done", "gate_act", "h_ready", "h_turned", "hT_ready", "down2_done", "yexp_ready", "placed", "selg_turned", "selgT_ready", "xs_scaled", "experts_summed", "x5_ready", "ln_gb2_loaded", "xrows_ready", "xs_turned", "selg_ready", "ada_rows_ready", "ada_turned")

        block = ctx.enter_context(nc.Block())

        @block.sync
        def _(sp):
            sp.dma_start(x, I["x"].rearrange("b (j p) d -> p (b j) d", p=P)).then_inc(S["x_loaded"], 16)
            sp.dma_start(consts[:], I["consts"]).then_inc(S["consts_loaded"], 16)
            sp.dma_start(cols[:], I["cols"]).then_inc(S["cols_loaded"], 16)
            with nc.allow_non_contiguous_dma(reason="64-byte rows of the low-rank projection"):
                sp.dma_start(w_alow, w_gla[:, 3072:3088].rearrange("(k p) r -> p k r", p=P)).then_inc(S["alpha_loaded"], 16)
            sp.dma_start(w_aup, I["l0_gla_w_alpha_up"]).then_inc(S["alpha_loaded"], 16)
            sp.dma_start(b_alpha, I["l0_gla_b_alpha"].unsqueeze(0)).then_inc(S["alpha_loaded"], 16)
            sp.dma_start(dt_row, I["dt_bias_2"].broadcast_to([P, NH])).then_inc(S["rows_small_loaded"], 16)
            sp.dma_start(alog_row, I["a_log_2"].broadcast_to([P, NH])).then_inc(S["rows_small_loaded"], 16)
            for n in range(N_FIRST):
                load_ring(sp, n)

            def load_up(i, s, used=None):
                if used is not None:
                    sp.wait_ge(S["up_done"], used)
                w = I["l0_ffn_w_up"].rearrange("(k p) c -> p k c", p=P)
                for g in range(2):
                    sp.dma_start(up_w[s][:, :, g, :], w[:, :, bass.ds(i * P + g * FF, P)]).then_inc(S[f"up{s}_loaded"], 16)

            def load_down(i, s, used=None):
                if used is not None:
                    sp.wait_ge(S["down_done"], used)
                sp.dma_start(down_w[s], I["l0_ffn_w_down"][bass.ds(i * P, P), :]).then_inc(S[f"down{s}_loaded"], 16)

            sp.wait_ge(*after("alpha_done", 1))
            for i in range(2):
                load_up(i, i)
                load_down(i, i)

            def load_ada(i, used=None):
                if used is not None:
                    sp.wait_ge(S["ada_done"], used)
                sp.dma_start(ada_w, I["w_ada_2"].rearrange("b (k p) c -> p (b k) c", p=P)[:, :, bass.ds(i * HALF, HALF)]).then_inc(S["ada_loaded"], 16)

            sp.wait_ge(S["y_turned"], 4)
            load_ada(0)
            for n in range(N_FIRST, N_FIRST + RING):
                load_ring(sp, n)
            with sp.Fori(1, FT // 2) as i:
                load_up(i * 2, 0, i * 2 - 1)
                load_up(i * 2 + 1, 1, i * 2)
                load_ada(i, i)
                load_down(i * 2, 0, i * 2 - 1)
                load_down(i * 2 + 1, 1, i * 2)
            load_ada(11, 11)
            sp.dma_start(fnorm, I["final_norm"].unsqueeze(0).broadcast_to([P, D])).then_inc(S["fnorm_loaded"], 16)
            for n in range(N_FIRST + RING, N_SECOND):
                load_ring(sp, n)
            sp.wait_ge(S["dn_o"], 4)
            sp.dma_start(ln_g, I["ln_g_2"][:, 0, :].broadcast_to([P, D])).then_inc(S["ln_gb_loaded"], 16)
            sp.dma_start(ln_b, I["ln_b_2"][:, 0, :].broadcast_to([P, D])).then_inc(S["ln_gb_loaded"], 16)
            w_r = sp.dma_start(w_route[:, :, 0:NG], I["w_route_grp_2"].rearrange("b (k p) c -> p (b k) c", p=P))
            w_r.then_inc(S["route_loaded"], 16)
            sp.dma_start(w_route[:, :, NG:], I["w_route_exp_2"].rearrange("b (k p) c -> p (b k) c", p=P)).then_inc(S["route_loaded"], 16)

            def load_matrix(e, s, m):
                w, name, k = ((gate_w, "w_gate_2", KD), (up2_w, "w_up_2", KD), (down2_w, "w_down_2", 4))[m]
                sp.dma_start(w[s].rearrange("p (k c) -> p k c", k=k),
                             I[name].rearrange("b e (k p) c -> p (b e) k c", p=P)[:, bass.ds(e, 1)]).then_inc(
                                 S[f"expert{s}_loaded"], 16)

            load_matrix(0, 0, 1)
            sp.wait_ge(S["chunk_done"], N_SECOND - 3)
            load_matrix(1, 1, 1)
            sp.wait_ge(S["chunk_done"], N_SECOND - 2)
            load_matrix(1, 1, 2)
            sp.wait_ge(S["mixed_ready"], 2)
            load_matrix(0, 0, 0)
            sp.wait_ge(S["chunk_done"], N_SECOND - 1)
            load_matrix(0, 0, 2)
            sp.wait_ge(S["chunk_done"], N_SECOND)
            load_matrix(1, 1, 0)
            sp.wait_ge(S["x4_ready"], 2)
            for m in range(3):
                load_matrix(2, 2, m)
            sp.wait_ge(S["logits_done"], 1)
            sp.dma_start(ln_g2, I["ln_g_2"][:, 1, :].broadcast_to([P, D])).then_inc(S["ln_gb2_loaded"], 16)
            sp.dma_start(ln_b2, I["ln_b_2"][:, 1, :].broadcast_to([P, D])).then_inc(S["ln_gb2_loaded"], 16)

            def load_expert(e, s, done):
                sp.wait_ge(S["expert_done"], done)
                for m in range(3):
                    load_matrix(e, s, m)

            with sp.Fori(1, NE // NSLOT) as i:
                for s in range(NSLOT):
                    load_expert(i * NSLOT + s, s, i * NSLOT + s - 2)
            for e in range(LAST, NE):
                load_expert(e, e - LAST, e - 2)
            for j in range(NT):
                sp.wait_ge(S["x5_ready"], j + 1)
                sp.dma_start(out.rearrange("b (j p) d -> p (b j) d", p=P)[:, j, :], x[:, j, :]).then_inc(S["stored"], 16)
            sp.wait_ge(S["stored"], 32)

        @block.tensor
        def _(pe):
            def turn_rows(src, banks, done):
                for j in range(NT):
                    for kk in range(2):
                        for q in range(4):
                            m = pe.transpose(ps[:, banks[2 * j + kk], q * P:(q + 1) * P],
                                             src[:, j, (4 * kk + q) * P:(4 * kk + q + 1) * P], ident)
                        m.then_inc(S[done] if done in S else made(done), 1)

            def project_cols(n, banks, act):
                for m4 in range(4):
                    for k in range(KD):
                        m = pe.matmul(ps[:, banks[m4 // 2], (m4 % 2) * T:(m4 % 2) * T + T],
                                      chunk8(n)[:, k, m4 * P:(m4 + 1) * P], act[:, k, :], start=(k == 0), stop=(k == KD - 1))
                m.then_inc(S["chunk_done"], 1)

            def project_rows(n, banks, act):
                for j in range(NT):
                    for k in range(KD):
                        m = pe.matmul(ps[:, banks[j], :], act[:, k, j * P:(j + 1) * P], chunk8(n)[:, k, :],
                                      start=(k == 0), stop=(k == KD - 1))
                m.then_inc(S["chunk_done"], 1)

            pe.wait_ge(S["consts_loaded"], 16)
            pe.wait_ge(S["rows_scaled"], 2)
            turn_rows(xn, (0, 1, 2, 3), "turned")
            pe.wait_ge(S["turned_copied"], 4)
            pe.wait_ge(S["alpha_loaded"], 48)
            for k in range(KD):
                m = pe.matmul(ps[0:GRANK, 4, 0:T], w_alow[:, k, :], hT[:, k, :], start=(k == 0), stop=(k == KD - 1))
            m.then_inc(made("alow_done"), 1)
            ring_wait(pe, 0)
            project_cols(0, (0, 1), act=hT)
            pe.wait_ge(*after("alow_copied", 1))
            for j in range(NT):
                pe.matmul(ps[:, 5 + j, :], alT[:, j * P:(j + 1) * P], w_aup, start=True, stop=False)
                m = pe.matmul(ps[:, 5 + j, :], const("ones")[0:1, :], b_alpha, start=False, stop=True)
            m.then_inc(made("alpha_done"), 1)
            ring_wait(pe, 1)
            project_cols(1, (2, 3), act=hT)
            pe.wait_ge(*after("logs_ready", 1))
            for j in range(NT):
                for h in range(GH):
                    m = pe.matmul(ps[:, 5 + j, h * P:(h + 1) * P], la[:, j, h * P:(h + 1) * P], const("upto"), start=True, stop=True)
            m.then_inc(made("cum_done"), 1)
            ring_wait(pe, 2)
            project_rows(2, (4, 7), hT)
            ring_wait(pe, 3)
            pe.wait_ge(*after("q_ready", 1))
            project_rows(3, (0, 1), hT)
            ring_wait(pe, 4)
            pe.wait_ge(S["v_copied"], 2)
            project_rows(4, (4, 7), hT)
            ring_wait(pe, 5)
            pe.wait_ge(*after("k_ready", 2))
            project_rows(5, (2, 3), hT)
            for j in range(NT):
                for h in range(GH):
                    m = pe.transpose(ps[:, 5 + j, h * P:(h + 1) * P], kend[:, h, j * P:(j + 1) * P], ident)
                m.then_inc(S["kend_turned"], 1)
            pe.wait_ge(S["v_copied"], 4)
            for j in range(NT):
                for h in range(GH):
                    t = slice(j * P, (j + 1) * P)
                    m = pe.matmul(ps[:, j, h * P:(h + 1) * P], kinv[:, h, t], qd[:, h, t], start=True, stop=True)
                m.then_inc(S["gscores_done"], 1)

            O_BANK = {(0, 0): 2, (0, 1): 3, (1, 0): 4, (1, 1): 7}

            def gla_update(c, banks):
                j, r = c // 2, (c % 2) * CH
                for h in range(GH):
                    m = pe.matmul(ps[:, banks[h // 2], (h % 2) * GDV:(h % 2 + 1) * GDV],
                                  kend_rows[r:r + CH, j, h * P:(h + 1) * P], v_rows[r:r + CH, j, h * GDV:(h + 1) * GDV],
                                  start=True, stop=True)
                m.then_inc(S["gla_upd"], 1)

            def gla_intra(j):
                for h in range(GH):
                    m = pe.matmul(ps[:, O_BANK[j, h // 2], (h % 2) * GDV:(h % 2 + 1) * GDV], sc_t[:, 4 * j + h, :],
                                  v_rows[:, j, h * GDV:(h + 1) * GDV], start=(h % 2 == 0), stop=False, skip_group_check=True)

            def gla_inter(c, last):
                j, r = c // 2, (c % 2) * CH
                pe.wait_ge(S["gla_state"], c)
                for h in range(GH):
                    m = pe.matmul(ps[r:r + CH, O_BANK[j, h // 2], (h % 2) * GDV:(h % 2 + 1) * GDV],
                                  qd[:, h, c * CH:(c + 1) * CH], state[:, h, :], start=False, stop=last, skip_group_check=True)
                m.then_inc(S["gla_inter"], 1)

            pe.wait_ge(S["kend_copied"], 2)
            gla_update(0, (5, 6))
            pe.wait_ge(S["gscores_masked"], 2)
            gla_update(1, (0, 1))
            pe.wait_ge(S["r_ready"], 4)
            gla_intra(0)
            gla_inter(1, True)
            gla_update(2, (5, 6))
            gla_intra(1)
            gla_inter(2, False)
            gla_inter(3, True)
            pe.wait_ge(S["y_ready"], 2)
            turn_rows(y_rows, (0, 1, 5, 6), "y_turned")
            pe.wait_ge(S["yT_ready"], 4)
            ring_wait(pe, 6)
            project_rows(6, (2, 4), yT)
            ring_wait(pe, 7)
            project_rows(7, (3, 7), yT)
            pe.wait_ge(S["rows_scaled"], 4)
            turn_rows(xn, (4, 5, 6, 7), "turned")
            for j in range(NT):
                for half in range(2):
                    pe.matmul(ps[:, 2 * j + half, :], ident, x[:, j, half * HALF:(half + 1) * HALF], start=True, stop=False)
            pe.wait_ge(S["turned_copied"], 8)

            def ff_up(i, s, free):
                pe.wait_ge(S[f"up{s}_loaded"], (i // 2 + 1) * 32 if isinstance(i, int) else free[1])
                if free[0] is not None:
                    pe.wait_ge(S["conv_ready"], free[0])
                for g in range(2):
                    for k in range(KD):
                        m = pe.matmul(ps[:, 4 + s, g * T:(g + 1) * T], up_w[s][:, k, g, :], hT[:, k, :],
                                      start=(k == 0), stop=(k == KD - 1))
                m.then_inc(S["up_done"], 1)

            def ff_down(done, loaded, s, last=False):
                pe.wait_ge(S["hm_ready"], done)
                pe.wait_ge(S[f"down{s}_loaded"], loaded)
                for j in range(NT):
                    for half in range(2):
                        m = pe.matmul(ps[:, 2 * j + half, :], hm[s][:, j * P:(j + 1) * P],
                                      down_w[s][:, half * HALF:(half + 1) * HALF], start=False, stop=last)
                m.then_inc(S["down_done"], 1)

            def ada(loaded):
                pe.wait_ge(S["ada_loaded"], loaded)
                for k in range(KD):
                    for q in range(4):
                        m = pe.matmul(ps[q * 32:(q + 1) * 32, 6, 0:P], cond[:, k:k + 1].broadcast_to([P, 32]),
                                      ada_w[:, k, q * P:(q + 1) * P], start=(k == 0), stop=(k == KD - 1))
                m.then_inc(S["ada_done"], 1)

            def ada_turn(n, used=None):
                pe.wait_ge(S["ada_rows_ready"], n)
                if used is not None:
                    pe.wait_ge(S["mod_ready"], used)
                pe.transpose(ps[:, 7, 0:P], ada_rows, ident).then_inc(S["ada_turned"], 1)

            ff_up(0, 0, (None,))
            ff_up(1, 1, (None,))
            pe.wait_ge(S["cond_ready"], 1)
            ada(16)
            ff_down(1, 16, 0)
            ada_turn(1)
            with pe.Fori(1, FT // 2) as i:
                ff_up(i * 2, 0, (i * 2 - 1, i * 32 + 32))
                ff_down(i * 2, i * 16, 1)
                ff_up(i * 2 + 1, 1, (i * 2, i * 32 + 32))
                ada(i * 16 + 16)
                ff_down(i * 2 + 1, i * 16 + 16, 0)
                ada_turn(i + 1, i)
            ada(16 * 12)
            ff_down(FT, 16 * (FT // 2), 1, last=True)
            ada_turn(12, 11)
            def turn_k(src, done):
                for k in range(KD):
                    for j in range(NT):
                        m = pe.transpose(ps[:, 4 + k // 2, (k % 2) * T + j * P:(k % 2) * T + (j + 1) * P], src[:, j, k * P:(k + 1) * P], ident)
                    if k % 2:
                        m.then_inc(S[done] if done in S else made(done), 1)

            pe.wait_ge(S["conv_ready"], FT)
            pe.wait_ge(S["mod_ready"], 12)
            pe.wait_ge(S["x3_ready"], 2)
            turn_k(x, "x_turned")
            pe.wait_ge(S["h1_ready"], 8)
            ring_wait(pe, C_CKV)
            for j in range(NT):
                for k in range(KD):
                    m = pe.matmul(ps[:, 0, j * LAT:(j + 1) * LAT], h1T[:, k, j * P:(j + 1) * P],
                                  chunk(C_CKV)[:, k * LAT:(k + 1) * LAT], start=(k == 0), stop=(k == KD - 1))
            m.then_inc(S["chunk_done"], 1)
            ring_wait(pe, C_KW)
            kw = chunk(C_KW)[:, 0:KD * 72].rearrange("p (k c) -> p k c", k=KD)
            for k in range(KD):
                pe.matmul(ps[0:IDH, 1, 0:T], kw[:, k, 0:IDH], h1T[:, k, :], start=(k == 0), stop=(k == KD - 1))
            for j in range(NT):
                for k in range(KD):
                    m = pe.matmul(ps[:, 2, j * IH:(j + 1) * IH], h1T[:, k, j * P:(j + 1) * P], kw[:, k, IDH:72],
                                  start=(k == 0), stop=(k == KD - 1))
            m.then_inc(S["chunk_done"], 1)
            ring_wait(pe, C_QI)
            project_cols(C_QI, (4, 5), act=h1T)

            def index_scores(j):
                for h in range(IH):
                    r, q = (h % 2) * IDH, h // 2
                    m = pe.matmul(ps[:, 4 + (h % 2) * 2 + q // 2, (q % 2) * T:(q % 2 + 1) * T],
                                  qiT[r:r + IDH, q, j * P:(j + 1) * P], kiT[r:r + IDH, :], start=True, stop=True)
                m.then_inc(S["rel_done"], 1)

            pe.wait_ge(S["qidx_ready"], 1)
            pe.wait_ge(S["kidx_ready"], 2)
            index_scores(0)
            ring_wait(pe, C_QA[0])
            pe.wait_ge(S["widx_ready"], 1)
            project_cols(C_QA[0], (2, 3), act=h1T)
            pe.wait_ge(S["rel_ready"], 4)
            index_scores(1)
            pe.wait_ge(S["ckv_ready"], 2)
            for c in range(2):
                for j in range(NT):
                    m = pe.transpose(ps[:, 0, c * T + j * P:c * T + (j + 1) * P], ckv[:, j, c * P:(c + 1) * P], ident)
            m.then_inc(S["ckv_turned"], 1)
            ring_wait(pe, C_QA[1])
            pe.wait_ge(S["qatt_ready"], 1)
            project_cols(C_QA[1], (2, 3), act=h1T)
            ring_wait(pe, C_UK)
            uk = chunk(C_UK)[:, 0:16 * P].rearrange("p (m d) -> p m d", m=16)
            pe.wait_ge(S["ckvT_ready"], 1)
            pe.wait_ge(S["qatt_ready"], 2)
            for h in range(AH):
                for c in range(2):
                    m = pe.matmul(ps[:, h // 2, (h % 2) * T:(h % 2 + 1) * T], uk[:, 2 * h + c, :], ckvT[:, c, :], start=(c == 0), stop=(c == 1))
            m.then_inc(S["chunk_done"], 1)
            ring_wait(pe, C_UV)
            uv = chunk(C_UV)[:, 0:16 * P].rearrange("p (h c d) -> p c h d", h=AH, c=2)
            pe.wait_ge(S["kh_ready"], 2)
            for j in range(NT):
                for half in range(2):
                    for c in range(2):
                        m = pe.matmul(ps[:, 2 * j + half, :], ckvT[:, c, j * P:(j + 1) * P], uv[:, c, 4 * half:4 * half + 4, :], start=(c == 0), stop=(c == 1))
            m.then_inc(S["chunk_done"], 1)
            pe.wait_ge(S["rel_ready"], 8)
            for i in range(6):
                ring_wait(pe, C_QKVD[i])
                if i >= 2:
                    pe.wait_ge(S["conv2_ready"], 4 * (i - 1))
                project_cols(C_QKVD[i], (4, 5) if i % 2 == 0 else (6, 7), act=h1T)
            pe.wait_ge(S["vh_ready"], 4)
            GROUPS = [(j, g) for j in range(NT) for g in range(2)]

            def att_scores(n):
                j, g = GROUPS[n]
                if n >= 1:
                    pe.wait_ge(S["att_masked"], n)
                for i in range(4):
                    h, w = 4 * g + i, P * (j + 1)
                    m = pe.matmul(ps[:, i // 2, (i % 2) * T:(i % 2) * T + w], qaT[:, h, j * P:(j + 1) * P], khT[:, h, 0:w], start=True, stop=True)
                m.then_inc(S["att_scores"], 1)

            def att_out(n):
                j, g = GROUPS[n]
                pe.wait_ge(S["att_prob"], n + 1)
                if n >= 1:
                    pe.wait_ge(S["att_probT"], n)
                for i in range(4):
                    for s in range(j + 1):
                        m = pe.transpose(ps[:, 4 + i // 2, ((i % 2) * 2 + s) * P:((i % 2) * 2 + s + 1) * P], prob[n % 2][:, i, s * P:(s + 1) * P], ident)
                m.then_inc(S["att_turned"], 1)
                pe.wait_ge(S["att_probT"], n + 1)
                if n == 0:
                    pe.wait_ge(S["gate_a_ready"], 1)
                if n >= 2:
                    pe.wait_ge(S["ya_ready"], n - 1)
                for i in range(4):
                    h = 4 * g + i
                    for s in range(j + 1):
                        m = pe.matmul(ps[:, 2 + n % 2, i * P:(i + 1) * P], vh[:, s, h * P:(h + 1) * P], probT[n % 2][:, i, s, :],
                                      start=(s == 0), stop=(s == j))
                m.then_inc(S["att_pv"], 1)

            att_scores(0)
            ring_wait(pe, C_GA[0])
            project_cols(C_GA[0], (2, 3), act=h1T)
            pe.wait_ge(S["conv2_ready"], 24)
            ring_wait(pe, C_GA[1])
            for n in range(4):
                if n + 1 < 4:
                    att_scores(n + 1)
                for k in range(KD):
                    m = pe.matmul(ps[:, 6 + n // 2, (n % 2) * T:(n % 2 + 1) * T], chunk8(C_GA[1])[:, k, n * P:(n + 1) * P], h1T[:, k, :],
                                  start=(k == 0), stop=(k == KD - 1))
                if n == 3:
                    m.then_inc(S["chunk_done"], 1)
                att_out(n)
            ring_wait(pe, C_AB)
            ab = chunk(C_AB)[:, 0:KD * 16].rearrange("p (k c) -> p k c", k=KD)
            pe.wait_ge(S["att_masked"], 4)
            for j in range(NT):
                for k in range(KD):
                    m = pe.matmul(ps[:, 0, j * 16:(j + 1) * 16], h1T[:, k, j * P:(j + 1) * P], ab[:, k, :], start=(k == 0), stop=(k == KD - 1))
            m.then_inc(S["chunk_done"], 1)
            pe.wait_ge(S["gate_a_ready"], 2)
            pe.wait_ge(S["ya_ready"], 4)
            for i, (r, b0) in enumerate(((rq, 4), (rk, 0))):
                pe.wait_ge(*after("l2_sq", i + 1))
                if i == 1:
                    pe.wait_ge(*after("ab_y", 1))
                for b in range(4):
                    m = pe.matmul(bank(b0 + b), const("ones"), r[:, 2 * b:2 * b + 2, :], start=True, stop=True)
                m.then_inc(made("l2_sum"), 1)
            pe.wait_ge(S["l2_log"], 1)
            for i in range(2):
                ring_wait(pe, C_BRA[i])
                project_cols(C_BRA[i], (4 + 2 * i, 5 + 2 * i), act=yaT)
            pe.wait_ge(*after("g_ready", 1))
            pe.wait_ge(S["l2_log"], 2)
            for j in range(NT):
                pe.matmul(ps[:, 0, j * 8:(j + 1) * 8], const("upto"), g_in[:, j * 8:(j + 1) * 8], start=True, stop=True)
                m = pe.matmul(ps[:, 0, 16 + j * 8:24 + j * 8], const("chunk"), g_in[:, j * 8:(j + 1) * 8], start=True, stop=True)
            m.then_inc(made("gcols_done"), 1)
            pe.wait_ge(S["mixed_a_ready"], 2)
            for h in range(NH):
                for j in range(NT):
                    m = pe.matmul(ps[:, 4 + h // 2, (h % 2) * T + j * P:(h % 2) * T + (j + 1) * P],
                                  g_in[:, j * 8 + h:j * 8 + h + 1].broadcast_to([P, P]), const("upto"), start=True, stop=True)
            m.then_inc(made("GB_done"), 1)
            pe.wait_ge(*after("gcols_ready", 1))
            for h in range(NH):
                for j in range(NT):
                    m = pe.matmul(ps[:, h // 2, (h % 2) * T + j * P:(h % 2) * T + (j + 1) * P],
                                  beta[:, j * 8 + h:j * 8 + h + 1].broadcast_to([P, P]), ident, start=True, stop=True)
            m.then_inc(made("bB_done"), 1)

            def each(out0, f):
                for n in range(16):
                    m = f(ps[:, out0 + n // 4, (n % 4) * P:(n % 4 + 1) * P], n // 2, n % 2, n)
                return m

            def span(j):
                return slice(j * P, (j + 1) * P)

            pe.wait_ge(*after("qk_norm", 2))
            pe.wait_ge(*after("eGB_ready", 1))
            each(4, lambda o, h, j, n: pe.matmul(o, kT[:, h, span(j)], kT[:, h, span(j)], start=True, stop=True)).then_inc(made("kk_done"), 1)
            pe.wait_ge(*after("dbeta_ready", 1))
            each(0, lambda o, h, j, n: pe.matmul(o, kT[:, h, span(j)], qT[:, h, span(j)], start=True, stop=True)).then_inc(made("kq_done"), 1)
            pe.wait_ge(*after("AT_ready", 1))
            for j in range(NT):
                for h in range(NH):
                    m = pe.transpose(ps[:, 4 + 2 * j + h // 4, (h % 4) * P:(h % 4 + 1) * P], kT[:, h, span(j)], ident)
            m.then_inc(made("k_turned"), 1)
            pe.wait_ge(*after("qkT_ready", 1))
            for j in range(NT):
                for h in range(NH):
                    m = pe.transpose(ps[:, 2 * j + h // 4, (h % 4) * P:(h % 4 + 1) * P], vT[:, h, span(j)], ident)
            m.then_inc(made("v_turned"), 1)
            pe.wait_ge(*after("k_rows_ready", 2))
            for i in range(2):
                ring_wait(pe, C_Z[i])
                project_rows(C_Z[i], (4 + i, 6 + i), h1T)
            pe.wait_ge(S["XT_ready"], 1)
            pe.wait_ge(S["z_ready"], 4)
            each(4, lambda o, h, j, n: pe.transpose(o, XT[:, n, :], ident)).then_inc(made("X_turned"), 1)
            pe.wait_ge(*after("v_rows_ready", 1))

            def four(g, out0, f):
                for n in range(4 * g, 4 * g + 4):
                    m = f(ps[:, out0 + g, (n % 4) * P:(n % 4 + 1) * P], n)
                return m

            for level in range(1, 6):
                A_l = AT_level[level % 2]
                pe.wait_ge(S["level_masked"], level + 1)
                for g in range(4):
                    pe.wait_ge(S["X_ready"], 4 * (level - 1) + g + 1)
                    if level > 1:
                        pe.wait_ge(S["XT_ready"], 4 * (level - 2) + g + 2)
                    four(g, 0, lambda o, n: pe.matmul(o, A_l[:, n, :], X[:, n, :], start=True, stop=True)).then_inc(S["T1_done"], 1)
                for g in range(4):
                    pe.wait_ge(S["N1_ready"], 4 * (level - 1) + g + 1)
                    if level < 5:
                        four(g, 4, lambda o, n: pe.matmul(o, XT[:, n, :], N1[:, n, :], start=True, stop=True)).then_inc(S["X_done"], 1)
                    four(g, 0, lambda o, n: pe.matmul(o, N1[:, n, :], XT[:, n, :], start=True, stop=True)).then_inc(S["XT_done"], 1)
            pe.wait_ge(S["XT_ready"], 1 + 4 * 5)
            pe.wait_ge(S["X_ready"], 4 * 5)
            each(4, lambda o, h, j, n: pe.matmul(o, kbG[:, j, h * P:(h + 1) * P], XT[:, n, :], start=True, stop=True)).then_inc(made("w_done"), 1)

            def dn_heads(f):
                for h in range(NH):
                    m = f(h)
                return m

            for j in range(NT):
                if j == 1:
                    pe.wait_ge(S["vnew_ready"], 2)
                dn_heads(lambda h: pe.matmul(ps[:, h // 4, (h % 4) * P:(h % 4 + 1) * P], XT[:, 2 * h + j, :], vbeta[:, j, h * P:(h + 1) * P],
                                             start=(h % 4 == 0), stop=False, skip_group_check=True)).then_inc(S["u_done"], 1)
                for half in range(2):
                    c, r = 2 * j + half, half * CH
                    ob = 2 if j == 0 else 6

                    def part(b0, h):
                        return ps[r:r + CH, b0 + h // 4, (h % 4) * P:(h % 4 + 1) * P]

                    if c > 0:
                        pe.wait_ge(S["dstate_ready"], c)
                        pe.wait_ge(S["qd2_ready"], 1)
                        pe.wait_ge(S["nw_ready"], 1)
                        dn_heads(lambda h: pe.matmul(part(0, h), nwT[:, 2 * h + j, r:r + CH], dstate[:, h, :], start=False, stop=True,
                                                     skip_group_check=True)).then_inc(S["ws_done"], 1)
                        dn_heads(lambda h: pe.matmul(part(ob, h), qT[:, h, c * CH:(c + 1) * CH], dstate[:, h, :], start=(h % 4 == 0), stop=False,
                                                     skip_group_check=True)).then_inc(S["dn_inter"], 1)
                    pe.wait_ge(S["vnew_ready"], c + 1)
                    if c < NCH - 1:
                        if c == 0:
                            pe.wait_ge(S["nw_ready"], 1)
                        dn_heads(lambda h: pe.matmul(ps[:, 4 + h // 4, (h % 4) * P:(h % 4 + 1) * P], ktail[r:r + CH, j, h * P:(h + 1) * P],
                                                     vnew[r:r + CH, h, :], start=True, stop=True)).then_inc(S["dn_upd"], 1)
                    dn_heads(lambda h: pe.matmul(part(ob, h), qkT[r:r + CH, 2 * h + j, r:r + CH], vnew[r:r + CH, h, :],
                                                 start=(c == 0 and h % 4 == 0), stop=True, skip_group_check=True)).then_inc(S["dn_o"], 1)
            for i, banks in enumerate(((0, 1), (4, 5))):
                ring_wait(pe, C_GD[i])
                project_cols(C_GD[i], banks, act=h1T)
            pe.wait_ge(S["yd_ready"], 2)
            pe.wait_ge(S["gate_d_ready"], 2)
            turn_rows(yd_rows, (0, 1, 4, 5), "yd_turned")
            pe.wait_ge(S["ydT_ready"], 4)
            for i, banks in enumerate(((2, 3), (6, 7))):
                ring_wait(pe, C_BRD[i])
                project_cols(C_BRD[i], banks, act=ydT)
            pe.wait_ge(S["mixed_ready"], 1)
            for k in range(KD):
                m = pe.matmul(ps[:, 2 + k // 4, (k % 4) * P:(k % 4 + 1) * P], mod[:, 16 + k:17 + k].broadcast_to([P, P]), ident, start=True, stop=True)
            m.then_inc(S["gt_done"], 1)
            pe.wait_ge(S["mixed_ready"], 2)
            for i, banks in enumerate(((0, 4), (1, 5))):
                ring_wait(pe, C_WO[i])
                project_rows(C_WO[i], banks, mixed)
            pe.wait_ge(S["x4_ready"], 2)
            turn_k(x, "h2_turned")
            pe.wait_ge(S["h2_ready"], 8)
            pe.wait_ge(S["route_loaded"], 32)
            NR = NG + NE
            for k in range(KD):
                m = pe.matmul(ps[0:NR, 4, 0:T], w_route[:, k, :], h2T[:, k, :], start=(k == 0), stop=(k == KD - 1))
            m.then_inc(S["logits_done"], 1)
            pe.wait_ge(S["logitsT_ready"], 1)
            for j in range(NT):
                m = pe.transpose(ps[:, 5, j * NR:(j + 1) * NR], logitsT[:, j * P:(j + 1) * P], ident[0:NR, 0:NR])
            m.then_inc(S["logits_turned"], 1)
            for k in range(KD):
                m = pe.matmul(ps[:, 6 + k // 4, (k % 4) * P:(k % 4 + 1) * P], mod[:, 40 + k:41 + k].broadcast_to([P, P]), ident, start=True, stop=True)
            m.then_inc(S["gt_done"], 1)
            pe.wait_ge(S["zero_ready"], 1)
            for b in range(4):
                m = pe.matmul(bank(b), zero_row, consts[0:1, 0:HALF], start=True, stop=False, skip_group_check=True)
            pe.wait_ge(S["chosen_ready"], 1)
            pe.matmul(ps[:, 5, 0:NE], const("earlier"), chosen[:, 0:NE], start=True, stop=True)
            pe.matmul(ps[:, 5, NE:2 * NE], const("ones"), chosen[:, 0:NE], start=True, stop=False)
            pe.matmul(ps[:, 5, NE:2 * NE], const("earlier"), chosen[:, NE:2 * NE], start=False, stop=True)
            pe.matmul(ps[:, 5, 2 * NE:3 * NE], const("ones"), chosen[:, 0:NE], start=True, stop=False)
            pe.matmul(ps[:, 5, 2 * NE:3 * NE], const("ones"), chosen[:, NE:2 * NE], start=False, stop=True).then_inc(S["ranks_done"], 1)
            pe.wait_ge(S["tables_ready"], 1)
            blocks, gathers, places = (pe.alloc_register(n) for n in ("pe_blocks", "pe_gathers", "pe_places"))
            for r in (blocks, gathers, places):
                pe.reg_mov(r, 0)

            def gather(s, again=False):
                before = pe.snap(gathers)
                if again:
                    pe.wait_ge(S["xs_ready"], before)
                pe.wait_ge(S["sel_ready"], before + 1)
                for j in range(NT):
                    for q in range(4):
                        m = pe.matmul(ps[q * SLOTS:(q + 1) * SLOTS, 4, 0:T], sel[s][:, j, :], x[:, j, q * T:(q + 1) * T], start=(j == 0), stop=(j == 1))
                m.then_inc(S["xs_done"], 1)
                pe.reg_add(gathers, gathers, 1)

            def turn_gathered():
                pe.wait_ge(S["xrows_ready"], pe.snap(gathers))
                for t in range(2):
                    m = pe.transpose(ps[:, 4, T + t * P:T + (t + 1) * P], xrows[:, t * P:(t + 1) * P], ident)
                m.then_inc(S["xs_turned"], 1)

            def turn_selection(src, selected):
                pe.wait_ge(S["selg_ready"], selected)
                for j in range(NT):
                    m = pe.transpose(ps[:, 6, j * P:(j + 1) * P], src[:, j, :], ident)
                m.then_inc(S["selg_turned"], 1)

            def place(rows, n):
                turned = pe.snap(places) + 1
                pe.wait_ge(S["yexp_ready"], n * 4 + 3)
                pe.wait_ge(S["selgT_ready"], turned)
                for j in range(NT):
                    for half in range(2):
                        m = pe.matmul(ps[:, 2 * j + half, :], selgT[:, j * P:(j + 1) * P], rows[:, half * HALF:(half + 1) * HALF],
                                      start=False, stop=False, skip_group_check=True)
                m.then_inc(S["placed"], 1)
                pe.reg_add(places, places, 1)

            def gate_up(s, n):
                pe.wait_ge(S["xs_ready"], n)
                for k in range(KD):
                    for q in range(4):
                        w = (gate_w, up2_w)[q // 2][s].rearrange("p (k c) -> p k c", k=KD)[:, k, (q % 2) * T:(q % 2 + 1) * T]
                        m = pe.matmul(ps[q * SLOTS:(q + 1) * SLOTS, 5, 0:T], xsel[s][:, k, :], w, start=(k == 0), stop=(k == KD - 1))
                m.then_inc(S["gate_up_done"], 1)

            def turn_hidden(n):
                pe.wait_ge(S["h_ready"], n + 1)
                for t in range(2):
                    m = pe.transpose(ps[:, 5, T + t * P:T + (t + 1) * P], hrows[:, t * P:(t + 1) * P], ident)
                m.then_inc(S["h_turned"], 1)

            def down(s, n):
                dw = down2_w[s].rearrange("p (k c) -> p k c", k=4)
                pe.wait_ge(S["yexp_ready"], n * 4 + 3)
                pe.wait_ge(S["hT_ready"], n + 1)
                for kt in range(4):
                    for q in range(4):
                        m = pe.matmul(ps[q * SLOTS:(q + 1) * SLOTS, 7, 0:T], hidT[:, kt % 2, (kt // 2) * SLOTS:(kt // 2 + 1) * SLOTS],
                                      dw[:, kt, q * T:(q + 1) * T], start=(kt == 0), stop=(kt == 3))
                m.then_inc(S["down2_done"], 1)
                pe.reg_add(blocks, blocks, 1)

            def pe_first_block(s, group_start, ahead):
                n = pe.snap(blocks)
                gate_up(s, pe.snap(gathers))
                if group_start:
                    turn_selection(selg3, n + 2)
                if ahead:
                    gather((s + 1) % NSLOT)
                turn_hidden(n)
                if group_start:
                    place(y3, n)
                if ahead:
                    turn_gathered()
                down(s, n)

            def pe_more(s):
                n = pe.snap(blocks)
                gather(s, again=True)
                turn_gathered()
                gate_up(s, pe.snap(gathers))
                turn_hidden(n)
                down(s, n)
                turn_selection(selg_over, n + 3)
                place(y_over, n + 1)

            def pe_expert(e, g, loaded, ahead=True):
                s = g
                pe.wait_ge(S[f"expert{s}_loaded"], loaded)
                count = pe.value_load(count_i[0:1, bass.ds(e, 1)], min_val=0, max_val=T)
                pe_first_block(s, g == 0, ahead)
                with pe.If(count > SLOTS):
                    pe_more(s)
                with pe.If(count > 2 * SLOTS):
                    with pe.Fori(2, T // SLOTS):
                        pe_more(s)
                pe.drain().then_inc(S["expert_done"], 1)

            gather(0)
            turn_gathered()
            with pe.Fori(0, NE // NSLOT) as i:
                for g in range(NSLOT):
                    pe_expert(i * NSLOT + g, g, i * 48 + 48)
            for e in range(LAST, NE):
                pe_expert(e, e - LAST, (NE // NSLOT + 1) * 48, ahead=(e < NE - 1))
            turn_selection(selg3, pe.snap(blocks) + 2)
            place(y3, pe.snap(blocks))
            pe.drain().then_inc(S["experts_summed"], 1)

        @block.scalar
        def _(act):
            def add_squares(srcs, first=0, squares=sq):
                for i, src in enumerate(srcs, first):
                    act.activation(squares[:, i * src.shape[-1]:(i + 1) * src.shape[-1]], src, ACT.Square, accum_out=ss[:, i:i + 1]).then_inc(S["square_summed"], 1)

            def take_root(r, n):
                act.wait_ge(S["norm_var"], r + 1)
                act.activation(rstd[:, 0:n], rstd[:, 0:n], ACT.Sqrt).then_inc(S["root_taken"], 1)

            def norm_root(r, srcs, n):
                add_squares(srcs)
                take_root(r, n)

            def centred_root(n):
                for j in range(NT):
                    act.wait_ge(S["ln_in"], NT * n + j + 1)
                    act.activation(lnt[:, j, :], x[:, j, :], ACT.Copy, accum_out=lsum[:, j:j + 1]).then_inc(S["ln_sum"], 1)
                for j in range(NT):
                    act.wait_ge(S["ln_mean"], NT * n + j + 1)
                    act.activation(lnt[:, j, :], x[:, j, :], ACT.Square, bias=lsum[:, j:j + 1], accum_out=ss[:, j:j + 1]).then_inc(S["square_summed"], 1)
                take_root(6 + n, NT)

            act.wait_ge(S["x_loaded"], 16)
            norm_root(0, [x[:, j, :] for j in range(NT)], NT)
            act.wait_ge(*after("alpha_done", 1))
            z = bank(5, 2).rearrange("p (j c) -> p j c", j=NT)
            act.activation(soft, z, ACT.Abs).then_inc(S["act_step"], 1)
            act.wait_ge(S["act_step"], 1)
            act.activation(soft, soft, ACT.Exp, scale=-1.0).then_inc(S["act_step"], 1)
            act.wait_ge(S["act_step"], 2)
            act.activation(soft, soft, ACT.Ln, bias=1.0).then_inc(made("alpha_soft"), 1)
            act.wait_ge(*after("cum_done", 1))
            by_head = bank(5, 2).rearrange("p (j h t) -> p h j t", j=NT, h=GH)
            act.activation(cum.rearrange("p h (j t) -> p h j t", j=NT), by_head, ACT.Copy, scale=1.0 / GTAU).then_inc(made("cum_ready"), 1)
            act.wait_ge(*after("cum_ready", 1))
            act.activation(eb, cum, ACT.Exp).then_inc(made("decays_ready"), 1)
            act.activation(enb, cum, ACT.Exp, scale=-1.0).then_inc(made("decays_ready"), 1)
            act.wait_ge(*after("end_diff", 1))
            act.activation(kx, kx, ACT.Exp).then_inc(made("end_decay"), 1)
            for half, banks in ((0, (4, 7)), (1, (0, 1))):
                act.wait_ge(S["chunk_done"], 3 + half)
                for j in range(NT):
                    act.activation(v_rows[:, j, half * HALF:(half + 1) * HALF], bank(banks[j]), ACT.Copy).then_inc(S["v_copied"], 1)
            for half, banks in ((0, (4, 7)), (1, (2, 3))):
                act.wait_ge(S["chunk_done"], 5 + half)
                for j in range(NT):
                    act.activation(r_rows[:, j, half * HALF:(half + 1) * HALF], bank(banks[j]), ACT.Silu).then_inc(S["r_ready"], 1)
            for j in range(NT):
                act.wait_ge(S["kend_turned"], j + 1)
                act.activation(kend_rows[:, j, :], bank(5 + j), ACT.Copy).then_inc(S["kend_copied"], 1)
            act.wait_ge(S["gla_inter"], 3)
            o_banks = {(0, 0): 2, (0, 1): 3, (1, 0): 4, (1, 1): 7}
            norm_root(1, [bank(o_banks[j, h // 2])[:, (h % 2) * GDV:(h % 2 + 1) * GDV] for j in range(NT) for h in range(GH)], NT * GH)
            act.wait_ge(S["cols_loaded"], 16)
            act.activation(cond, col("cond"), ACT.Silu).then_inc(S["cond_ready"], 1)
            act.wait_ge(S["x1_ready"], 4)
            norm_root(2, [x[:, j, :] for j in range(NT)], NT)

            def ff_taps(done, s, i):
                act.wait_ge(S["up_done"], done + 1)
                for g in range(2):
                    act.activation(conv[s][:, g, :], ps[:, 4 + s, g * T:(g + 1) * T], ACT.Identity,
                                   scale=cols[:, bass.ds(COLS["conv_w"][0] + 2 * 2 * FT + g * FT + i, 1)],
                                   bias=cols[:, bass.ds(COLS["conv_b"][0] + g * FT + i, 1)]).then_inc(S["conv_tap"], 1)
                act.wait_ge(S["conv_ready"], done + 1)
                act.activation(sig[s], conv[s][:, 0, :], ACT.Silu).then_inc(S["gate_sig"], 1)

            ff_taps(0, 0, 0)
            ff_taps(1, 1, 1)
            with act.Fori(1, FT // 2) as i:
                for s in range(2):
                    act.wait_ge(S["hm_ready"], i * 2 + s - 1)
                    ff_taps(i * 2 + s, s, i * 2 + s)
            act.wait_ge(S["x2_ready"], 1)
            norm_root(3, [x[:, j, :] for j in range(NT)], NT)
            act.wait_ge(S["mod_plus"], 2)
            for k in range(4):
                act.wait_ge(S["x_turned"], k // 2 + 1)
                act.activation(h1T[:, k, :], ps[:, 4 + k // 2, (k % 2) * T:(k % 2 + 1) * T], ACT.Identity, scale=mod[:, 8 + k:9 + k], bias=mod[:, k:k + 1]).then_inc(S["h1_ready"], 1)
            act.wait_ge(S["chunk_done"], C_CKV + 1)
            norm_root(4, [ps[:, 0, j * LAT:(j + 1) * LAT] for j in range(NT)], NT)
            act.wait_ge(S["chunk_done"], C_KW + 1)
            act.activation(kiT[IDH:P, :], ps[0:IDH, 1, 0:T], ACT.Copy).then_inc(S["kidx_ready"], 1)
            act.wait_ge(S["chunk_done"], C_QI + 1)
            act.activation(qiT.rearrange("p k t -> p (k t)"), bank(4, 2), ACT.Copy).then_inc(S["qidx_ready"], 1)
            for j in range(NT):
                act.wait_ge(S["rel_done"], j + 1)
                if j == 1:
                    act.wait_ge(S["rel_used"], 1)
                else:
                    act.wait_ge(S["ckv_ready"], 2)
                for b in range(4):
                    act.activation(relu[:, b, :], bank(4 + b), ACT.Relu).then_inc(S["rel_ready"], 1)
                act.wait_ge(S["chunk_done"], C_QA[j] + 1)
                act.activation(qaT[:, 4 * j:4 * j + 4, :].rearrange("p k t -> p (k t)"), bank(2, 2), ACT.Copy).then_inc(S["qatt_ready"], 1)
            act.wait_ge(S["chunk_done"], C_UK + 1)
            for i in range(2):
                act.activation(khT[:, 4 * i:4 * i + 4, :].rearrange("p k t -> p (k t)"), bank(2 * i, 2), ACT.Copy).then_inc(S["kh_ready"], 1)
            act.wait_ge(S["chunk_done"], C_UV + 1)
            for j in range(NT):
                act.activation(vh[:, j, :], bank(2 * j, 2), ACT.Copy).then_inc(S["vh_ready"], 2)
            for n in range(24):
                act.wait_ge(S["chunk_done"], C_QKVD[n // 4] + 1)
                b = 4 + (n // 4) % 2 * 2 + (n % 4) // 2
                act.activation(dnT[:, n, :], ps[:, b, (n % 2) * T:(n % 2 + 1) * T], ACT.Copy,
                               scale=col("dn_conv")[:, 3 * 24 + n:3 * 24 + n + 1]).then_inc(S["conv2_tap"], 1)
            for i in range(3):
                act.wait_ge(S["conv2_ready"], 8 * (i + 1))
                act.activation(dnT[:, 8 * i:8 * i + 8, :], dnT[:, 8 * i:8 * i + 8, :], ACT.Silu).then_inc(S["dn_qkv_ready"], 1)
            def gate_a(i, b0):
                act.wait_ge(S["chunk_done"], C_GA[i] + 1)
                act.activation(mixed[:, 4 * i:4 * i + 4, :].rearrange("p k t -> p (k t)"), bank(b0, 2), ACT.Sigmoid).then_inc(S["gate_a_ready"], 1)

            for n in range(4):
                j = n // 2
                act.wait_ge(S["att_max"], n + 1)
                for i in range(4):
                    w = P * (j + 1)
                    act.activation(prob[n % 2][:, i, 0:w], prob[n % 2][:, i, 0:w], ACT.Exp, scale=ATT_SCALE, bias=amax[:, 4 * n + i:4 * n + i + 1],
                                   accum_out=asum[:, 4 * n + i:4 * n + i + 1]).then_inc(S["att_exp"], 1)
                if n == 0:
                    gate_a(0, 2)
                act.wait_ge(S["att_turned"], n + 1)
                if n >= 2:
                    act.wait_ge(S["att_pv"], n - 1)
                act.activation(probT[n % 2][:, :, 0:j + 1, :].rearrange("p h s q -> p h (s q)"),
                               bank(4, 2).rearrange("p (h c) -> p h c", h=4)[:, :, 0:P * (j + 1)], ACT.Copy).then_inc(S["att_probT"], 1)
            gate_a(1, 6)
            act.wait_ge(S["att_pv"], 4)
            act.wait_ge(S["eps_ready"], 1)
            act.activation(rq, qT, ACT.Square).then_inc(made("l2_sq"), 1)
            act.activation(rk, kT, ACT.Square).then_inc(made("l2_sq"), 1)
            act.wait_ge(S["chunk_done"], C_AB + 1)
            ab = ps[:, 0, 0:32].rearrange("p (j c) -> p j c", j=NT)
            act.activation(beta.rearrange("p (j c) -> p j c", j=NT), ab[:, :, 8:16], ACT.Sigmoid).then_inc(made("beta_ready"), 1)
            act.wait_ge(*after("ab_y", 1))
            act.activation(soft_g, g_in, ACT.Abs).then_inc(made("ab_abs"), 1)
            act.wait_ge(*after("ab_abs", 1))
            act.activation(soft_g, soft_g, ACT.Exp, scale=-1.0).then_inc(made("ab_abs"), 1)
            act.wait_ge(*after("ab_abs", 2))
            act.wait_ge(S["rows_small_loaded"], 32)
            act.activation(ea_row, alog_row, ACT.Exp).then_inc(made("ea_ready"), 1)
            act.activation(soft_g, soft_g, ACT.Ln, bias=1.0).then_inc(made("ab_soft"), 1)
            for i, (r, b0) in enumerate(((rq, 4), (rk, 0))):
                act.wait_ge(*after("l2_sum", i + 1))
                act.activation(r.rearrange("p k t -> p (k t)"), bank(b0, 4), ACT.Ln, bias=eps_col).then_inc(S["l2_log"], 1)
            for i, r in enumerate((rq, rk)):
                act.wait_ge(S["l2_log"], i + 1)
                act.activation(r, r, ACT.Exp, scale=-0.5).then_inc(made("l2_root"), 1)
            act.wait_ge(*after("gcols_ready", 1))
            act.activation(eG, G_col, ACT.Exp).then_inc(made("G_exp"), 1)
            act.wait_ge(*after("tail_diff", 1))
            act.activation(tail, tail, ACT.Exp).then_inc(made("G_exp"), 1)
            act.wait_ge(*after("dec_ready", 1))
            act.activation(decay, decay, ACT.Exp).then_inc(made("dec_exp"), 1)
            act.activation(eGB.rearrange("p n c -> p (n c)"), bank(4, 4), ACT.Exp).then_inc(made("eGB_ready"), 1)
            for i in range(2):
                act.wait_ge(S["chunk_done"], C_Z[i] + 1)
                act.wait_ge(*after("qkT_ready", 1))
                for j in range(NT):
                    act.activation(z_rows[:, j, i * HALF:(i + 1) * HALF], bank(4 + i + 2 * j), ACT.Silu).then_inc(S["z_ready"], 1)
            act.wait_ge(*after("X_turned", 1))
            for g in range(4):
                act.activation(X[:, 4 * g:4 * g + 4, :].rearrange("p n c -> p (n c)"), bank(4 + g), ACT.Copy).then_inc(S["X_ready"], 1)
            for n in range(16):
                act.wait_ge(S["X_done"], n + 1)
                g = n % 4
                act.activation(X[:, 4 * g:4 * g + 4, :].rearrange("p n c -> p (n c)"), bank(4 + g), ACT.Copy).then_inc(S["X_ready"], 1)
            act.wait_ge(*after("w_done", 1))
            act.activation(nwT.rearrange("p n c -> p (n c)"), bank(4, 4), ACT.Copy, scale=-1.0).then_inc(S["nw_ready"], 1)
            for j in range(NT):
                act.wait_ge(S["dn_o"], 2 * j + 2)
                add_squares([ps[:, (2 if j == 0 else 6) + h // 4, (h % 4) * P:(h % 4 + 1) * P] for h in range(NH)], j * NH, unit(12))
            take_root(5, NT * NH)
            for i, b0 in enumerate((0, 4)):
                act.wait_ge(S["chunk_done"], C_GD[i] + 1)
                act.activation(gate_d[:, 4 * i:4 * i + 4, :].rearrange("p k t -> p (k t)"), bank(b0, 2), ACT.Sigmoid).then_inc(S["gate_d_ready"], 1)
            act.wait_ge(S["gt_done"], 1)
            act.activation(gt_row, bank(2, 2), ACT.Copy).then_inc(S["gt_ready"], 1)
            centred_root(0)
            act.wait_ge(S["x4_ready"], 2)
            for k in range(4):
                act.wait_ge(S["h2_turned"], k // 2 + 1)
                act.activation(h2T[:, k, :], ps[:, 4 + k // 2, (k % 2) * T:(k % 2 + 1) * T], ACT.Identity, scale=mod[:, 32 + k:33 + k],
                               bias=mod[:, 24 + k:25 + k]).then_inc(S["h2_ready"], 1)
            act.wait_ge(S["logits_ready"], 1)
            act.activation(grp[:, :, 4:8], grp[:, :, 0:4], ACT.Exp).then_inc(S["group_exp"], 1)
            act.wait_ge(S["ratio_in"], 1)
            act.activation(ratio, ratio, ACT.Exp).then_inc(S["ratio_exp"], 1)
            act.wait_ge(S["gt_done"], 2)
            act.activation(gt_row2, bank(6, 2), ACT.Copy).then_inc(S["gt_ready"], 1)
            act.wait_ge(S["tables_ready"], 1)
            blocks, gathers, turns = (act.alloc_register(n) for n in ("act_blocks", "act_gathers", "act_turns"))
            for r in (blocks, gathers, turns):
                act.reg_mov(r, 0)

            def copy_gathered():
                act.wait_ge(S["xs_done"], act.snap(gathers) + 1)
                act.activation(xrows, ps[:, 4, 0:T], ACT.Copy).then_inc(S["xrows_ready"], 1)
                act.reg_add(gathers, gathers, 1)

            def copy_selection():
                act.reg_add(turns, turns, 1)
                act.wait_ge(S["selg_turned"], act.snap(turns))
                act.activation(selgT, ps[:, 6, 0:T], ACT.Copy).then_inc(S["selgT_ready"], 1)

            def act_block(dst, a, group_start=False, ahead=False, more=False):
                if more:
                    copy_gathered()
                n = act.snap(blocks)
                act.wait_ge(S["gate_up_done"], n + 1)
                act.activation(gact, ps[0:2 * SLOTS, 5, 0:T], ACT.Silu).then_inc(S["gate_act"], 1)
                if group_start:
                    copy_selection()
                if ahead:
                    copy_gathered()
                act.wait_ge(S["h_turned"], n + 1)
                act.activation(hidT, ps[:, 5, T:2 * T].rearrange("p (t c) -> p t c", t=2)[:, :, 0:2 * SLOTS], ACT.Copy).then_inc(S["hT_ready"], 1)
                used = act.snap(turns)
                act.wait_ge(S["down2_done"], n + 1)
                act.wait_ge(S["placed"], used)
                for q in range(2):
                    act.activation(dst[a:a + SLOTS, q * T:(q + 1) * T], ps[q * SLOTS:(q + 1) * SLOTS, 7, 0:T], ACT.Copy).then_inc(S["yexp_ready"], 1)
                if more:
                    copy_selection()
                act.reg_add(blocks, blocks, 1)

            def act_expert(e, g, ahead=True):
                count = act.value_load(count_i[0:1, bass.ds(e, 1)], min_val=0, max_val=T)
                act_block(y3, g * SLOTS, g == 0, ahead)
                with act.If(count > SLOTS):
                    act_block(y_over, 0, more=True)
                with act.If(count > 2 * SLOTS):
                    with act.Fori(2, T // SLOTS):
                        act_block(y_over, 0, more=True)

            copy_gathered()
            with act.Fori(0, NE // NSLOT) as i:
                for g in range(NSLOT):
                    act_expert(i * NSLOT + g, g)
            for e in range(LAST, NE):
                act_expert(e, e - LAST, ahead=(e < NE - 1))
            copy_selection()
            centred_root(1)

        @block.vector
        def _(dve):
            steps = [0]

            def step(ins):
                steps[0] += 1
                ins.then_inc(S["dve_step"], 1)
                dve.wait_ge(S["dve_step"], steps[0])

            def norm_scale(r, sums, n, width, eps=RMS_EPS):
                dve.wait_ge(S["square_summed"], sums)
                dve.tensor_scalar(rstd[:, 0:n], ss[:, 0:n], 1.0 / width, eps, ALU.mult, ALU.add).then_inc(S["norm_var"], 1)
                dve.wait_ge(S["root_taken"], r + 1)
                step(dve.reciprocal(rstd[:, 0:n], rstd[:, 0:n]))

            def scale_rows(dst):
                for j in range(NT):
                    dve.tensor_scalar(dst[:, j, :], x[:, j, :], rstd[:, j:j + 1], None, ALU.mult).then_inc(S["rows_scaled"], 1)

            def copy_turned(dst, banks, gain, turned, first, done):
                for j in range(NT):
                    for kk in range(2):
                        dve.wait_ge(S[turned], first + 2 * j + kk + 1)
                        dve.tensor_tensor(dst[:, 4 * kk:4 * kk + 4, j * P:(j + 1) * P],
                                          bank(banks[2 * j + kk]).rearrange("p (k t) -> p k t", k=4),
                                          gain[:, 4 * kk:4 * kk + 4].unsqueeze(2).broadcast_to([P, 4, P]), ALU.mult).then_inc(S[done] if done in S else made(done), 1)

            norm_scale(0, NT, NT, D)
            scale_rows(xn)
            dve.wait_ge(S["cols_loaded"], 16)
            copy_turned(hT, (0, 1, 2, 3), col("norm1"), "turned", 0, "turned_copied")
            dve.wait_ge(*after("alow_done", 1))
            dve.tensor_copy(alT, ps[0:GRANK, 4, 0:T]).then_inc(made("alow_copied"), 1)
            dve.wait_ge(*after("alpha_soft", 1))
            z = bank(5, 2).rearrange("p (j c) -> p j c", j=NT)
            dve.scalar_tensor_tensor(out=la, in0=z, scalar=0.0, in1=soft, op0=ALU.min, op1=ALU.subtract).then_inc(made("logs_ready"), 1)
            dve.wait_ge(*after("cum_ready", 1))
            by_chunk = cum.rearrange("p h (c t) -> p (h c) t", t=CH)
            dve.tensor_tensor(kx.rearrange("p h (c t) -> p (h c) t", t=CH), by_chunk[:, :, CH - 1:CH].broadcast_to([P, GH * NCH, CH]),
                              by_chunk, ALU.subtract).then_inc(made("end_diff"), 1)
            dve.wait_ge(*after("decays_ready", 2))
            dve.scalar_tensor_tensor(out=qd.rearrange("p h t -> p (h t)"), in0=bank(0, 2), scalar=GDK ** -0.5,
                                     in1=eb.rearrange("p h t -> p (h t)"), op0=ALU.mult, op1=ALU.mult).then_inc(made("q_ready"), 1)
            dve.tensor_tensor(kinv.rearrange("p h t -> p (h t)"), bank(2, 2), enb.rearrange("p h t -> p (h t)"), ALU.mult).then_inc(made("k_ready"), 1)
            dve.wait_ge(*after("end_decay", 1))
            dve.tensor_tensor(kend.rearrange("p h t -> p (h t)"), bank(2, 2), kx.rearrange("p h t -> p (h t)"), ALU.mult).then_inc(made("k_ready"), 1)
            for j in range(NT):
                dve.wait_ge(S["gscores_done"], j + 1)
                dve.tensor_tensor(sc_t[:, 4 * j:4 * j + 4, :], bank(j).rearrange("p (h t) -> p h t", h=4),
                                  const("upto").unsqueeze(1).broadcast_to([P, 4, P]), ALU.mult).then_inc(S["gscores_masked"], 1)
            dve.wait_ge(S["gla_upd"], 1)
            dve.tensor_copy(state.rearrange("p h c -> p (h c)"), bank(5, 2)).then_inc(S["gla_state"], 1)
            for c, banks in ((1, (0, 1)), (2, (5, 6))):
                dve.wait_ge(S["gla_upd"], c + 1)
                dve.wait_ge(S["gla_inter"], c)
                dve.wait_ge(S["gla_state"], c)
                for h in range(GH):
                    at = c * CH + CH - 1
                    m = dve.scalar_tensor_tensor(out=state[:, h, :], in0=state[:, h, :], scalar=eb[:, h, at:at + 1],
                                                 in1=bank(banks[h // 2])[:, (h % 2) * GDV:(h % 2 + 1) * GDV], op0=ALU.mult, op1=ALU.add)
                m.then_inc(S["gla_state"], 1)
            norm_scale(1, NT + NT * GH, NT * GH, GDV)
            o_banks = {(0, 0): 2, (0, 1): 3, (1, 0): 4, (1, 1): 7}
            for j in range(NT):
                for h in range(GH):
                    g = slice(h * GDV, (h + 1) * GDV)
                    m = dve.scalar_tensor_tensor(out=y_rows[:, j, g], in0=bank(o_banks[j, h // 2])[:, (h % 2) * GDV:(h % 2 + 1) * GDV],
                                                 scalar=rstd[:, 4 * j + h:4 * j + h + 1], in1=r_rows[:, j, g], op0=ALU.mult, op1=ALU.mult)
                m.then_inc(S["y_ready"], 1)
            copy_turned(yT, (0, 1, 5, 6), col("out_norm"), "y_turned", 0, "yT_ready")
            for half, banks in ((0, (2, 4)), (1, (3, 7))):
                dve.wait_ge(S["chunk_done"], 7 + half)
                for j in range(NT):
                    c = slice(half * HALF, (half + 1) * HALF)
                    dve.tensor_tensor(x[:, j, c], x[:, j, c], bank(banks[j]), ALU.add).then_inc(S["x1_ready"], 1)
            dve.wait_ge(S["x1_ready"], 4)
            norm_scale(2, NT + NT * GH + NT, NT, D)
            scale_rows(xn)
            copy_turned(hT, (4, 5, 6, 7), col("norm2"), "turned", 4, "turned_copied")

            def ff_conv(done, s, i, taps):
                dve.wait_ge(S["conv_tap"], taps)
                for tap, gap in ((1, 1), (0, 2)):
                    for g in range(2):
                        m = dve.scalar_tensor_tensor(out=conv[s][:, g, gap:], in0=ps[:, 4 + s, g * T:(g + 1) * T - gap],
                                                     scalar=cols[:, bass.ds(COLS["conv_w"][0] + tap * 2 * FT + g * FT + i, 1)],
                                                     in1=conv[s][:, g, gap:], op0=ALU.mult, op1=ALU.add)
                        if tap == 1:
                            m.then_inc(S["conv_part"], 1)
                            if g == 1:
                                dve.wait_ge(S["conv_part"], taps)
                m.then_inc(S["conv_ready"], 1)

            def ff_mul(done, s, free):
                dve.wait_ge(S["gate_sig"], done + 1)
                if free is not None:
                    dve.wait_ge(S["down_done"], free)
                dve.tensor_tensor(hm[s], sig[s], conv[s][:, 1, :], ALU.mult).then_inc(S["hm_ready"], 1)

            def take_ada(done):
                dve.wait_ge(S["ada_done"], done)
                dve.tensor_copy(ada_rows, ps[:, 6, 0:P]).then_inc(S["ada_rows_ready"], 1)

            def modulation(i, done):
                dve.wait_ge(S["ada_turned"], done)
                dve.tensor_tensor(mod[:, bass.ds(i * 4, 4)], ps[:, 7, 0:P].rearrange("p (q r) -> p q r", q=4)[:, :, 0], cols[:, bass.ds(COLS["b_ada"][0] + i * 4, 4)], ALU.add).then_inc(S["mod_ready"], 1)

            for i in range(2):
                ff_conv(i, i, i, 2 * i + 2)
                ff_mul(i, i, None)
            take_ada(1)
            with dve.Fori(1, FT // 2) as i:
                for s in range(2):
                    ff_conv(i * 2 + s, s, i * 2 + s, i * 4 + 2 * s + 2)
                    ff_mul(i * 2 + s, s, i * 2 + s - 1)
                    if s == 0:
                        modulation(i - 1, i)
                take_ada(i + 1)
            modulation(10, 11)
            take_ada(12)
            modulation(11, 12)
            dve.wait_ge(S["down_done"], FT)
            dve.tensor_copy(unit(0), bank(0, 4)).then_inc(S["x2_ready"], 1)
            dve.wait_ge(S["x2_ready"], 1)
            norm_scale(3, 2 * NT + NT * GH + NT, NT, D)
            dve.wait_ge(S["fnorm_loaded"], 16)
            for j in range(NT):
                dve.scalar_tensor_tensor(out=x[:, j, :], in0=x[:, j, :], scalar=rstd[:, j:j + 1], in1=fnorm,
                                         op0=ALU.mult, op1=ALU.mult).then_inc(S["x3_ready"], 1)
            dve.wait_ge(S["mod_ready"], 12)
            dve.tensor_scalar(mod[:, 8:24], mod[:, 8:24], 1.0, None, ALU.add).then_inc(S["mod_plus"], 1)
            dve.tensor_scalar(mod[:, 32:48], mod[:, 32:48], 1.0, None, ALU.add).then_inc(S["mod_plus"], 1)
            dve.wait_ge(S["mod_plus"], 2)
            for k in range(4, KD):
                dve.wait_ge(S["x_turned"], k // 2 + 1)
                dve.tensor_scalar(h1T[:, k, :], ps[:, 4 + k // 2, (k % 2) * T:(k % 2 + 1) * T], mod[:, 8 + k:9 + k], mod[:, k:k + 1], ALU.mult, ALU.add).then_inc(S["h1_ready"], 1)
            step(dve.tensor_scalar(causneg.rearrange("p j s -> p (j s)"), consts[:, CONSTS["causal0"][0]:CONSTS["causal0"][0] + 2 * T],
                                   -NEG, NEG, ALU.mult, ALU.add))
            norm_scale(4, 4 * NT + NT * GH, NT, LAT)
            for j in range(NT):
                dve.tensor_scalar(ckv[:, j, :], ps[:, 0, j * LAT:(j + 1) * LAT], rstd[:, j:j + 1], None, ALU.mult).then_inc(S["ckv_ready"], 1)
            dve.wait_ge(S["chunk_done"], C_KW + 1)
            dve.tensor_scalar(widx, ps[:, 2, 0:2 * IH], INDEX_SCALE, None, ALU.mult).then_inc(S["widx_ready"], 1)
            dve.wait_ge(S["kidx_ready"], 1)
            dve.tensor_copy(kiT[0:IDH, :], ps[0:IDH, 1, 0:T]).then_inc(S["kidx_ready"], 1)
            dve.wait_ge(S["widx_ready"], 1)
            for j in range(NT):
                if j == 1:
                    dve.wait_ge(S["ckv_turned"], 1)
                    dve.tensor_tensor(ckvT, bank(0).rearrange("p (c t) -> p c t", c=2), col("kv_g").unsqueeze(2).broadcast_to([P, 2, T]),
                                      ALU.mult).then_inc(S["ckvT_ready"], 1)
                for b in range(4):
                    dve.wait_ge(S["rel_ready"], 4 * j + b + 1)
                    for c in range(2):
                        h = b // 2 + 2 * (2 * (b % 2) + c)
                        w = widx[:, j * IH + h:j * IH + h + 1]
                        if b == 0 and c == 0:
                            step(dve.tensor_scalar(score[:, j, :], relu[:, b, 0:T], w, None, ALU.mult))
                        else:
                            m = dve.scalar_tensor_tensor(out=score[:, j, :], in0=relu[:, b, c * T:(c + 1) * T], scalar=w, in1=score[:, j, :],
                                                         op0=ALU.mult, op1=ALU.add)
                            step(m)
                causal = const(f"causal{j}")
                dve.tensor_tensor(score[:, j, :], score[:, j, :], causal, ALU.mult).then_inc(S["rel_used"], 1)
                dve.wait_ge(S["rel_used"], j + 1)
                step(dve.tensor_tensor(score[:, j, :], score[:, j, :], causneg[:, j, :], ALU.add))
                for _ in range(TOPK // 8):
                    step(dve.max(best, score[:, j, :]))
                    step(dve.match_replace(score[:, j, :], best, score[:, j, :], TAKEN))
                step(dve.tensor_scalar(keep[:, j, :], score[:, j, :], (NEG + TAKEN) / 2, None, ALU.is_lt))
                step(dve.tensor_tensor(keep[:, j, :], keep[:, j, :], causal, ALU.mult))
                step(dve.tensor_scalar(keep[:, j, :], keep[:, j, :], -NEG, NEG, ALU.mult, ALU.add))
            for n in range(24):
                dve.wait_ge(S["conv2_tap"], n // 2 * 2 + 2)
                b = 4 + (n // 4) % 2 * 2 + (n % 4) // 2
                for tap in (2, 1, 0):
                    gap = 3 - tap
                    m = dve.scalar_tensor_tensor(out=dnT[:, n, gap:], in0=ps[:, b, (n % 2) * T:(n % 2 + 1) * T - gap],
                                                 scalar=col("dn_conv")[:, tap * 24 + n:tap * 24 + n + 1], in1=dnT[:, n, gap:], op0=ALU.mult, op1=ALU.add)
                    if tap:
                        step(m)
                m.then_inc(S["conv2_ready"], 1)
            for n in range(4):
                j, w = n // 2, P * (n // 2 + 1)
                dve.wait_ge(S["att_scores"], n + 1)
                if n >= 2:
                    dve.wait_ge(S["att_turned"], n - 1)
                dve.tensor_tensor(prob[n % 2][:, :, 0:w], bank(0, 2).rearrange("p (h s) -> p h s", h=4)[:, :, 0:w],
                                  keep[:, j, 0:w].unsqueeze(1).broadcast_to([P, 4, w]), ALU.add).then_inc(S["att_masked"], 1)
                dve.wait_ge(S["att_masked"], n + 1)
                step(dve.reduce_max(amax[:, 4 * n:4 * n + 4], prob[n % 2][:, :, 0:w], AX_X))
                dve.tensor_scalar(amax[:, 4 * n:4 * n + 4], amax[:, 4 * n:4 * n + 4], -ATT_SCALE, None, ALU.mult).then_inc(S["att_max"], 1)
                dve.wait_ge(S["att_exp"], 4 * n + 4)
                step(dve.reciprocal(asum[:, 4 * n:4 * n + 4], asum[:, 4 * n:4 * n + 4]))
                for i in range(4):
                    m = dve.tensor_scalar(prob[n % 2][:, i, 0:w], prob[n % 2][:, i, 0:w], asum[:, 4 * n + i:4 * n + i + 1], None, ALU.mult)
                m.then_inc(S["att_prob"], 1)
                for done in ((n - 1,) if n < 3 else (2, 3)):
                    if done >= 0:
                        dve.wait_ge(S["att_pv"], done + 1)
                        dve.tensor_copy(yaT[:, 4 * (done % 2):4 * (done % 2) + 4, done // 2 * P:(done // 2 + 1) * P],
                                        bank(2 + done % 2).rearrange("p (h q) -> p h q", h=4)).then_inc(S["ya_ready"], 1)
            dve.wait_ge(*after("beta_ready", 1))
            dve.wait_ge(S["rows_small_loaded"], 32)
            ab = ps[:, 0, 0:32].rearrange("p (j c) -> p j c", j=NT)
            per_head = lambda row: row.unsqueeze(1).broadcast_to([P, NT, NH])
            gj = g_in.rearrange("p (j c) -> p j c", j=NT)
            dve.tensor_tensor(gj, ab[:, :, 0:8], per_head(dt_row), ALU.add).then_inc(made("ab_y"), 1)
            dve.wait_ge(*after("ab_y", 1))
            dve.wait_ge(*after("ab_soft", 1))
            dve.wait_ge(*after("ea_ready", 1))
            step(dve.scalar_tensor_tensor(out=g_in, in0=g_in, scalar=0.0, in1=soft_g, op0=ALU.max, op1=ALU.add))
            dve.scalar_tensor_tensor(out=gj, in0=gj, scalar=-1.0, in1=per_head(ea_row), op0=ALU.mult, op1=ALU.mult).then_inc(made("g_ready"), 1)
            for i, (r, t, s) in enumerate(((rq, qT, NDK ** -0.5), (rk, kT, 1.0))):
                dve.wait_ge(*after("l2_root", i + 1))
                dve.scalar_tensor_tensor(out=t, in0=t, scalar=s, in1=r, op0=ALU.mult, op1=ALU.mult).then_inc(made("qk_norm"), 1)
            for i in range(2):
                dve.wait_ge(S["chunk_done"], C_BRA[i] + 1)
                dve.wait_ge(S["gate_a_ready"], i + 1)
                m4 = mixed[:, 4 * i:4 * i + 4, :].rearrange("p k t -> p (k t)")
                dve.tensor_tensor(m4, m4, bank(4 + 2 * i, 2), ALU.mult).then_inc(S["mixed_a_ready"], 1)
            dve.wait_ge(*after("gcols_done", 1))
            dve.tensor_copy(small[:, 208:240], ps[:, 0, 0:32]).then_inc(made("gcols_ready"), 1)
            dve.wait_ge(*after("gcols_ready", 1))
            dve.tensor_tensor(tail, G_end, G_col, ALU.subtract).then_inc(made("tail_diff"), 1)
            dve.wait_ge(*after("GB_done", 1))
            for n in range(16):
                h, j = n // 2, n % 2
                m = dve.tensor_scalar(decay[:, n, :], ps[:, 4 + n // 4, (n % 4) * P:(n % 4 + 1) * P], G_col[:, j * 8 + h:j * 8 + h + 1], 0.0,
                                      ALU.subtract, ALU.min)
            m.then_inc(made("dec_ready"), 1)
            dve.wait_ge(*after("G_exp", 2))
            step(dve.tensor_tensor(beG, beta, eG, ALU.mult))
            dve.wait_ge(*after("dec_exp", 1))

            def all16(c):
                return c.unsqueeze(1).broadcast_to([P, 16, P])

            step(dve.tensor_tensor(decay, decay, all16(const("upto")), ALU.mult))
            dve.wait_ge(*after("bB_done", 1))
            dve.tensor_tensor(decay_beta.rearrange("p n c -> p (n c)"), bank(0, 4), decay.rearrange("p n c -> p (n c)"), ALU.mult).then_inc(made("dbeta_ready"), 1)
            dve.wait_ge(*after("kk_done", 1))
            dve.wait_ge(*after("dbeta_ready", 1))
            dve.tensor_tensor(AT.rearrange("p n c -> p (n c)"), bank(4, 4), decay_beta.rearrange("p n c -> p (n c)"), ALU.mult).then_inc(made("AT_ready"), 1)
            dve.wait_ge(*after("kq_done", 1))
            dve.tensor_tensor(qkT.rearrange("p n c -> p (n c)"), bank(0, 4), decay.rearrange("p n c -> p (n c)"), ALU.mult).then_inc(made("qkT_ready"), 1)

            def rows_times(dst, b0, scal, done):
                for j in range(NT):
                    m = dve.tensor_tensor(dst[:, j, :].rearrange("p (h c) -> p h c", h=NH), bank(b0 + 2 * j, 2).rearrange("p (h c) -> p h c", h=NH),
                                          scal[:, j * 8:(j + 1) * 8].unsqueeze(2).broadcast_to([P, NH, P]), ALU.mult)
                m.then_inc(S[done] if done in S else made(done), 1)

            dve.wait_ge(*after("k_turned", 1))
            rows_times(kbG, 4, beG, "k_rows_ready")
            rows_times(ktail, 4, tail, "k_rows_ready")
            dve.wait_ge(*after("v_turned", 1))
            rows_times(vbeta, 0, beta, "v_rows_ready")
            dve.wait_ge(S["level_masked"], 1)
            dve.scalar_tensor_tensor(out=XT, in0=AT_level[0], scalar=-1.0, in1=all16(ident), op0=ALU.mult, op1=ALU.add).then_inc(S["XT_ready"], 1)
            for level in range(1, 6):
                for g in range(4):
                    n = 4 * (level - 1) + g + 1
                    dve.wait_ge(S["T1_done"], n)
                    dve.scalar_tensor_tensor(out=N1[:, 4 * g:4 * g + 4, :], in0=bank(g).rearrange("p (n c) -> p n c", n=4), scalar=-1.0,
                                             in1=ident.unsqueeze(1).broadcast_to([P, 4, P]), op0=ALU.mult, op1=ALU.add).then_inc(S["N1_ready"], 1)
                for g in range(4):
                    n = 4 * (level - 1) + g + 1
                    dve.wait_ge(S["XT_done"], n)
                    dve.tensor_copy(XT[:, 4 * g:4 * g + 4, :].rearrange("p n c -> p (n c)"), bank(g)).then_inc(S["XT_ready"], 1)
            for j in range(NT):
                for half in range(2):
                    c, r = 2 * j + half, half * CH
                    if half == 0:
                        dve.wait_ge(S["u_done"], j + 1)
                    if c > 0:
                        dve.wait_ge(S["ws_done"], c)
                    dve.tensor_copy(vnew[r:r + CH].rearrange("p h c -> p (h c)"), ps[r:r + CH, 0:2, :].rearrange("p b c -> p (b c)")).then_inc(S["vnew_ready"], 1)
                    if c == NCH - 1:
                        break
                    dve.wait_ge(S["dn_upd"], c + 1)
                    if c == 0:
                        dve.tensor_copy(dstate.rearrange("p h c -> p (h c)"), bank(4, 2)).then_inc(S["dstate_ready"], 1)
                    else:
                        dve.wait_ge(S["dn_inter"], c)
                        dve.wait_ge(S["dstate_ready"], c)
                        for h in range(NH):
                            m = dve.scalar_tensor_tensor(out=dstate[:, h, :], in0=dstate[:, h, :],
                                                         scalar=eGB[:, 2 * h + j, r + CH - 1:r + CH], in1=ps[:, 4 + h // 4, (h % 4) * P:(h % 4 + 1) * P],
                                                         op0=ALU.mult, op1=ALU.add)
                        m.then_inc(S["dstate_ready"], 1)
            norm_scale(5, 4 * NT + NT * GH + NT * NH, NT * NH, P)
            for j in range(NT):
                for h in range(NH):
                    hs = slice(h * P, (h + 1) * P)
                    m = dve.scalar_tensor_tensor(out=yd_rows[:, j, hs], in0=ps[:, (2 if j == 0 else 6) + h // 4, (h % 4) * P:(h % 4 + 1) * P],
                                                 scalar=rstd[:, 8 * j + h:8 * j + h + 1], in1=z_rows[:, j, hs], op0=ALU.mult, op1=ALU.mult)
                m.then_inc(S["yd_ready"], 1)
            copy_turned(ydT, (0, 1, 4, 5), col("dn_g").broadcast_to([P, 8]), "yd_turned", 0, "ydT_ready")
            for i, b0 in enumerate((2, 6)):
                dve.wait_ge(S["chunk_done"], C_BRD[i] + 1)
                dve.wait_ge(S["gate_d_ready"], 2)
                part = slice(4 * i, 4 * i + 4)
                flat = "p k t -> p (k t)"
                step(dve.tensor_tensor(gate_d[:, part, :].rearrange(flat), bank(b0, 2), gate_d[:, part, :].rearrange(flat), ALU.mult))
                dve.tensor_tensor(mixed[:, part, :].rearrange(flat), mixed[:, part, :].rearrange(flat), gate_d[:, part, :].rearrange(flat),
                                  ALU.add).then_inc(S["mixed_ready"], 1)

            def layer_norm(n, banks, waits, gate, sums, params, gain, shift, done):
                for j in range(NT):
                    for half in range(2):
                        dve.wait_ge(*waits[half])
                        c = slice(half * HALF, (half + 1) * HALF)
                        step(dve.tensor_tensor(lnt[:, j, c], bank(banks[j, half]), gate[:, c], ALU.mult))
                    dve.scalar_tensor_tensor(out=x[:, j, :], in0=x[:, j, :], scalar=ALPHA, in1=lnt[:, j, :], op0=ALU.mult, op1=ALU.add).then_inc(S["ln_in"], 1)
                for j in range(NT):
                    dve.wait_ge(S["ln_sum"], NT * n + j + 1)
                    dve.tensor_scalar(lsum[:, j:j + 1], lsum[:, j:j + 1], -1.0 / D, None, ALU.mult).then_inc(S["ln_mean"], 1)
                dve.wait_ge(S["ln_mean"], NT * n + NT)
                dve.wait_ge(*params)
                for j in range(NT):
                    step(dve.scalar_tensor_tensor(out=centred[:, j, :], in0=x[:, j, :], scalar=lsum[:, j:j + 1], in1=gain, op0=ALU.add, op1=ALU.mult))
                norm_scale(6 + n, sums, NT, D, LN_EPS)
                for j in range(NT):
                    dve.scalar_tensor_tensor(out=x[:, j, :], in0=centred[:, j, :], scalar=rstd[:, j:j + 1], in1=shift, op0=ALU.mult, op1=ALU.add).then_inc(S[done], 1)

            dve.wait_ge(S["gt_ready"], 1)
            SUMS5 = 4 * NT + NT * GH + NT * NH
            layer_norm(0, {(0, 0): 0, (1, 0): 4, (0, 1): 1, (1, 1): 5},
                       [(S["chunk_done"], C_WO[0] + 1), (S["chunk_done"], C_WO[1] + 1)], gt_row, SUMS5 + NT,
                       (S["ln_gb_loaded"], 32), ln_g, ln_b, "x4_ready")
            for k in range(4, KD):
                dve.wait_ge(S["h2_turned"], k // 2 + 1)
                dve.tensor_scalar(h2T[:, k, :], ps[:, 4 + k // 2, (k % 2) * T:(k % 2 + 1) * T], mod[:, 32 + k:33 + k], mod[:, 24 + k:25 + k],
                                  ALU.mult, ALU.add).then_inc(S["h2_ready"], 1)
            dve.memset(zero_row, 0.0).then_inc(S["zero_ready"], 1)
            for t in (selg3, selg_over):
                dve.memset(t, 0.0).then_inc(S["selg_ready"], 1)
            for t in (y3, y_over, hrows):
                dve.memset(t, 0.0).then_inc(S["yexp_ready"], 1)

            def wide8(c, n=8):
                return c.unsqueeze(2).broadcast_to([P, NT, n])

            def earliest_max(values, n, top, onehot):
                step(dve.reduce_max(top, values, AX_X))
                step(dve.tensor_tensor(cand[:, :, 0:n], values, wide8(top, n), ALU.is_equal))
                step(dve.tensor_tensor(cand[:, :, 0:n], cand[:, :, 0:n], const("first")[:, 0:n].unsqueeze(1).broadcast_to([P, NT, n]), ALU.mult))
                step(dve.reduce_max(first, cand[:, :, 0:n], AX_X))
                step(dve.tensor_tensor(onehot, cand[:, :, 0:n], wide8(first, n), ALU.is_equal))

            dve.wait_ge(S["logits_done"], 1)
            dve.tensor_copy(logitsT, ps[0:NG + NE, 4, 0:T]).then_inc(S["logitsT_ready"], 1)
            dve.wait_ge(S["logits_turned"], 1)
            step(dve.tensor_copy(logits.rearrange("p j c -> p (j c)"), ps[:, 5, 0:72]))
            earliest_max(logits[:, :, 0:NG], NG, gmax, pickg[:, :, 0:NG])
            dve.tensor_tensor(grp[:, :, 0:NG], logits[:, :, 0:NG], wide8(gmax, NG), ALU.subtract).then_inc(S["logits_ready"], 1)
            for j in range(NT):
                step(dve.tensor_tensor(spread[:, j], logits[:, j, NG:].rearrange("p (g i) -> p g i", g=NG),
                                       pickg[:, j, 0:NG].unsqueeze(2).broadcast_to([P, NG, EPG]), ALU.mult))
                step(dve.reduce_sum(ing[:, j, :], spread[:, j].rearrange("p g i -> p i g"), AX_X))
            earliest_max(ing, EPG, top1, pick1)
            step(dve.scalar_tensor_tensor(out=ing2, in0=pick1, scalar=NEG, in1=ing, op0=ALU.mult, op1=ALU.add))
            earliest_max(ing2, EPG, top2, pick2)
            dve.tensor_tensor(ratio, top2, top1, ALU.subtract).then_inc(S["ratio_in"], 1)
            dve.wait_ge(S["group_exp"], 1)
            step(dve.reduce_sum(gsum, grp[:, :, 4:8], AX_X))
            dve.wait_ge(S["ratio_exp"], 1)
            step(dve.scalar_tensor_tensor(out=gat1, in0=ratio, scalar=1.0, in1=gsum, op0=ALU.add, op1=ALU.mult))
            step(dve.reciprocal(gat1, gat1))
            step(dve.tensor_tensor(gat2, gat1, ratio, ALU.mult))
            step(dve.tensor_tensor(gate8, pick1, wide8(gat1), ALU.mult))
            step(dve.tensor_tensor(cand, pick2, wide8(gat2), ALU.mult))
            step(dve.tensor_tensor(gate8, gate8, cand, ALU.add))
            step(dve.tensor_tensor(both8, pick1, pick2, ALU.add))
            for src, dst in ((both8, chosen), (gate8, gates_e)):
                for j in range(NT):
                    m = dve.tensor_tensor(dst[:, j * NE:(j + 1) * NE].rearrange("p (g i) -> p g i", g=NG), src[:, j].unsqueeze(1).broadcast_to([P, NG, EPG]),
                                          pickg[:, j, 0:NG].unsqueeze(2).broadcast_to([P, NG, EPG]), ALU.mult)
                    if dst is chosen and j == 1:
                        m.then_inc(S["chosen_ready"], 1)
                    else:
                        step(m)
            dve.wait_ge(S["ranks_done"], 1)
            dve.wait_ge(S["chosen_ready"], 1)
            step(dve.scalar_tensor_tensor(out=rank, in0=ps[:, 5, 0:2 * NE], scalar=1.0, in1=chosen, op0=ALU.add, op1=ALU.mult))
            step(dve.tensor_scalar(rank, rank, -1.0, None, ALU.add))
            dve.tensor_copy(count_i, ps[:, 5, 2 * NE:3 * NE]).then_inc(S["tables_ready"], 1)
            dve.wait_ge(S["tables_ready"], 1)
            blocks, gathers, turns = (dve.alloc_register(n) for n in ("dve_blocks", "dve_gathers", "dve_turns"))
            for r in (blocks, gathers, turns):
                dve.reg_mov(r, 0)

            def rank_slots(e, b):
                slots = consts[:, bass.ds(CONSTS["slot"][0] + b * SLOTS, SLOTS)]
                return slots, [rank[:, bass.ds(j * NE + e, 1)] for j in range(NT)]

            def select(e, b, s):
                slots, ranks = rank_slots(e, b)
                for j in range(NT):
                    m = dve.tensor_scalar(sel[s][:, j, :], slots, ranks[j], None, ALU.is_equal)
                m.then_inc(S["sel_ready"], 1)

            def select_weighted(e, b, dst, a):
                slots, ranks = rank_slots(e, b)
                dve.wait_ge(S["selg_turned"], dve.snap(turns))
                for j in range(NT):
                    m = dve.tensor_scalar(dst[:, j, a:a + SLOTS], slots, ranks[j], gates_e[:, bass.ds(j * NE + e, 1)], ALU.is_equal, ALU.mult)
                m.then_inc(S["selg_ready"], 1)

            def take_gathered(s):
                n = dve.snap(gathers)
                dve.wait_ge(S["xs_turned"], n + 1)
                xs = ps[:, 4, T:2 * T].rearrange("p (t q s) -> p q t s", t=2, q=4)
                by_tile = lambda c: c.rearrange("p (q t) -> p q t", t=2).unsqueeze(3).broadcast_to([P, 4, 2, SLOTS])
                dst = xsel[s].rearrange("p (q t) s -> p q t s", t=2)
                dve.tensor_tensor(dst, xs, by_tile(mod[:, 32:40]), ALU.mult).then_inc(S["xs_scaled"], 1)
                dve.wait_ge(S["xs_scaled"], n + 1)
                dve.tensor_tensor(dst, dst, by_tile(mod[:, 24:32]), ALU.add).then_inc(S["xs_ready"], 1)
                dve.reg_add(gathers, gathers, 1)

            def dve_block(e, b, s, dst, a, selg, group_start=False, ahead=False, more=False):
                if group_start:
                    dve.reg_add(turns, turns, 1)
                if ahead:
                    select(e + 1, 0, (s + 1) % NSLOT)
                if more:
                    select(e, b, s)
                    take_gathered(s)
                n = dve.snap(blocks)
                dve.wait_ge(S["gate_act"], n + 1)
                dve.tensor_tensor(hrows[0:2 * SLOTS, :], gact, ps[2 * SLOTS:P, 5, 0:T], ALU.mult).then_inc(S["h_ready"], 1)
                select_weighted(e, b, selg, a)
                if ahead:
                    take_gathered((s + 1) % NSLOT)
                used = dve.snap(turns)
                dve.wait_ge(S["down2_done"], n + 1)
                dve.wait_ge(S["placed"], used)
                for q in range(2, 4):
                    dve.tensor_copy(dst[a:a + SLOTS, q * T:(q + 1) * T], ps[q * SLOTS:(q + 1) * SLOTS, 7, 0:T]).then_inc(S["yexp_ready"], 1)
                if more:
                    dve.reg_add(turns, turns, 1)
                dve.reg_add(blocks, blocks, 1)

            def dve_expert(e, g, ahead=True, last=False):
                count = dve.value_load(count_i[0:1, bass.ds(e, 1)], min_val=0, max_val=T)
                if last:
                    dve.memset(selg3[:, :, (g + 1) * SLOTS:], 0.0)
                dve_block(e, 0, g, y3, g * SLOTS, selg3, g == 0, ahead)
                with dve.If(count > SLOTS):
                    dve_block(e, 1, g, y_over, 0, selg_over, more=True)
                with dve.If(count > 2 * SLOTS):
                    with dve.Fori(2, T // SLOTS) as b:
                        dve_block(e, b, g, y_over, 0, selg_over, more=True)

            dve.wait_ge(S["yexp_ready"], 3)
            dve.wait_ge(S["selg_ready"], 2)
            select(0, 0, 0)
            take_gathered(0)
            with dve.Fori(0, NE // NSLOT) as i:
                for g in range(NSLOT):
                    dve_expert(i * NSLOT + g, g)
            for e in range(LAST, NE):
                dve_expert(e, e - LAST, ahead=(e < NE - 1), last=(e == NE - 1))
            dve.wait_ge(S["gt_ready"], 2)
            dve.wait_ge(S["experts_summed"], 1)
            layer_norm(1, {(0, 0): 0, (0, 1): 1, (1, 0): 2, (1, 1): 3}, [(S["gt_ready"], 2), (S["gt_ready"], 2)], gt_row2, SUMS5 + 2 * NT,
                       (S["ln_gb2_loaded"], 32), ln_g2, ln_b2, "x5_ready")

        @block.gpsimd
        def _(pool):
            pool.memset(eps_col, 1e-6).then_inc(S["eps_ready"], 1)
            pool.wait_ge(S["consts_loaded"], 16)
            pool.wait_ge(*after("AT_ready", 1))
            for level in range(6):
                if level == 0:
                    pool.wait_ge(*after("qk_norm", 2))
                if level == 2:
                    pool.wait_ge(S["XT_ready"], 1)
                if level >= 3:
                    pool.wait_ge(S["T1_done"], 4 * (level - 2))
                up = const(f"up{level}").unsqueeze(1).broadcast_to([P, 16, P])
                pool.tensor_tensor(AT_level[level % 2], AT, up, ALU.mult).then_inc(S["level_masked"], 1)
            pool.wait_ge(*after("qkT_ready", 1))
            pool.wait_ge(*after("eGB_ready", 1))
            pool.tensor_tensor(probs(10), probs(10), eGB, ALU.mult).then_inc(S["qd2_ready"], 1)


INPUTS = [
    "x", "l0_gla_w_in", "l0_gla_w_alpha_up", "l0_gla_b_alpha", "l0_gla_w_out", "l0_ffn_w_up", "l0_ffn_w_down", "final_norm",
    "w_ada_2", "w_in_2", "w_uk_2", "w_uv_2", "a_log_2", "dt_bias_2", "w_br_att_2", "w_br_dn_2", "w_out_2",
    "w_route_grp_2", "w_route_exp_2", "w_gate_2", "w_up_2", "w_down_2", "ln_g_2", "ln_b_2",
]


def to_cols(a):
    a = np.asarray(a).reshape(-1, P)
    return a.T


def lay_out(inputs):
    arrays = {n: np.ascontiguousarray(inputs[n]) for n in INPUTS}
    parts = {
        "norm1": inputs["l0_norm1"], "out_norm": inputs["l0_gla_out_norm"], "norm2": inputs["l0_norm2"],
        "conv_w": inputs["l0_ffn_conv_w"], "conv_b": inputs["l0_ffn_conv_b"], "cond": inputs["c_2"],
        "b_ada": inputs["b_ada_2"], "kv_g": inputs["kv_norm_g_2"], "dn_conv": inputs["conv_w_2"], "dn_g": inputs["dn_norm_g_2"],
    }
    arrays["cols"] = np.ascontiguousarray(np.concatenate([to_cols(parts[n]) for n in COLS], axis=1))
    arrays["consts"] = CONST_TABLE
    return arrays


def kernel(**inputs):
    import concourse.bacc as bacc
    from concourse.bass_utils import run_bass_kernel_spmd

    nc = bacc.Bacc("TRN2", target_bir_lowering=False, num_devices=1)
    arrays = lay_out(inputs)
    I = {n: nc.dram_tensor(f"in_{n}", a.shape, F32, kind="ExternalInput").ap() for n, a in arrays.items()}
    out = nc.dram_tensor("out", (1, T, D), F32, kind="ExternalOutput").ap()
    build_program(nc, I, out)
    r = run_bass_kernel_spmd(nc, [{f"in_{n}": a for n, a in arrays.items()}], core_ids=[0])
    return r.results[0]["out"]
```
